# Optimizing a Trainium2 kernel written in Bass

```python
import jax, jax.numpy as jnp
from jax import lax
import numpy as np

D_MODEL = 1024
BATCH = 1
SEQ = 2048
DEPTH = 1

D_MIX = D_MODEL
D_LRU = D_MIX // 2
LRU_HEADS = 8
LRU_HEAD_DIM = D_LRU // LRU_HEADS
CONV_WIDTH = 4
LRU_C = 8.0
D_HGRN = D_MIX - D_LRU
HGRN_HEADS = 8
HGRN_HEAD_DIM = D_HGRN // HGRN_HEADS
HGRN_CHUNK = 64
N_GROUPS = 4
EXPERTS_PER_GROUP = 8
N_EXPERTS = N_GROUPS * EXPERTS_PER_GROUP
TOP_K = 2
D_EXPERT = D_MODEL // 2
MOE_BLOCK = 128
NORM_EPS = 1e-6
PROJ_WIDTH = 2 * D_LRU + 5 * D_HGRN

kernel_name = 'hybrid_rglru_hgrn2_hmoe_encoder'

def rms_norm(x, w):
    xf = x.astype(jnp.float32)
    y = xf * lax.rsqrt(jnp.mean(xf * xf, axis=-1, keepdims=True) + NORM_EPS)
    return (y * w.astype(jnp.float32)).astype(x.dtype)

def centred_depthwise_conv(x, w, b):
    pad_l = CONV_WIDTH // 2
    pad_r = CONV_WIDTH - 1 - pad_l
    y = lax.conv_general_dilated(x, w[:, None, :].astype(x.dtype), window_strides=(1,),
                                 padding=[(pad_l, pad_r)], dimension_numbers=('NWC', 'WIO', 'NWC'),
                                 feature_group_count=x.shape[-1])
    return y + b.astype(x.dtype)

def linear_scan(a, b, reverse):
    def combine(left, right):
        a_l, b_l = left
        a_r, b_r = right
        return a_l * a_r, a_r * b_l + b_r
    _, h = lax.associative_scan(combine, (a, b), reverse=reverse, axis=1)
    return h

def rg_lru_direction(xc, wa, ba, wx, bx, lam, reverse):
    bsz, seq, _ = xc.shape
    xh = xc.reshape(bsz, seq, LRU_HEADS, LRU_HEAD_DIM)
    r = jax.nn.sigmoid(jnp.einsum('bshi,hij->bshj', xh, wa).reshape(bsz, seq, D_LRU) + ba)
    i = jax.nn.sigmoid(jnp.einsum('bshi,hij->bshj', xh, wx).reshape(bsz, seq, D_LRU) + bx)
    log_a = -LRU_C * r * jax.nn.softplus(-lam)
    u = jnp.sqrt(-jnp.expm1(2.0 * log_a)) * (i * xc)
    return linear_scan(jnp.exp(log_a), u, reverse)

def hgrn2_chunkwise(q, k, v, log_f):
    bsz, seq, heads, dk = q.shape
    dv = v.shape[-1]
    n_chunks = seq // HGRN_CHUNK

    def to_chunks(t):
        return t.reshape(bsz, n_chunks, HGRN_CHUNK, heads, t.shape[-1]).transpose(1, 0, 3, 2, 4)

    incl = jnp.tril(jnp.ones((HGRN_CHUNK, HGRN_CHUNK), dtype=bool))[:, :, None]

    def step(state, chunk):
        qc, kc, vc, lf = chunk
        b = jnp.cumsum(lf, axis=2)
        inter = jnp.einsum('bhtd,bhde->bhte', qc * jnp.exp(b), state)
        diff = b[:, :, :, None, :] - b[:, :, None, :, :]
        decay = jnp.exp(jnp.where(incl, diff, -jnp.inf))
        scores = jnp.einsum('bhtd,bhsd,bhtsd->bhts', qc, kc, decay)
        intra = jnp.einsum('bhts,bhse->bhte', scores, vc)
        b_last = b[:, :, -1:, :]
        new_state = (jnp.exp(b_last[:, :, 0, :])[..., None] * state
                     + jnp.einsum('bhsd,bhse->bhde', kc * jnp.exp(b_last - b), vc))
        return new_state, inter + intra

    state0 = jnp.zeros((bsz, heads, dk, dv), jnp.float32)
    _, o = lax.scan(step, state0, (to_chunks(q), to_chunks(k), to_chunks(v), to_chunks(log_f)))
    return o.transpose(1, 0, 3, 2, 4).reshape(bsz, seq, heads, dv)

def hgrn2_direction(q, v, f_logit, lb, reverse):
    f = lb + (1.0 - lb) * jax.nn.sigmoid(f_logit)
    log_f = jnp.log(f)
    k = 1.0 - f
    if reverse:
        flip = lambda t: jnp.flip(t, axis=1)
        return flip(hgrn2_chunkwise(flip(q), flip(k), flip(v), flip(log_f)))
    return hgrn2_chunkwise(q, k, v, log_f)

def hybrid_mixer(h, w_in, conv_w, conv_b, lru_wa, lru_ba, lru_wx, lru_bx, lru_lambda,
                 norm_lru_w, lb, norm_hgrn_w, w_out):
    f32 = jnp.float32
    bsz, seq, _ = h.shape
    proj = h @ w_in
    cuts = [D_LRU, 2 * D_LRU, 2 * D_LRU + D_HGRN, 2 * D_LRU + 2 * D_HGRN,
            2 * D_LRU + 3 * D_HGRN, 2 * D_LRU + 4 * D_HGRN]
    x_lru, y_lru, q, f_fwd, f_bwd, v_in, g = jnp.split(proj, cuts, axis=-1)

    xc = centred_depthwise_conv(x_lru, conv_w, conv_b).astype(f32)
    lru = (rg_lru_direction(xc, lru_wa[0].astype(f32), lru_ba[0].astype(f32), lru_wx[0].astype(f32),
                            lru_bx[0].astype(f32), lru_lambda[0].astype(f32), False)
           + rg_lru_direction(xc, lru_wa[1].astype(f32), lru_ba[1].astype(f32), lru_wx[1].astype(f32),
                              lru_bx[1].astype(f32), lru_lambda[1].astype(f32), True))
    lru = rms_norm(lru * jax.nn.gelu(y_lru.astype(f32)), norm_lru_w)

    heads = lambda t: t.astype(f32).reshape(bsz, seq, HGRN_HEADS, HGRN_HEAD_DIM)
    qh, vh = heads(q), heads(v_in)
    lbh = lb.astype(f32).reshape(HGRN_HEADS, HGRN_HEAD_DIM)
    hg = hgrn2_direction(qh, vh, heads(f_fwd), lbh, False) + hgrn2_direction(qh, vh, heads(f_bwd), lbh, True)
    hg = rms_norm(hg, norm_hgrn_w.reshape(HGRN_HEADS, HGRN_HEAD_DIM)) * jax.nn.silu(heads(g))

    merged = jnp.concatenate([lru, hg.reshape(bsz, seq, D_HGRN)], axis=-1).astype(h.dtype)
    return merged @ w_out

def hierarchical_moe(h, wg_r, bg_r, we_r, be_r, w_gate, w_up, w_down):
    f32 = jnp.float32
    bsz, seq, d = h.shape
    xf = h.reshape(-1, d)
    m = xf.shape[0]
    g_logits = (xf @ wg_r + bg_r).astype(f32)
    g_idx = jnp.argmax(g_logits, axis=-1)
    p_group = jnp.take_along_axis(jax.nn.softmax(g_logits, axis=-1), g_idx[:, None], axis=1)[:, 0]
    e_logits = (xf @ we_r + be_r).astype(f32).reshape(m, N_GROUPS, EXPERTS_PER_GROUP)
    e_in_g = jnp.take_along_axis(e_logits, g_idx[:, None, None], axis=1)[:, 0]
    top_v, top_i = lax.top_k(e_in_g, TOP_K)
    w_tok = p_group[:, None] * jax.nn.softmax(top_v, axis=-1)
    expert = g_idx[:, None] * EXPERTS_PER_GROUP + top_i

    n_assign = m * TOP_K
    e_flat = expert.reshape(-1).astype(jnp.int32)
    tok_flat = jnp.repeat(jnp.arange(m, dtype=jnp.int32), TOP_K)
    w_flat = w_tok.reshape(-1)
    order = jnp.argsort(e_flat)
    e_s, tok_s, w_s = e_flat[order], tok_flat[order], w_flat[order]
    counts = jnp.bincount(e_flat, length=N_EXPERTS).astype(jnp.int32)
    start = jnp.cumsum(counts) - counts
    padded = ((counts + MOE_BLOCK - 1) // MOE_BLOCK) * MOE_BLOCK
    pend = jnp.cumsum(padded)
    pstart = pend - padded
    dest = pstart[e_s] + (jnp.arange(n_assign, dtype=jnp.int32) - start[e_s])
    n_rows = n_assign + N_EXPERTS * MOE_BLOCK
    n_blocks = n_rows // MOE_BLOCK
    tok_buf = jnp.zeros((n_rows,), jnp.int32).at[dest].set(tok_s)
    w_buf = jnp.zeros((n_rows,), f32).at[dest].set(w_s)
    blk_start = jnp.arange(n_blocks, dtype=jnp.int32) * MOE_BLOCK
    blk_expert = jnp.minimum(jnp.sum(pend[None, :] <= blk_start[:, None], axis=1), N_EXPERTS - 1)
    x_buf = xf[tok_buf].reshape(n_blocks, MOE_BLOCK, d)

    def expert_block(args):
        xb, e = args
        return (jax.nn.silu(xb @ w_gate[e]) * (xb @ w_up[e])) @ w_down[e]

    y_buf = lax.map(expert_block, (x_buf, blk_expert)).reshape(n_rows, d)
    y = jnp.zeros((m, d), h.dtype).at[tok_buf].add((y_buf * w_buf[:, None]).astype(h.dtype))
    return y.reshape(bsz, seq, d)

def setup_inputs(seed: int = 0) -> dict:
    key = jax.random.key(seed)
    ks = jax.random.split(key, 26)
    f32 = jnp.float32
    nrm = lambda k, shape, scale: jax.random.normal(k, shape, f32) * scale
    a_lo = 0.9 ** (1.0 / LRU_C)
    a_hi = 0.999 ** (1.0 / LRU_C)
    a0 = jax.random.uniform(ks[12], (DEPTH, 2, D_LRU), f32, minval=a_lo, maxval=a_hi)
    return {
        'x': nrm(ks[0], (BATCH, SEQ, D_MODEL), 1.0),
        'c': nrm(ks[1], (BATCH, D_MODEL), 1.0),
        'ada_w': nrm(ks[2], (DEPTH, D_MODEL, 6 * D_MODEL), 0.5 * D_MODEL ** -0.5),
        'ada_b': nrm(ks[3], (DEPTH, 6 * D_MODEL), 0.02),
        'norm_mix_w': 1.0 + nrm(ks[4], (DEPTH, D_MODEL), 0.02),
        'w_in': nrm(ks[5], (DEPTH, D_MODEL, PROJ_WIDTH), D_MODEL ** -0.5),
        'conv_w': nrm(ks[6], (DEPTH, CONV_WIDTH, D_LRU), 0.5),
        'conv_b': nrm(ks[7], (DEPTH, D_LRU), 0.02),
        'lru_wa': nrm(ks[8], (DEPTH, 2, LRU_HEADS, LRU_HEAD_DIM, LRU_HEAD_DIM), LRU_HEAD_DIM ** -0.5),
        'lru_ba': nrm(ks[9], (DEPTH, 2, D_LRU), 0.02),
        'lru_wx': nrm(ks[10], (DEPTH, 2, LRU_HEADS, LRU_HEAD_DIM, LRU_HEAD_DIM), LRU_HEAD_DIM ** -0.5),
        'lru_bx': nrm(ks[11], (DEPTH, 2, D_LRU), 0.02),
        'lru_lambda': jnp.log(a0) - jnp.log1p(-a0),
        'norm_lru_w': 1.0 + nrm(ks[13], (DEPTH, D_LRU), 0.02),
        'hgrn_lb': nrm(ks[14], (DEPTH, D_HGRN), 0.5),
        'norm_hgrn_w': 1.0 + nrm(ks[15], (DEPTH, D_HGRN), 0.02),
        'w_out': nrm(ks[16], (DEPTH, D_MIX, D_MODEL), D_MIX ** -0.5),
        'norm_ffn_w': 1.0 + nrm(ks[17], (DEPTH, D_MODEL), 0.02),
        'router_group_w': nrm(ks[18], (DEPTH, D_MODEL, N_GROUPS), D_MODEL ** -0.5),
        'router_group_b': nrm(ks[19], (DEPTH, N_GROUPS), 0.01),
        'router_expert_w': nrm(ks[20], (DEPTH, D_MODEL, N_EXPERTS), D_MODEL ** -0.5),
        'router_expert_b': nrm(ks[21], (DEPTH, N_EXPERTS), 0.01),
        'expert_w_gate': nrm(ks[22], (DEPTH, N_EXPERTS, D_MODEL, D_EXPERT), D_MODEL ** -0.5),
        'expert_w_up': nrm(ks[23], (DEPTH, N_EXPERTS, D_MODEL, D_EXPERT), D_MODEL ** -0.5),
        'expert_w_down': nrm(ks[24], (DEPTH, N_EXPERTS, D_EXPERT, D_MODEL), D_EXPERT ** -0.5),
        'final_norm_w': 1.0 + nrm(ks[25], (D_MODEL,), 0.02),
    }

def reference(x, c, ada_w, ada_b, norm_mix_w, w_in, conv_w, conv_b, lru_wa, lru_ba, lru_wx, lru_bx,
              lru_lambda, norm_lru_w, hgrn_lb, norm_hgrn_w, w_out, norm_ffn_w, router_group_w,
              router_group_b, router_expert_w, router_expert_b, expert_w_gate, expert_w_up,
              expert_w_down, final_norm_w):
    lb_cum = jnp.cumsum(jax.nn.softmax(hgrn_lb.astype(jnp.float32), axis=0), axis=0)
    lb_all = lb_cum - lb_cum[0:1]
    cond = jax.nn.silu(c)
    for l in range(DEPTH):
        mod = (cond @ ada_w[l] + ada_b[l])[:, None, :]
        sh_mix, sc_mix, g_mix, sh_ffn, sc_ffn, g_ffn = jnp.split(mod, 6, axis=-1)
        h = rms_norm(x, norm_mix_w[l]) * (1.0 + sc_mix) + sh_mix
        x = x + g_mix * hybrid_mixer(h, w_in[l], conv_w[l], conv_b[l], lru_wa[l], lru_ba[l], lru_wx[l],
                                     lru_bx[l], lru_lambda[l], norm_lru_w[l], lb_all[l], norm_hgrn_w[l],
                                     w_out[l])
        h = rms_norm(x, norm_ffn_w[l]) * (1.0 + sc_ffn) + sh_ffn
        x = x + g_ffn * hierarchical_moe(h, router_group_w[l], router_group_b[l], router_expert_w[l],
                                         router_expert_b[l], expert_w_gate[l], expert_w_up[l],
                                         expert_w_down[l])
    return rms_norm(x, final_norm_w)


_drawn_inputs = setup_inputs


def setup_inputs(seed=0):
    import zlib

    import numpy as np

    out = dict(_drawn_inputs(seed))
    spreads = {}
    factors = {'norm_mix_w': 5.833,
     'conv_b': 3.35,
     'lru_ba': 8.0,
     'lru_bx': 8.0,
     'norm_lru_w': 8.0,
     'norm_hgrn_w': 8.0,
     'norm_ffn_w': 5.703,
     'router_group_b': 8.0,
     'router_expert_b': 26.494,
     'final_norm_w': 7.891}
    for name, (base, spread) in spreads.items():
        noise = np.random.default_rng([zlib.crc32(name.encode()), seed]).standard_normal(out[name].shape)
        drawn = base * np.exp(spread * noise) if base else spread * noise
        out[name] = __import__('jax').numpy.asarray(drawn.astype(out[name].dtype))
    for name, factor in factors.items():
        out[name] = (out[name] * factor).astype(out[name].dtype)
    return out
```

```python
from contextlib import ExitStack, contextmanager

import concourse.bass as bass
from concourse import mybir

F32 = mybir.dt.float32
F32R = mybir.dt.float32r
I32 = mybir.dt.int32
U32 = mybir.dt.uint32
ALU = mybir.AluOpType
ACT = mybir.ActivationFunctionType
AX = mybir.AxisListType.X

P = 128
BANK = 512
SEQ = 2048
D = 1024
KD = D // P
CH = 512
CT = CH // P
GROUPS = 7
TOK_TILES = SEQ // P
TOK_CHUNKS = SEQ // BANK
HEAD = 64
EPS = 1e-6
N_GROUPS = 4
EPG = 8
EXPERTS = N_GROUPS * EPG
F_EXP = 512
LRU_C = 8.0
ROUTES = N_GROUPS + EXPERTS
ASSIGN = 2 * SEQ
WINDOWS = EXPERTS + (ASSIGN - EXPERTS) // P
SURE = ASSIGN // P
ds = bass.ds

V_ADA_B, V_NORM_MIX, V_NORM_FFN, V_CONV_W, V_CONV_B, V_BA, V_BX, V_LAM, V_NORM_LRU, V_LB, V_NORM_HG, V_END = (
    0, 48, 56, 64, 80, 84, 92, 100, 108, 112, 116, 120)


class Chain:

    def __init__(self, eng, sem, base=0):
        self.eng, self.sem, self.base, self.n = eng, sem, base, 0

    def link(self, ins):
        ins.then_inc(self.sem, 1)
        self.n += 1
        self.eng.wait_ge(self.sem, self.base + self.n)


@contextmanager
def semaphores(nc):
    made = []

    def take(name):
        made.append(nc.alloc_semaphore(name))
        return made[-1]

    yield take
    nc.clear_and_free_semaphores(made)
    nc.all_engine_barrier()


def bcast_inner(ap, n):
    return ap.unsqueeze(ap.ndim).to_broadcast(list(ap.shape) + [n])


def phase_modulate(nc, t, g):
    with ExitStack() as ctx:
        sb = lambda n, s, d=F32: ctx.enter_context(nc.sbuf_tensor(n, s, d))
        sem = ctx.enter_context(semaphores(nc))
        bank = [ctx.enter_context(nc.psum_tensor(f"m_bank{i}", [P, BANK], F32)) for i in range(8)]
        cond = sb("cond", [P, KD])
        cond_in = sb("cond_in", [P, KD])
        cond_rep = sb("cond_rep", [P, KD, P])
        rows = sb("rows", [P, P])
        bias_row = sb("bias_row", [1, 2, D])
        fin_row = sb("fin_row", [1, D])
        ada = [sb(f"ada{i}", [P, KD, BANK]) for i in range(3)]
        mod_raw = sb("mod_raw", [P, 2, 16])
        shift = sb("shift_mix", [P, KD])
        scale = sb("scale_mix", [P, KD])
        xg = sb("xg", [P, 4, D])
        xn = sb("xn", [P, 4, D])
        junk = sb("junk", [P, 4, D])
        ssq = sb("ssq", [P, 4])
        std = sb("std", [P, 4])
        rstd = sb("rstd", [P, 4])
        c_in, rows_in, row_in, x_in = sem("c_in"), sem("rows_in"), sem("row_in"), sem("x_in")
        ada_in = [sem(f"ada_in{i}") for i in range(3)]
        ada_used = [sem(f"ada_used{i}") for i in range(3)]
        consts, cond_done, rep_done, rows_zero = sem("consts"), sem("cond_done"), sem("rep_done"), sem("rows_zero")
        cols_ps, cols_sb = sem("cols_ps"), sem("cols_sb")
        mod_ps, mod_sb, gate_ps, gate_sb = sem("mod_ps"), sem("mod_sb"), sem("gate_ps"), sem("gate_sb")
        affine, fin_ps, dve_chain, pool_chain, act_chain = (
            sem("affine"), sem("fin_ps"), sem("m_dve_chain"), sem("m_pool_chain"), sem("m_act_chain"))
        sq_done, std_done, xn_done, tr_done, h_act, h_dve = (
            sem("sq_done"), sem("std_done"), sem("xn_done"), sem("tr_done"), sem("h_act"), sem("h_dve"))
        block = ctx.enter_context(nc.Block())

        @block.sync
        def _(sp):
            sp.dma_start(cond_in[:], t["c"].rearrange("a (p j) -> (a p) j", j=KD)).then_inc(c_in, 16)
            sp.wait_ge(rows_zero, 1)
            for at, src in (
                (V_ADA_B, t["ada_b"].rearrange("a (r p) -> (a r) p", p=P)),
                (V_NORM_MIX, t["norm_mix_w"].rearrange("a (r p) -> (a r) p", p=P)),
                (V_NORM_FFN, t["norm_ffn_w"].rearrange("a (r p) -> (a r) p", p=P)),
                (V_CONV_W, t["conv_w"].rearrange("a j (r p) -> (a j r) p", p=P)),
                (V_CONV_B, t["conv_b"].rearrange("a (r p) -> (a r) p", p=P)),
                (V_BA, t["lru_ba"].rearrange("a d (r p) -> (a d r) p", p=P)),
                (V_BX, t["lru_bx"].rearrange("a d (r p) -> (a d r) p", p=P)),
                (V_LAM, t["lru_lambda"].rearrange("a d (r p) -> (a d r) p", p=P)),
                (V_NORM_LRU, t["norm_lru_w"].rearrange("a (r p) -> (a r) p", p=P)),
                (V_LB, t["hgrn_lb"].rearrange("a (r p) -> (a r) p", p=P)),
                (V_NORM_HG, t["norm_hgrn_w"].rearrange("a (r p) -> (a r) p", p=P)),
            ):
                sp.dma_start(rows[at:at + src.shape[0], :], src).then_inc(rows_in, 16)
            sp.dma_start(bias_row[:], t["ada_b"].rearrange("a (h v n) -> a h v n", h=2, v=3)[:, :, 2, :]).then_inc(row_in, 16)
            sp.dma_start(fin_row[:], t["final_norm_w"].rearrange("(a n) -> a n", a=1)).then_inc(row_in, 16)
            sp.dma_start(g["route_bias"][0:1, 0:N_GROUPS], t["router_group_b"]).then_inc(row_in, 16)
            sp.dma_start(g["route_bias"][0:1, N_GROUPS:ROUTES], t["router_expert_b"]).then_inc(row_in, 16)
            with sp.Fori(0, 2) as h:
                for q in range(6):
                    sp.wait_ge(ada_used[q % 3], h * 2 + q // 3)
                    sp.dma_start(ada[q % 3][:], t["ada_w"][0].rearrange("(p j) n -> p j n", j=KD)[
                        :, :, ds(h * (3 * D) + q * BANK, BANK)]).then_inc(ada_in[q % 3], 16)

        @block.gpsimd
        def _(pool):
            pc = Chain(pool, pool_chain)
            pool.memset(rows[:], 0.0).then_inc(rows_zero, 1)
            pool.memset(g["ones"][:], 1.0).then_inc(consts, 1)
            pool.memset(g["eps"][:], EPS).then_inc(consts, 1)
            pc.link(pool.memset(g["ident"][:], 0.0))
            pool.affine_select(out=g["ident"][:], in_=g["ident"][:], compare_op=ALU.not_equal, fill=1.0, base=0,
                               pattern=[[-1, P]], channel_multiplier=1).then_inc(consts, 1)
            with pool.Fori(0, TOK_CHUNKS) as i:
                pool.wait_ge(xn_done, i)
                pool.wait_ge(sq_done, i)
                pool.dma_start(xg[:], t["x"][0].rearrange("(a p) d -> p a d", p=P)[:, ds(i * 4, 4), :]).then_inc(x_in, 16)

        @block.scalar
        def _(act):
            act.wait_ge(c_in, 16)
            nc.scalar.activation(cond[:], cond_in[:], ACT.Silu).then_inc(cond_done, 1)
            act.wait_ge(consts, 3)
            with act.Fori(0, TOK_CHUNKS) as i:
                ac = Chain(act, act_chain, i)
                act.wait_ge(x_in, i * 16 + 16)
                act.wait_ge(std_done, i * 2)
                for a in range(4):
                    last = nc.scalar.activation(junk[:, a, :], xg[:, a, :], ACT.Square, accum_out=ssq[:, a:a + 1])
                last.then_inc(sq_done, 1)
                act.wait_ge(sq_done, i + 1)
                nc.scalar.activation(std[:], ssq[:], ACT.Sqrt, bias=g["eps"][:], scale=1.0 / D).then_inc(std_done, 1)
                act.wait_ge(affine, 2)
                for k in range(0, KD, 2):
                    act.wait_ge(tr_done, i * KD + k + 1)
                    nc.scalar.activation(g["hT"][:, k, ds(i * BANK, BANK)], bank[k][:], ACT.Identity,
                                         bias=shift[:, k:k + 1], scale=scale[:, k:k + 1]).then_inc(h_act, 1)

        @block.vector
        def _(dve):
            dve.wait_ge(cond_done, 1)
            dve.tensor_copy(cond_rep[:], bcast_inner(cond[:], P)).then_inc(rep_done, 1)
            dve.wait_ge(cols_ps, 1)
            dve.tensor_copy(g["cols"][:], bank[7][:, 0:P]).then_inc(cols_sb, 1)
            with dve.Fori(0, 2) as h:
                dve.wait_ge(mod_ps, h + 1)
                dve.tensor_copy(mod_raw[:, ds(h, 1), :], bank[0][:, 0:16].unsqueeze(1)).then_inc(mod_sb, 1)
                for q in range(2):
                    dve.wait_ge(gate_ps, h * 2 + q + 1)
                    dve.tensor_copy(g["gates"][:, ds(h, 1), q * BANK:(q + 1) * BANK],
                                    bank[1 + q][:].unsqueeze(1)).then_inc(gate_sb, 1)
            dc = Chain(dve, dve_chain)
            dve.wait_ge(mod_sb, 2)
            dve.wait_ge(cols_sb, 1)
            dve.tensor_tensor(shift[:], mod_raw[:, 0, 0:8], g["cols"][:, 0:8], ALU.add).then_inc(affine, 1)
            dc.link(dve.tensor_tensor(scale[:], mod_raw[:, 0, 8:16], g["cols"][:, 8:16], ALU.add))
            dve.scalar_tensor_tensor(out=scale[:], in0=scale[:], scalar=1.0, in1=g["cols"][:, V_NORM_MIX:V_NORM_MIX + 8],
                                     op0=ALU.add, op1=ALU.mult).then_inc(affine, 1)
            dve.tensor_tensor(g["shift_ffn"][:], mod_raw[:, 1, 0:8], g["cols"][:, 24:32], ALU.add)
            dc.link(dve.tensor_tensor(g["scale_ffn"][:], mod_raw[:, 1, 8:16], g["cols"][:, 32:40], ALU.add))
            dve.scalar_tensor_tensor(out=g["scale_ffn"][:], in0=g["scale_ffn"][:], scalar=1.0,
                                     in1=g["cols"][:, V_NORM_FFN:V_NORM_FFN + 8], op0=ALU.add, op1=ALU.mult)
            for q in range(2):
                dve.wait_ge(fin_ps, q + 1)
                dve.tensor_copy(g["final_w"][:, q * BANK:(q + 1) * BANK], bank[3 + q][:]).then_inc(cols_sb, 1)
            dve.wait_ge(affine, 2)
            with dve.Fori(0, TOK_CHUNKS) as i:
                dve.wait_ge(std_done, i * 2 + 1)
                dve.reciprocal(rstd[:], std[:]).then_inc(std_done, 1)
                dve.wait_ge(std_done, i * 2 + 2)
                dve.wait_ge(tr_done, i * KD)
                dve.wait_ge(x_in, i * 16 + 16)
                for a in range(4):
                    last = dve.tensor_scalar(xn[:, a, :], xg[:, a, :], rstd[:, a:a + 1], None, ALU.mult)
                last.then_inc(xn_done, 1)
                for k in range(1, KD, 2):
                    dve.wait_ge(tr_done, i * KD + k + 1)
                    dve.tensor_scalar(g["hT"][:, k, ds(i * BANK, BANK)], bank[k][:], scale[:, k:k + 1],
                                      shift[:, k:k + 1], ALU.mult, ALU.add).then_inc(h_dve, 1)

        @block.tensor
        def _(pe):
            pe.wait_ge(consts, 3)
            pe.wait_ge(rows_in, 16 * 11)
            pe.transpose(bank[7][:, 0:P], rows[:], g["ident"][:]).then_inc(cols_ps, 1)
            pe.wait_ge(row_in, 64)
            for q in range(2):
                pe.matmul(bank[3 + q][:], g["ones"][0:1, :], fin_row[:, q * BANK:(q + 1) * BANK],
                          start=True, stop=True).then_inc(fin_ps, 1)
            pe.wait_ge(rep_done, 1)
            pe.wait_ge(cond_done, 1)
            with pe.Fori(0, 2) as h:
                pe.wait_ge(mod_sb, h)
                for q in range(4):
                    pe.wait_ge(ada_in[q % 3], h * 32 + 16 * (q // 3) + 16)
                    for m in range(4):
                        for j in range(KD):
                            mm = pe.matmul(bank[0][:, 4 * q + m:4 * q + m + 1], ada[q % 3][:, j, m * P:(m + 1) * P],
                                           cond[:, j:j + 1], start=(j == 0), stop=(j == KD - 1))
                    mm.then_inc(ada_used[q % 3], 1)
                pe.matmul(bank[5][:, 0:1], g["ident"][:], g["ident"][:, 0:1], start=True, stop=True).then_inc(mod_ps, 1)
                for q in range(4, 6):
                    pe.wait_ge(ada_in[q % 3], h * 32 + 32)
                    pe.wait_ge(gate_sb, h * 2)
                    for j in range(KD):
                        pe.matmul(bank[q - 3][:], cond_rep[:, j, :], ada[q % 3][:, j, :], start=(j == 0), stop=False)
                    pe.matmul(bank[q - 3][:], g["ones"][0:1, :], bias_row[:, ds(h, 1), (q - 4) * BANK:(q - 3) * BANK],
                              start=False, stop=True).then_inc(gate_ps, 1)
                    pe.matmul(bank[5][:, 0:1], g["ident"][:], g["ident"][:, 0:1], start=True,
                              stop=True).then_inc(ada_used[q % 3], 1)
            with pe.Fori(0, TOK_CHUNKS) as i:
                pe.wait_ge(xn_done, i + 1)
                pe.wait_ge(cols_sb, 3)
                pe.wait_ge(gate_sb, 4)
                pe.wait_ge(mod_sb, 2)
                for k in range(KD):
                    pe.wait_ge(h_dve if k % 2 else h_act, i * (KD // 2))
                    for a in range(4):
                        tr = pe.transpose(bank[k][:, a * P:(a + 1) * P], xn[:, a, k * P:(k + 1) * P], g["ident"][:])
                    tr.then_inc(tr_done, 1)


def persistent(nc, ctx):
    sb = lambda n, s, d=F32: ctx.enter_context(nc.sbuf_tensor(n, s, d))
    return dict(
        ident=sb("ident", [P, P]), ones=sb("ones", [P, P]), eps=sb("eps", [P, 1]),
        cols=sb("cols", [P, P]), gates=sb("gates", [P, 2, D]), final_w=sb("final_w", [P, D]),
        shift_ffn=sb("shift_ffn", [P, KD]), scale_ffn=sb("scale_ffn", [P, KD]), route_bias=sb("route_bias", [1, ROUTES]),
    )


def persistent2(nc, ctx, g):
    sb = lambda n, s, d=F32: ctx.enter_context(nc.sbuf_tensor(n, s, d))
    g["logits"] = sb("logits", [P, TOK_TILES, ROUTES])
    g["weight"] = [sb(f"weight{k}", [P, TOK_TILES]) for k in range(2)]
    g["dest"] = [sb(f"dest{k}", [P, TOK_TILES], U32) for k in range(2)]
    g["window"] = sb("window", [1, WINDOWS + 1], I32)


def wait_apart(eng, sem, value, passed):
    eng.wait_ge(sem, value)
    eng.sem_inc(passed, 1)


def phase_project(nc, t, g):
    with ExitStack() as ctx:
        sb = lambda n, s, d=F32: ctx.enter_context(nc.sbuf_tensor(n, s, d))
        sem = ctx.enter_context(semaphores(nc))
        bank = [ctx.enter_context(nc.psum_tensor(f"p_bank{i}", [P, BANK], F32)) for i in range(8)]
        hT = g["hT"]
        w = [sb(f"w_in{m}", [P, KD, P]) for m in range(CT)]
        stage = [sb(f"proj_stage{i}", [P, SEQ]) for i in range(2)]
        xin = sb("lru_x", [P, SEQ + 3])
        xc = sb("lru_xc", [P, SEQ])
        y = sb("lru_y", [P, SEQ])
        R = [sb(f"lru_r{d}", [P, SEQ]) for d in range(2)]
        I = [sb(f"lru_i{d}", [P, SEQ]) for d in range(2)]
        T = [sb(f"lru_t{d}", [P, SEQ]) for d in range(2)]
        gw = sb("lru_gate_w", [P, 4, P])
        par = sb("lru_par", [P, 12])
        neg = sb("lru_neg", [P, 2])
        sp = [sb(f"softplus{i}", [P, 8]) for i in range(5)]
        tmp = xin[:, 2:2 + SEQ]
        w_in = [sem(f"w_in_s{m}") for m in range(CT)]
        mm_done, evac, stored = sem("mm_done"), sem("evac"), [sem(f"stored{i}") for i in range(2)]
        x_in, y_in, gw_in, gw_zero = sem("lru_x_in"), sem("lru_y_in"), sem("gw_in"), sem("gw_zero")
        conv_done, gate_mm, gate_act = sem("conv_done"), sem("gate_mm"), sem("gate_act")
        ea, tanh_done, exp_done, pre_root, root_done, gelu_done = (
            sem("softplus_exp"), sem("tanh_done"), sem("exp_done"), sem("pre_root"), sem("root_done"), sem("gelu_done"))
        lru_done, lru_stored, chain, par_done = sem("lru_done"), sem("lru_stored"), sem("lru_chain"), sem("par_done")
        zero_out = sem("zero_out")
        zeros = sb("zeros", [P, D])
        CHAIN = 11
        block = ctx.enter_context(nc.Block())
        src_w = t["w_in"][0].rearrange("(k p) n -> p k n", p=P)

        def over_groups(eng, body):
            body(0, None)
            body(1, None)
            with eng.Fori(0, CT) as i:
                body(i + 2, i)
            body(GROUPS - 1, None)

        @block.sync
        def _(q):
            for m in range(CT):
                q.dma_start(w[m][:], src_w[:, :, m * P:(m + 1) * P]).then_inc(w_in[m], 16)

            def body(gr, i):
                if i is not None:
                    q.wait_ge(lru_stored, i * 16)
                    q.wait_ge(gw_zero, 1)
                    for s in range(2):
                        q.wait_ge(stored[s], 64)
                    q.dma_start(xin[:, 2:2 + SEQ], t["projT"][ds(i * P, P), :]).then_inc(x_in, 16)
                    q.dma_start(y[:], t["projT"][ds(i * P + CH, P), :]).then_inc(y_in, 16)
                    for half in range(2):
                        at = slice(half * HEAD, (half + 1) * HEAD)
                        for gate, name in ((0, "lru_wa"), (2, "lru_wx")):
                            q.dma_start(gw[at, gate:gate + 2, at], t[name][0].rearrange("d h i j -> h i d j")[
                                ds(i * 2 + half, 1), :, :, :].rearrange("h i d j -> (h i) d j")).then_inc(gw_in, 16)
                for m in range(CT):
                    q.wait_ge(evac, gr * 16 + m * 4 + 4)
                    q.dma_start(t["projT"][ds(gr * CH + m * P, P), :], stage[m % 2][:]).then_inc(stored[m % 2], 16)
                    if not (isinstance(gr, int) and gr == GROUPS - 1):
                        q.wait_ge(mm_done, gr * 16 + m * 4 + 4)
                        q.dma_start(w[m][:], src_w[:, :, ds((gr + 1) * CH + m * P, P)]).then_inc(w_in[m], 16)
                if i is not None:
                    q.wait_ge(lru_done, i + 1)
                    q.dma_start(t["mergedT"][ds(i * P, P), :], tmp).then_inc(lru_stored, 16)

            over_groups(q, body)
            q.wait_ge(lru_stored, 16 * CT)
            for s in range(2):
                q.wait_ge(stored[s], 16 * 2 * GROUPS)

        @block.gpsimd
        def _(pool):
            pool.memset(xin[:], 0.0)
            pool.memset(zeros[:], 0.0)
            pool.memset(gw[:], 0.0).then_inc(gw_zero, 1)
            pool.wait_ge(gw_zero, 1)
            with pool.Fori(SURE, WINDOWS + 1) as i:
                pool.dma_start(t["ybuf"][ds(i * P, P), :], zeros[:]).then_inc(zero_out, 16)
            pool.wait_ge(zero_out, 16 * (WINDOWS + 1 - SURE))

        @block.scalar
        def _(act):
            nc.scalar.activation(sp[0][:], g["cols"][:, V_LAM:V_LAM + 8], ACT.Abs).then_inc(ea, 1)
            act.wait_ge(ea, 1)
            nc.scalar.activation(sp[1][:], sp[0][:], ACT.Exp, scale=-1.0).then_inc(ea, 1)

            def body(gr, i):
                for m in range(CT):
                    for c in range(TOK_CHUNKS):
                        act.wait_ge(mm_done, gr * 16 + m * 4 + c + 1)
                        if c == 0:
                            act.wait_ge(stored[m % 2], gr * 32 if m < 2 else gr * 32 + 16)
                        nc.scalar.activation(stage[m % 2][:, c * BANK:(c + 1) * BANK], bank[c][:],
                                             ACT.Copy).then_inc(evac, 1)
                    if i is None:
                        continue
                    if m == 0:
                        act.wait_ge(par_done, i + 1)
                        for k in range(4):
                            dst = (R[0], R[1], I[0], I[1])[k]
                            for c in range(TOK_CHUNKS):
                                act.wait_ge(gate_mm, i * 16 + k * 4 + c + 1)
                                nc.scalar.activation(dst[:, c * BANK:(c + 1) * BANK], bank[4 + c][:], ACT.Sigmoid,
                                                     bias=par[:, 5 + k:6 + k]).then_inc(gate_act, 1)
                    if m == 1:
                        act.wait_ge(gate_act, i * 16 + 16)
                        for d in range(2):
                            nc.scalar.activation(T[d][:], R[d][:], ACT.Tanh, scale=par[:, 9 + d:10 + d]).then_inc(tanh_done, 1)
                        act.wait_ge(tanh_done, i * 2 + 2)
                        for d in range(2):
                            nc.scalar.activation(R[d][:], R[d][:], ACT.Exp, scale=neg[:, d:d + 1]).then_inc(exp_done, 1)
                    if m == 2:
                        for d in range(2):
                            act.wait_ge(pre_root, i * 2 + d + 1)
                            nc.scalar.activation(T[d][:], T[d][:], ACT.Sqrt).then_inc(root_done, 1)
                        act.wait_ge(y_in, i * 16 + 16)
                        nc.scalar.activation(y[:], y[:], ACT.Gelu_apprx_tanh).then_inc(gelu_done, 1)

            over_groups(act, body)

        @block.vector
        def _(dve):
            dc = Chain(dve, chain)
            lam = g["cols"][:, V_LAM:V_LAM + 8]
            dve.wait_ge(ea, 2)
            e, u, z, z2, s = sp[1][:], sp[2][:], sp[3][:], sp[0][:], sp[4][:]
            dc.link(dve.tensor_scalar(u, e, 2.0, None, ALU.add))
            dc.link(dve.reciprocal(u, u))
            dc.link(dve.tensor_tensor(z, e, u, ALU.mult))
            dc.link(dve.tensor_tensor(z2, z, z, ALU.mult))
            dc.link(dve.tensor_scalar(s, z2, 1.0 / 17, 1.0 / 15, ALU.mult, ALU.add))
            for n in (13, 11, 9, 7, 5, 3, 1):
                dc.link(dve.tensor_tensor(s, s, z2, ALU.mult))
                dc.link(dve.tensor_scalar(s, s, 1.0 / n, None, ALU.add))
            dc.link(dve.tensor_tensor(s, s, z, ALU.mult))
            dc.link(dve.tensor_scalar(u, lam, -1.0, 0.0, ALU.mult, ALU.max))
            dc.link(dve.tensor_scalar(u, u, LRU_C, None, ALU.mult))
            dc.link(dve.scalar_tensor_tensor(out=lam, in0=s, scalar=2.0 * LRU_C, in1=u, op0=ALU.mult, op1=ALU.add))
            first = dc.n
            table = g["cols"][:, V_CONV_W:V_LB].rearrange("p (r k) -> p r k", k=CT)
            with dve.Fori(0, CT) as i:
                dc = Chain(dve, chain, i * CHAIN + first)
                dc.link(dve.tensor_copy(par[:].unsqueeze(2), table[:, :, ds(i, 1)]))
                dve.tensor_scalar(neg[:], par[:, 9:11], -1.0, None, ALU.mult).then_inc(par_done, 1)
                dve.wait_ge(x_in, i * 16 + 16)
                dc.link(dve.tensor_scalar(xc[:], xin[:, 0:SEQ], par[:, 0:1], par[:, 4:5], ALU.mult, ALU.add))
                for j in range(1, 4):
                    ins = dve.scalar_tensor_tensor(out=xc[:], in0=xin[:, j:j + SEQ], scalar=par[:, j:j + 1], in1=xc[:],
                                                   op0=ALU.mult, op1=ALU.add)
                    if j < 3:
                        dc.link(ins)
                    else:
                        ins.then_inc(conv_done, 1)
                dve.wait_ge(conv_done, i + 1)
                dve.wait_ge(gate_act, i * 16 + 16)
                for d in range(2):
                    dve.tensor_tensor(I[d][:], I[d][:], xc[:], ALU.mult)
                for d in range(2):
                    dve.wait_ge(exp_done, i * 2 + d + 1)
                    dc.link(dve.tensor_tensor(tmp, R[d][:], R[d][:], ALU.mult))
                    dve.scalar_tensor_tensor(out=T[d][:], in0=tmp, scalar=1.0, in1=T[d][:],
                                             op0=ALU.add, op1=ALU.mult).then_inc(pre_root, 1)
                    dve.wait_ge(pre_root, i * 2 + d + 1)
                for d in range(2):
                    dve.wait_ge(root_done, i * 2 + d + 1)
                    dc.link(dve.tensor_tensor(I[d][:], I[d][:], T[d][:], ALU.mult))
                    if d == 0:
                        dc.link(dve.tensor_tensor_scan(T[0][:], R[0][:], I[0][:], 0.0, ALU.mult, ALU.add))
                    else:
                        dc.link(dve.tensor_tensor_scan(T[1][:, ::-1], R[1][:, ::-1], I[1][:, ::-1], 0.0,
                                                       ALU.mult, ALU.add))
                dc.link(dve.tensor_tensor(T[0][:], T[0][:], T[1][:], ALU.add))
                dve.wait_ge(gelu_done, i + 1)
                dve.tensor_tensor(tmp, T[0][:], y[:], ALU.mult).then_inc(lru_done, 1)
                assert dc.n == CHAIN

        @block.tensor
        def _(pe):
            def body(gr, i):
                for m in range(CT):
                    pe.wait_ge(w_in[m], gr * 16 + 16)
                    for c in range(TOK_CHUNKS):
                        if m == 0:
                            pe.wait_ge(evac, gr * 16)
                        else:
                            pe.wait_ge(evac, gr * 16 + m * 4 + c - 3)
                        for k in range(KD):
                            mm = pe.matmul(bank[c][:], w[m][:, k, :], hT[:, k, c * BANK:(c + 1) * BANK],
                                           start=(k == 0), stop=(k == KD - 1))
                        mm.then_inc(mm_done, 1)
                    if i is not None and m == 0:
                        pe.wait_ge(conv_done, i + 1)
                        pe.wait_ge(gw_in, i * 64 + 64)
                        for k in range(4):
                            for c in range(TOK_CHUNKS):
                                n = k * 4 + c - 3
                                pe.wait_ge(gate_act, i * 16 + n if n > 0 else i * 16)
                                pe.matmul(bank[4 + c][:], gw[:, k, :], xc[:, c * BANK:(c + 1) * BANK],
                                          start=True, stop=True).then_inc(gate_mm, 1)

            over_groups(pe, body)


LEVELS = 7
CHUNKS = TOK_TILES


def phase_hgrn(nc, t, g):
    with ExitStack() as ctx:
        sb = lambda n, s, d=F32: ctx.enter_context(nc.sbuf_tensor(n, s, d))
        sem = ctx.enter_context(semaphores(nc))
        sem2 = lambda n: [sem(f"{n}{i}") for i in range(2)]
        bank = [ctx.enter_context(nc.psum_tensor(f"h_bank{i}", [P, BANK], F32)) for i in range(8)]
        W = [P, CT, P]
        v_tok = sb("v_tok", [P, CHUNKS, CH])
        s_bwd = sb("s_bwd", [P, CHUNKS + 1, CT, P])
        s_fwd = [sb(f"s_fwd{i}", W) for i in range(2)]
        decayed = sb("decayed", W)
        masks = sb("masks", [P, LEVELS, P], I32)
        xor_i = sb("xor_i", [P, 2, P], I32)
        xor_f = sb("xor_f", [P, P])
        ge = sb("ge", [P, LEVELS + 1, P])
        lbt = sb("lbt", [P, 4, CT])
        ones_row = sb("ones_row", [P, P])
        a_f = [sb(f"a_f{i}", W) for i in range(2)]
        a_v = [sb(f"a_v{i}", W) for i in range(2)]
        a_k = [sb(f"a_k{i}", W) for i in range(2)]
        a_e = [sb(f"a_e{i}", W) for i in range(2)]
        a_ktok = [sb(f"a_ktok{i}", [P, CH]) for i in range(2)]
        a_p = [sb(f"a_p{i}", [P, CT]) for i in range(2)]
        sem_names = ("f_in", "v_in", "a_sig", "a_gate", "a_keys", "a_kd", "a_ktr", "a_vtr", "a_kev", "a_vev", "a_kv")
        f_in, v_in, a_sig, a_gate, a_keys, a_kd, a_ktr, a_vtr, a_kev, a_vev, a_kv = (sem2(n) for n in sem_names)
        a_state, a_chain, zeroed, lb_done, lb_exp, mask_chain, iota_done = (
            sem("a_state"), sem("a_chain"), sem("zeroed"), sem("lb_done"), sem("lb_exp"), sem("mask_chain"), sem("iota_done"))
        passed = sem("passed")
        g["masks"], g["v_tok"], g["s_bwd"], g["lbt"] = masks, v_tok, s_bwd, lbt
        src = lambda group, c: t["projT"][group * CH:(group + 1) * CH, :].rearrange("(j p) n -> p j n", p=P)[:, :, ds(c, P)]
        A_CHAIN = 7

        with nc.Block() as block:
            @block.sync
            def _(q):
                with q.Fori(0, CHUNKS // 2) as i:
                    for r in range(2):
                        c = q.snap((CHUNKS - 1 - r) * P - i * (2 * P))
                        wait_apart(q, a_keys[r], i, passed)
                        q.dma_start(a_f[r][:], src(4, c)).then_inc(f_in[r], 16)
                        q.wait_ge(a_vtr[r], i)
                        q.dma_start(a_v[r][:], src(5, c)).then_inc(v_in[r], 16)

            @block.gpsimd
            def _(pool):
                for x in (s_bwd[:], s_fwd[0][:], s_fwd[1][:]):
                    pool.memset(x, 0.0)
                pool.memset(ones_row[:], 1.0)
                for r in range(2):
                    last = pool.memset(a_e[r][:], 1.0)
                last.then_inc(zeroed, 1)
                pool.iota(xor_i[:, 0, :], [[0, P]], base=0, channel_multiplier=1)
                pool.iota(xor_i[:, 1, :], [[1, P]], base=0, channel_multiplier=0).then_inc(iota_done, 1)
                pool.wait_ge(lb_done, 1)
                with pool.Fori(0, CHUNKS // 2) as i:
                    for r in range(2):
                        wait_apart(pool, a_sig[r], i + 1, passed)
                        for j in range(CT):
                            last = pool.tensor_scalar(a_f[r][:, j, :], a_f[r][:, j, :], lbt[:, 3, j:j + 1], lbt[:, 2, j:j + 1],
                                                      ALU.mult, ALU.add)
                        last.then_inc(a_gate[r], 1)
                        pool.wait_ge(a_gate[r], i + 1)
                        wait_apart(pool, a_ktr[r], i, passed)
                        pool.tensor_scalar(a_k[r][:], a_f[r][:], -1.0, 1.0, ALU.mult, ALU.add).then_inc(a_kd[r], 1)

            @block.scalar
            def _(act):
                act.wait_ge(lb_exp, 1)
                nc.scalar.activation(lbt[:, 0, :], lbt[:, 1, :], ACT.Exp).then_inc(lb_exp, 1)
                with act.Fori(0, CHUNKS // 2) as i:
                    for r in range(2):
                        act.wait_ge(f_in[r], i * 16 + 16)
                        nc.scalar.activation(a_f[r][:], a_f[r][:], ACT.Sigmoid).then_inc(a_sig[r], 1)
                        act.wait_ge(a_ktr[r], i + 1)
                        act.wait_ge(a_kv[r], i)
                        nc.scalar.activation(a_ktok[r][:], bank[r][:], ACT.Copy).then_inc(a_kev[r], 1)

            @block.vector
            def _(dve):
                mc = Chain(dve, mask_chain)
                dve.wait_ge(iota_done, 1)
                mc.link(dve.tensor_tensor(xor_i[:, 0, :], xor_i[:, 0, :], xor_i[:, 1, :], ALU.bitwise_xor))
                mc.link(dve.tensor_copy(xor_f[:], xor_i[:, 0, :]))
                for l in range(LEVELS + 1):
                    last = dve.tensor_scalar(ge[:, l, :], xor_f[:], float(1 << l), None, ALU.is_ge)
                mc.link(last)
                dve.tensor_tensor(masks[:], ge[:, 0:LEVELS, :], ge[:, 1:LEVELS + 1, :], ALU.subtract)
                raw = g["cols"][:, V_LB:V_LB + CT]
                dve.tensor_tensor(lbt[:, 1, :], raw, raw, ALU.subtract).then_inc(lb_exp, 1)
                dve.wait_ge(lb_exp, 2)
                mc.link(dve.reciprocal(lbt[:, 1, :], lbt[:, 0, :]))
                mc.link(dve.tensor_tensor(lbt[:, 1, :], lbt[:, 1, :], lbt[:, 0, :], ALU.mult))
                mc.link(dve.tensor_tensor(lbt[:, 2, :], lbt[:, 1, :], lbt[:, 1, :], ALU.subtract))
                dve.tensor_scalar(lbt[:, 3, :], lbt[:, 2, :], -1.0, 1.0, ALU.mult, ALU.add).then_inc(lb_done, 1)
                dve.wait_ge(zeroed, 1)
                with dve.Fori(0, CHUNKS // 2) as i:
                    for r in range(2):
                        dc = Chain(dve, a_chain, i * 4 + r * 2)
                        c = dve.snap((CHUNKS - 1 - r) - i * 2)
                        dve.wait_ge(a_gate[r], i + 1)
                        dve.wait_ge(a_keys[r], i)
                        for j in range(CT):
                            last = dve.tensor_tensor_scan(a_e[r][:, j, 1:P], a_f[r][:, j, 0:P - 1], ones_row[:, 0:P - 1], 1.0,
                                                          ALU.mult, ALU.mult)
                        dc.link(last)
                        dve.tensor_tensor(a_p[r][:], a_e[r][:, :, P - 1], a_f[r][:, :, P - 1], ALU.mult)
                        dve.wait_ge(a_kd[r], i + 1)
                        dve.tensor_tensor(a_k[r][:], a_k[r][:], a_e[r][:], ALU.mult).then_inc(a_keys[r], 1)
                        dve.wait_ge(a_keys[r], i + 1)
                        wait_apart(dve, a_vtr[r], i + 1, passed)
                        dve.tensor_copy(v_tok[:, ds(c, 1), :], bank[2 + r][:].unsqueeze(1)).then_inc(a_vev[r], 1)
                        dve.wait_ge(a_state, i * 4 + r * 2)
                        dc.link(dve.tensor_tensor(decayed[:].unsqueeze(1), s_bwd[:, ds(c + 1, 1), :, :],
                                                  bcast_inner(a_p[r][:], P).unsqueeze(1), ALU.mult))
                        dve.wait_ge(a_kv[r], i + 1)
                        for half in range(2):
                            at = slice(half * HEAD, (half + 1) * HEAD)
                            kv = bank[4 + r][at, :].rearrange("p (j n) -> p j n", j=CT)[:, :, at]
                            dve.tensor_tensor(s_bwd[at, ds(c, 1), :, at], decayed[at, :, at].unsqueeze(1), kv.unsqueeze(1),
                                              ALU.add).then_inc(a_state, 1)

            @block.tensor
            def _(pe):
                with pe.Fori(0, CHUNKS // 2) as i:
                    for r in range(2):
                        c = pe.snap((CHUNKS - 1 - r) - i * 2)
                        pe.wait_ge(v_in[r], i * 16 + 16)
                        pe.wait_ge(a_vev[r], i)
                        for j in range(CT):
                            tr = pe.transpose(bank[2 + r][:, j * P:(j + 1) * P], a_v[r][:, j, :], g["ident"][:])
                        tr.then_inc(a_vtr[r], 1)
                        pe.wait_ge(a_keys[r], i + 1)
                        pe.wait_ge(a_kev[r], i)
                        for j in range(CT):
                            tr = pe.transpose(bank[r][:, j * P:(j + 1) * P], a_k[r][:, j, :], g["ident"][:])
                        tr.then_inc(a_ktr[r], 1)
                        pe.wait_ge(a_vev[r], i + 1)
                        pe.wait_ge(a_state, i * 4)
                        wait_apart(pe, a_kev[r], i + 1, passed)
                        for j in range(CT):
                            mm = pe.matmul(bank[4 + r][:, j * P:(j + 1) * P], a_ktok[r][:, j * P:(j + 1) * P],
                                           v_tok[:, ds(c, 1), j * P:(j + 1) * P], start=True, stop=True)
                        mm.then_inc(a_kv[r], 1)

        qkv = ("q", "ff", "fb", "gate")
        inp = {n: [sb(f"b_{n}{i}", W) for i in range(2)] for n in qkv}
        QF, KF, QB, KB = ([sb(f"{n}{i}", W) for i in range(2)] for n in ("qf", "kf", "qb", "kb"))
        kd = sb("k_diag", W)
        PF, PB = ([sb(f"{n}{l}", [P, CT, P >> l]) for l in range(1, LEVELS + 1)] for n in ("pf", "pb"))
        score = sb("score", [P, 2, CT, P])
        ktok = sb("ktok", [P, CH])
        sq = sb("o_sq", [P, CH])
        ss, rs, rinv = sb("o_ss", [P, 8]), sb("o_rms", [P, 8]), sb("o_rinv", [P, 8])
        on = sb("o_norm", [P, CH])
        mrg = [sb(f"mrg{i}", W) for i in range(2)]
        loaded = {n: sem2(f"in_{n}") for n in qkv}
        sig, silu = sem("b_sig"), sem("b_silu")
        gate_f, init_v, init_p = sem("b_gate"), sem("b_init_v"), sem("b_init_p")
        up_v, up_p, up_a, lvl, taken = sem("up_v"), sem("up_p"), sem("up_a"), sem("lvl"), sem("taken")
        ktr, kev, kvs, st, o_mm, o_sqd, o_ss, o_rms, o_rinv, o_n, o_tr, mrg_done, mrg_out, vch, pch = (sem(n) for n in (
            "b_ktr", "b_kev", "b_kv", "b_state", "o_mm", "o_sqd", "o_ssd", "o_rmsd", "o_rinvd", "o_nd", "o_tr",
            "mrg_done", "mrg_out", "b_vch", "b_pch"))
        mrg_out = sem2("mrg_stored")

        def halves(x, l):
            return x.rearrange("p j (n two a) -> p (j n) two a", two=2, a=1 << l)

        def whole(x, l):
            return x.rearrange("p j (n two) -> p (j n) two", two=2)

        with nc.Block() as block:
            @block.sync
            def _(q):
                with q.Fori(0, CHUNKS // 2) as i:
                    for r in range(2):
                        c = i * (2 * P) + r * P
                        n = i * 2 + r
                        for name, group in (("ff", 3), ("fb", 4), ("q", 2), ("gate", 6)):
                            q.wait_ge(mrg_out[r], i * 16)
                            q.dma_start(inp[name][r][:], src(group, c)).then_inc(loaded[name][r], 16)
                        q.wait_ge(mrg_done, n + 1)
                        q.dma_start(t["mergedT"][CH:2 * CH, :].rearrange("(j p) n -> p j n", p=P)[:, :, ds(c, P)],
                                    mrg[r][:]).then_inc(mrg_out[r], 16)
                for r in range(2):
                    q.wait_ge(mrg_out[r], 16 * (CHUNKS // 2))

            @block.gpsimd
            def _(pool):
                with pool.Fori(0, CHUNKS // 2) as i:
                    for r in range(2):
                        n = i * 2 + r
                        f, b, q = inp["ff"][r], inp["fb"][r], inp["q"][r]
                        wait_apart(pool, sig, n * 2 + 2, passed)
                        for x in (f, b):
                            for j in range(CT):
                                last = pool.tensor_scalar(x[:, j, :], x[:, j, :], lbt[:, 3, j:j + 1], lbt[:, 2, j:j + 1],
                                                          ALU.mult, ALU.add)
                            last.then_inc(gate_f, 1)
                        pool.wait_ge(gate_f, n * 2 + 2)
                        wait_apart(pool, lvl, n * (LEVELS + 1), passed)
                        pool.tensor_scalar(KF[0][:], f[:], -1.0, 1.0, ALU.mult, ALU.add)
                        pool.tensor_scalar(KB[0][:], b[:], -1.0, 1.0, ALU.mult, ALU.add).then_inc(init_p, 1)
                        pool.wait_ge(init_p, n * 2 + 1)
                        pool.wait_ge(loaded["q"][r], i * 16 + 16)
                        pool.tensor_tensor(QB[0][:], q[:], b[:], ALU.mult).then_inc(init_p, 1)
                        pool.wait_ge(init_p, n * 2 + 2)
                        for l in range(LEVELS):
                            cur, nxt = l % 2, (l + 1) % 2
                            pb = whole(b[:] if l == 0 else PB[l - 1][:], l)
                            pool.wait_ge(lvl, n * (LEVELS + 1) + l + 1)
                            if l:
                                pool.wait_ge(up_a, n * LEVELS + l)
                            if l == LEVELS - 1:
                                pool.wait_ge(o_mm, n)
                            pool.tensor_tensor(halves(QB[nxt][:], l)[:, :, 0, :], halves(QB[cur][:], l)[:, :, 0, :],
                                               bcast_inner(pb[:, :, 1], 1 << l), ALU.mult)
                            pool.tensor_tensor(halves(KB[nxt][:], l)[:, :, 1, :], halves(KB[cur][:], l)[:, :, 1, :],
                                               bcast_inner(pb[:, :, 0], 1 << l), ALU.mult)
                            pool.tensor_tensor(PB[l][:].rearrange("p j n -> p (j n)"), pb[:, :, 0], pb[:, :, 1],
                                               ALU.mult).then_inc(up_p, 1)
                            pool.wait_ge(up_p, n * LEVELS + l + 1)

            @block.scalar
            def _(act):
                with act.Fori(0, CHUNKS // 2) as i:
                    for r in range(2):
                        n = i * 2 + r
                        for name in ("ff", "fb"):
                            act.wait_ge(loaded[name][r], i * 16 + 16)
                            nc.scalar.activation(inp[name][r][:], inp[name][r][:], ACT.Sigmoid).then_inc(sig, 1)
                        act.wait_ge(loaded["gate"][r], i * 16 + 16)
                        nc.scalar.activation(inp["gate"][r][:], inp["gate"][r][:], ACT.Silu).then_inc(silu, 1)
                        act.wait_ge(init_v, n * 2 + 2)
                        act.wait_ge(init_p, n * 2 + 2)
                        for l in range(LEVELS):
                            cur, nxt = l % 2, (l + 1) % 2
                            act.wait_ge(lvl, n * (LEVELS + 1) + l + 1)
                            if l:
                                act.wait_ge(up_v, n * LEVELS + l)
                                act.wait_ge(up_p, n * LEVELS + l)
                                act.wait_ge(up_a, n * LEVELS + l)
                            if l == LEVELS - 1:
                                act.wait_ge(o_mm, n)
                                act.wait_ge(ktr, n)
                            for x, h in ((QF, 0), (KF, 1), (QB, 1), (KB, 0)):
                                last = nc.scalar.activation(halves(x[nxt][:], l)[:, :, h, :], halves(x[cur][:], l)[:, :, h, :],
                                                            ACT.Copy)
                            last.then_inc(up_a, 1)
                        act.wait_ge(ktr, n + 1)
                        act.wait_ge(kvs, n)
                        nc.scalar.activation(ktok[:], bank[5][:], ACT.Copy).then_inc(kev, 1)
                        act.wait_ge(o_mm, n + 1)
                        act.wait_ge(o_ss, n)
                        nc.scalar.activation(sq[:], bank[4][:], ACT.Square).then_inc(o_sqd, 1)
                        act.wait_ge(o_ss, n + 1)
                        nc.scalar.activation(rs[:], ss[:], ACT.Sqrt, bias=g["eps"][:], scale=1.0 / HEAD).then_inc(o_rms, 1)

            @block.vector
            def _(dve):
                with dve.Fori(0, CHUNKS // 2) as i:
                    for r in range(2):
                        n = i * 2 + r
                        f, q = inp["ff"][r], inp["q"][r]
                        dve.wait_ge(gate_f, n * 2 + 1)
                        dve.wait_ge(loaded["q"][r], i * 16 + 16)
                        dve.wait_ge(lvl, n * (LEVELS + 1))
                        dve.tensor_tensor(QF[0][:], q[:], f[:], ALU.mult).then_inc(init_v, 1)
                        dve.wait_ge(init_p, n * 2 + 1)
                        dve.tensor_tensor(kd[:], KF[0][:], KB[0][:], ALU.add).then_inc(init_v, 1)
                        dve.wait_ge(init_v, n * 2 + 2)
                        dve.wait_ge(o_mm, n)
                        for l in range(-1, LEVELS):
                            base = n * (LEVELS + 1) + l + 2
                            if l >= 0:
                                cur, nxt = l % 2, (l + 1) % 2
                                pf = whole(f[:] if l == 0 else PF[l - 1][:], l)
                                dve.wait_ge(lvl, n * (LEVELS + 1) + l + 1)
                                if l:
                                    dve.wait_ge(up_a, n * LEVELS + l)
                                if l == LEVELS - 1:
                                    dve.wait_ge(ktr, n)
                                dve.tensor_tensor(halves(QF[nxt][:], l)[:, :, 1, :], halves(QF[cur][:], l)[:, :, 1, :],
                                                  bcast_inner(pf[:, :, 0], 1 << l), ALU.mult)
                                dve.tensor_tensor(halves(KF[nxt][:], l)[:, :, 0, :], halves(KF[cur][:], l)[:, :, 0, :],
                                                  bcast_inner(pf[:, :, 1], 1 << l), ALU.mult)
                                dve.tensor_tensor(PF[l][:].rearrange("p j n -> p (j n)"), pf[:, :, 0], pf[:, :, 1],
                                                  ALU.mult).then_inc(up_v, 1)
                                dve.wait_ge(up_v, n * LEVELS + l + 1)
                            wait_apart(dve, lvl, base, passed)
                            for half in range(2):
                                b = bank[2 * ((l + 1) % 2) + half][:].rearrange("p (j n) -> p j n", j=CT)
                                if l < 0:
                                    ins = dve.tensor_tensor(score[:, half, :, :], b,
                                                            g["ident"][:].unsqueeze(1).to_broadcast([P, CT, P]), ALU.mult)
                                else:
                                    ins = dve.copy_predicated(score[:, half, :, :],
                                                              masks[:, l, :].unsqueeze(1).to_broadcast([P, CT, P]), b)
                            ins.then_inc(taken, 1)
                            dve.wait_ge(taken, base)
                        dc = Chain(dve, vch, n * 2)
                        dve.wait_ge(st, n * 2)
                        dc.link(dve.tensor_tensor(decayed[:], s_fwd[r][:], bcast_inner(PF[LEVELS - 1][:, :, 0], P), ALU.mult))
                        dve.wait_ge(kvs, n + 1)
                        dve.wait_ge(o_mm, n)
                        for half in range(2):
                            at = slice(half * HEAD, (half + 1) * HEAD)
                            kv = bank[6][at, :].rearrange("p (j n) -> p j n", j=CT)[:, :, at]
                            dve.tensor_tensor(s_fwd[1 - r][at, :, at], decayed[at, :, at], kv, ALU.add).then_inc(st, 1)
                        dve.wait_ge(o_sqd, n + 1)
                        dve.wait_ge(o_rms, n)
                        dve.tensor_reduce(ss[:], sq[:].rearrange("p (h e) -> p h e", e=HEAD), AX, ALU.add).then_inc(o_ss, 1)
                        dve.wait_ge(o_rms, n + 1)
                        dc.link(dve.reciprocal(rinv[:], rs[:]))
                        dve.wait_ge(o_tr, n)
                        dve.tensor_tensor(on[:].rearrange("p (h e) -> p h e", e=HEAD), bank[4][:].rearrange("p (h e) -> p h e", e=HEAD),
                                          bcast_inner(rinv[:], HEAD), ALU.mult).then_inc(o_n, 1)
                        dve.wait_ge(o_tr, n + 1)
                        dve.wait_ge(silu, n + 1)
                        dve.wait_ge(mrg_out[r], i * 16)
                        dve.tensor_tensor(mrg[r][:], bank[7][:].rearrange("p (j n) -> p j n", j=CT), inp["gate"][r][:],
                                          ALU.mult).then_inc(mrg_done, 1)

            @block.tensor
            def _(pe):
                with pe.Fori(0, CHUNKS // 2) as i:
                    for r in range(2):
                        n = i * 2 + r
                        q = inp["q"][r]
                        pe.wait_ge(init_v, n * 2 + 2)
                        pe.wait_ge(init_p, n * 2 + 2)
                        for l in range(-1, LEVELS):
                            cur = l % 2
                            if l >= 1:
                                pe.wait_ge(up_v, n * LEVELS + l)
                                pe.wait_ge(up_p, n * LEVELS + l)
                                pe.wait_ge(up_a, n * LEVELS + l)
                            pe.wait_ge(taken, n * (LEVELS + 1) + (l if l > 0 else 0))
                            for half in range(2):
                                at = slice(half * HEAD, (half + 1) * HEAD)
                                for j in range(CT):
                                    out = bank[2 * ((l + 1) % 2) + half][:, j * P:(j + 1) * P]
                                    if l < 0:
                                        mm = pe.matmul(out, kd[at, j, :], q[at, j, :], start=True, stop=True)
                                        continue
                                    two = lambda x, w: x.rearrange("p (n two a) -> p n two a", two=2, a=1 << l)[:, :, w, :]
                                    pe.matmul(two(out, 1), KF[cur][at, j, :], two(QF[cur][at, j, :], 1), start=True, stop=True)
                                    mm = pe.matmul(two(out, 0), KB[cur][at, j, :], two(QB[cur][at, j, :], 0), start=True, stop=True)
                            mm.then_inc(lvl, 1)
                        last = LEVELS % 2
                        pe.wait_ge(up_v, n * LEVELS + LEVELS)
                        pe.wait_ge(up_p, n * LEVELS + LEVELS)
                        pe.wait_ge(up_a, n * LEVELS + LEVELS)
                        pe.wait_ge(kev, n)
                        for j in range(CT):
                            tr = pe.transpose(bank[5][:, j * P:(j + 1) * P], KF[last][:, j, :], g["ident"][:])
                        tr.then_inc(ktr, 1)
                        pe.wait_ge(st, n * 2)
                        pe.wait_ge(mrg_done, n)
                        for j in range(CT):
                            at = slice(j * P, (j + 1) * P)
                            pe.matmul(bank[4][:, at], QF[last][:, j, :], s_fwd[r][:, j, :], start=(j == 0), stop=False,
                                      skip_group_check=True)
                            pe.matmul(bank[4][:, at], QB[last][:, j, :], s_bwd[:, ds(n + 1, 1), j, :], start=False, stop=False,
                                      skip_group_check=True)
                        pe.wait_ge(kev, n + 1)
                        for j in range(CT):
                            mm = pe.matmul(bank[6][:, j * P:(j + 1) * P], ktok[:, j * P:(j + 1) * P],
                                           v_tok[:, ds(n, 1), j * P:(j + 1) * P], start=True, stop=True)
                        mm.then_inc(kvs, 1)
                        pe.wait_ge(taken, (n + 1) * (LEVELS + 1))
                        for j in range(CT):
                            for half in range(2):
                                at = slice(j * P + half * HEAD, j * P + (half + 1) * HEAD)
                                mm = pe.matmul(bank[4][:, at], score[:, half, j, :], v_tok[:, ds(n, 1), at], start=False,
                                               stop=(j == CT - 1 and half == 1), skip_group_check=True)
                        mm.then_inc(o_mm, 1)
                        pe.wait_ge(o_n, n + 1)
                        for j in range(CT):
                            tr = pe.transpose(bank[7][:, j * P:(j + 1) * P], on[:, j * P:(j + 1) * P], g["ident"][:])
                        tr.then_inc(o_tr, 1)


def phase_output(nc, t, g):
    with ExitStack() as ctx:
        sb = lambda n, s, d=F32: ctx.enter_context(nc.sbuf_tensor(n, s, d))
        sem = ctx.enter_context(semaphores(nc))
        sem2 = lambda n: [sem(f"{n}{i}") for i in range(2)]
        lru_ps = ctx.enter_context(nc.psum_tensor("lru_ps", [P, D], F32))
        hg_ps = ctx.enter_context(nc.psum_tensor("hg_ps", [P, D], F32))
        tr_ps = ctx.enter_context(nc.psum_tensor("tr_ps", [P, D], F32))
        sum_ps = ctx.enter_context(nc.psum_tensor("sum_ps", [P, BANK], F32))
        rt_ps = ctx.enter_context(nc.psum_tensor("rt_ps", [P, BANK], F32))
        wo = sb("wo", [P, KD, D])
        wr = sb("wr", [P, KD, ROUTES])
        wrs = sb("wrs", [P, KD, ROUTES])
        bias = sb("route_bias_all", [1, ROUTES])
        m = [sb(f"merged{i}", [P, KD, P]) for i in range(2)]
        xr = [sb(f"x_row{i}", [P, D]) for i in range(2)]
        x2 = [sb(f"x2_{i}", [P, D]) for i in range(2)]
        xh = [sb(f"xh_{i}", [P, D]) for i in range(2)]
        sq = [sb(f"lru_sq{i}", [P, CT, P]) for i in range(2)]
        junk = [sb(f"x2_sq{i}", [P, D]) for i in range(2)]
        xt = [sb(f"xh_t{i}", [P, KD, P]) for i in range(2)]
        st = [sb(f"stat{i}", [P, 8]) for i in range(2)]
        wo_in, wr_in, wo_done, wr_done, bias_ps, bias_done = (sem(n) for n in (
            "wo_in", "wr_in", "wo_done", "wr_done", "bias_ps", "bias_done"))
        m_in, xr_in, x2_out, xh_out = sem2("m_in"), sem2("xr_in"), sem2("x2_out"), sem2("xh_out")
        sq_done, sum_mm, lru_rms, lru_r, y_mm, acc, x2_done, x2_sq, x2_rms, x2_r, xh_done, xt_mm, xt_done, rt_mm, lg = (
            sem(n) for n in ("sq_d", "sum_mm", "lru_rms", "lru_r", "y_mm", "acc", "x2_done", "x2_sqd", "x2_rms", "x2_r",
                             "xh_done", "xt_mm", "xt_done", "rt_mm", "lg"))
        block = ctx.enter_context(nc.Block())

        @block.sync
        def _(q):
            q.dma_start(wo[:], t["w_out"][0].rearrange("(k p) n -> p k n", p=P)).then_inc(wo_in, 16)
            q.dma_start(wr[:, :, 0:N_GROUPS], t["router_group_w"][0].rearrange("(k p) n -> p k n", p=P)).then_inc(wr_in, 16)
            q.dma_start(wr[:, :, N_GROUPS:ROUTES], t["router_expert_w"][0].rearrange("(k p) n -> p k n", p=P)).then_inc(wr_in, 16)

            with q.Fori(0, TOK_TILES // 2) as i:
                for r in range(2):
                    row = q.snap(i * (2 * P) + r * P)
                    n = i * 2 + r
                    q.wait_ge(y_mm, i * 2 if r == 0 else i * 2)
                    q.wait_ge(x2_done, i * 2)
                    q.dma_start(m[r][:], t["mergedT"].rearrange("(k p) n -> p k n", p=P)[:, :, ds(row, P)]).then_inc(m_in[r], 16)
                    q.dma_start(xr[r][:], t["x"][0][ds(row, P), :]).then_inc(xr_in[r], 16)
                for r in range(2):
                    row = q.snap(i * (2 * P) + r * P)
                    n = i * 2 + r
                    q.wait_ge(x2_done, n + 1)
                    q.dma_start(t["x2"][ds(row, P), :], x2[r][:]).then_inc(x2_out[r], 16)
                    q.wait_ge(xh_done, n + 1)
                    q.dma_start(t["xh"][ds(row, P), :], xh[r][:]).then_inc(xh_out[r], 16)
            for s in (*x2_out, *xh_out):
                q.wait_ge(s, 16 * (TOK_TILES // 2))

        @block.gpsimd
        def _(pool):
            with pool.Fori(0, TOK_TILES // 2) as i:
                for r in range(2):
                    n = i * 2 + r
                    pool.wait_ge(m_in[r], i * 16 + 16)
                    pool.wait_ge(sum_mm, i * 2)
                    pool.tensor_tensor(sq[r][:], m[r][:, 0:CT, :], m[r][:, 0:CT, :], ALU.mult).then_inc(sq_done, 1)

        @block.scalar
        def _(act):
            with act.Fori(0, TOK_TILES // 2) as i:
                for r in range(2):
                    n = i * 2 + r
                    act.wait_ge(sum_mm, n + 1)
                    nc.scalar.activation(st[r][:, 0:1], sum_ps[:, 0:1], ACT.Sqrt, bias=g["eps"][:], scale=1.0 / CH).then_inc(lru_rms, 1)
                    act.wait_ge(x2_done, n + 1)
                    nc.scalar.activation(junk[r][:], x2[r][:], ACT.Square, accum_out=st[r][:, 2:3]).then_inc(x2_sq, 1)
                    act.wait_ge(x2_sq, n + 1)
                    nc.scalar.activation(st[r][:, 3:4], st[r][:, 2:3], ACT.Sqrt, bias=g["eps"][:], scale=1.0 / D).then_inc(x2_rms, 1)
                    act.wait_ge(xt_mm, n + 1)
                    act.wait_ge(rt_mm, i * 2)
                    nc.scalar.activation(xt[r][:].rearrange("p k n -> p (k n)"), tr_ps[:], ACT.Copy).then_inc(xt_done, 1)

        @block.vector
        def _(dve):
            dve.wait_ge(wo_in, 16)
            for k in range(KD):
                at = (V_NORM_LRU + k) if k < CT else (V_NORM_HG + k - CT)
                ins = dve.scalar_tensor_tensor(out=wo[:, k, :], in0=wo[:, k, :], scalar=g["cols"][:, at:at + 1],
                                               in1=g["gates"][:, 0, :], op0=ALU.mult, op1=ALU.mult)
            ins.then_inc(wo_done, 1)
            dve.wait_ge(wr_in, 32)
            dve.tensor_tensor(wrs[:], wr[:], bcast_inner(g["scale_ffn"][:], ROUTES), ALU.mult).then_inc(wr_done, 1)
            dve.wait_ge(bias_ps, 1)
            dve.tensor_tensor(bias[:], rt_ps[0:1, 0:ROUTES], g["route_bias"][:], ALU.add).then_inc(bias_done, 1)
            with dve.Fori(0, TOK_TILES // 2) as i:
                for r in range(2):
                    n = i * 2 + r
                    dve.wait_ge(lru_rms, n + 1)
                    dve.reciprocal(st[r][:, 1:2], st[r][:, 0:1]).then_inc(lru_r, 1)
                    dve.wait_ge(y_mm, n + 1)
                    dve.wait_ge(lru_r, n + 1)
                    dve.wait_ge(xr_in[r], i * 16 + 16)
                    dve.wait_ge(x2_out[r], i * 16)
                    dve.scalar_tensor_tensor(out=x2[r][:], in0=lru_ps[:], scalar=st[r][:, 1:2], in1=xr[r][:],
                                             op0=ALU.mult, op1=ALU.add).then_inc(acc, 1)
                    dve.wait_ge(acc, n + 1)
                    dve.tensor_tensor(x2[r][:], x2[r][:], hg_ps[:], ALU.add).then_inc(x2_done, 1)
                    dve.wait_ge(x2_rms, n + 1)
                    dve.reciprocal(st[r][:, 4:5], st[r][:, 3:4]).then_inc(x2_r, 1)
                    dve.wait_ge(x2_r, n + 1)
                    dve.wait_ge(xh_out[r], i * 16)
                    dve.wait_ge(xt_mm, i * 2)
                    dve.tensor_scalar(xh[r][:], x2[r][:], st[r][:, 4:5], None, ALU.mult).then_inc(xh_done, 1)
                    dve.wait_ge(rt_mm, n + 1)
                    dve.tensor_copy(g["logits"][:, ds(n, 1), :], rt_ps[:, 0:ROUTES].unsqueeze(1)).then_inc(lg, 1)

        @block.tensor
        def _(pe):
            pe.wait_ge(wr_in, 32)
            for k in range(KD):
                mm = pe.matmul(rt_ps[0:1, 0:ROUTES], g["shift_ffn"][:, k:k + 1], wr[:, k, :], start=(k == 0), stop=(k == KD - 1))
            mm.then_inc(bias_ps, 1)
            pe.wait_ge(wo_done, 1)

            def finish(n, r, i):
                pe.wait_ge(xh_done, n + 1)
                pe.wait_ge(xt_done, n)
                for k in range(KD):
                    tr = pe.transpose(tr_ps[:, k * P:(k + 1) * P], xh[r][:, k * P:(k + 1) * P], g["ident"][:])
                tr.then_inc(xt_mm, 1)
                pe.wait_ge(xt_done, n + 1)
                pe.wait_ge(lg, n)
                for k in range(KD):
                    pe.matmul(rt_ps[:, 0:ROUTES], xt[r][:, k, :], wrs[:, k, :], start=(k == 0), stop=False)
                pe.matmul(rt_ps[:, 0:ROUTES], g["ones"][0:1, :], bias[:], start=False, stop=True).then_inc(rt_mm, 1)

            pe.wait_ge(bias_done, 1)
            with pe.Fori(0, TOK_TILES // 2) as i:
                for r in range(2):
                    n = i * 2 + r
                    pe.wait_ge(sq_done, n + 1)
                    pe.wait_ge(lru_rms, n)
                    for k in range(CT):
                        mm = pe.matmul(sum_ps[:, 0:1], sq[r][:, k, :], g["ones"][:, 0:1], start=(k == 0), stop=(k == CT - 1))
                    mm.then_inc(sum_mm, 1)
                    pe.wait_ge(x2_done, n)
                    for ps, first in ((lru_ps, 0), (hg_ps, CT)):
                        for k in range(CT):
                            for h in range(2):
                                mm = pe.matmul(ps[:, h * BANK:(h + 1) * BANK], m[r][:, first + k, :],
                                               wo[:, first + k, h * BANK:(h + 1) * BANK], start=(k == 0), stop=(k == CT - 1),
                                               skip_group_check=True)
                    mm.then_inc(y_mm, 1)
                    finish(n, r, i)


def phase_route(nc, t, g):
    J = ASSIGN // 2 // P
    with ExitStack() as ctx:
        sb = lambda n, s, d=F32: ctx.enter_context(nc.sbuf_tensor(n, s, d))
        sem = ctx.enter_context(semaphores(nc))
        pos_ps = ctx.enter_context(nc.psum_tensor("pos_ps", [P, TOK_TILES, EXPERTS], F32))
        cnt_ps = ctx.enter_context(nc.psum_tensor("cnt_ps", [P, BANK], F32))
        T_, lg = TOK_TILES, g["logits"]
        g8 = sb("g8", [P, T_, 8])
        gm, em = sb("gm", [P, T_, 8]), sb("em", [P, T_, 8])
        gi, ei = sb("gi", [P, T_, 8], U32), sb("ei", [P, T_, 8], U32)
        gif, eif = sb("gif", [P, T_]), sb("eif", [P, T_, 2])
        ohg = sb("ohg", [P, T_, N_GROUPS])
        neg = sb("neg", [P, T_, N_GROUPS])
        ge_ = sb("g_exp", [P, T_, N_GROUPS])
        pg, dd, one_p = sb("p_group", [P, T_]), sb("top_gap", [P, T_]), sb("one_plus", [P, T_])
        el = sb("el", [P, T_, EXPERTS])
        oh = [sb(f"oh{k}", [P, T_, EXPERTS]) for k in range(2)]
        both = sb("both", [P, T_, EXPERTS])
        pre = sb("pre", [P, T_ + 1, EXPERTS])
        tri = sb("tri", [P, P])
        iota32, iotaJ, iotaW, tokid = sb("iota32", [P, EXPERTS]), sb("iotaJ", [P, J]), sb("iotaW", [P, WINDOWS + 1]), sb("tokid", [P, T_], I32)
        over = sb("over", [P, EXPERTS, J])
        nwin, pend, start = sb("nwin", [P, EXPERTS]), sb("pend", [P, EXPERTS]), sb("start_row", [P, EXPERTS])
        pos, picked, dest_f = sb("pos", [P, T_, EXPERTS]), sb("picked", [P, T_, EXPERTS]), sb("dest_f", [P, T_])
        wle, wexp = sb("wle", [1, WINDOWS + 1, EXPERTS]), sb("wexp", [1, WINDOWS + 1])
        zero_i = sb("zero_i", [P, WINDOWS + 2], I32)
        cst, chain, tri_set, gexp, texp, both_done, pos_mm, scat_ready, zero_in, scat = (sem(n) for n in (
            "r_consts", "r_chain", "tri_set", "g_expd", "t_expd", "both_done", "pos_mm", "scat_ready", "zero_stored", "scattered"))
        block = ctx.enter_context(nc.Block())

        @block.gpsimd
        def _(pool):
            pool.iota(iota32[:], [[1, EXPERTS]], base=0, channel_multiplier=0, allow_small_or_imprecise_dtypes=True)
            pool.iota(iotaJ[:], [[P, J]], base=0, channel_multiplier=0, allow_small_or_imprecise_dtypes=True)
            pool.iota(iotaW[:], [[1, WINDOWS + 1]], base=0, channel_multiplier=0, allow_small_or_imprecise_dtypes=True)
            pool.iota(tokid[:], [[P, T_]], base=0, channel_multiplier=1)
            pool.memset(zero_i[:], 0)
            pool.memset(g8[:], -3.0e38)
            pool.memset(pre[:, 0, :], 0.0)
            pool.memset(tri[:], 1.0).then_inc(tri_set, 1)
            pool.wait_ge(tri_set, 1)
            pool.affine_select(out=tri[:], in_=tri[:], compare_op=ALU.is_gt, fill=0.0, base=0, pattern=[[1, P]],
                               channel_multiplier=-1).then_inc(cst, 1)
            pool.wait_ge(cst, 1)
            pool.dma_start(t["slot_tok"].rearrange("(p w) a -> p (w a)", p=P), zero_i[:]).then_inc(zero_in, 16)
            pool.wait_ge(zero_in, 16)
            pool.wait_ge(scat_ready, 1)
            for i in range(T_):
                for k in range(2):
                    pool.indirect_dma_start(t["slot_tok"], bass.IndirectOffsetOnAxis(ap=g["dest"][k][:, i:i + 1], axis=0),
                                            tokid[:, i:i + 1], None).then_inc(scat, 16)
            pool.wait_ge(scat, 16 * 2 * T_)

        @block.scalar
        def _(act):
            act.wait_ge(gexp, 1)
            nc.scalar.activation(ge_[:], ge_[:], ACT.Exp).then_inc(gexp, 1)
            act.wait_ge(texp, 1)
            nc.scalar.activation(dd[:], dd[:], ACT.Exp).then_inc(texp, 1)

        @block.vector
        def _(dve):
            c = Chain(dve, chain)
            dve.wait_ge(cst, 1)
            c.link(dve.tensor_copy(g8[:, :, 0:N_GROUPS], lg[:, :, 0:N_GROUPS]))
            for i in range(T_):
                last = dve.max(gm[:, i, :], g8[:, i, :])
            c.link(last)
            for i in range(T_):
                last = dve.max_index(gi[:, i, :], gm[:, i, :], g8[:, i, :])
            c.link(last)
            c.link(dve.tensor_copy(gif[:], gi[:, :, 0]))
            c.link(dve.tensor_tensor(ohg[:], iota32[:, 0:N_GROUPS].unsqueeze(1).to_broadcast([P, T_, N_GROUPS]),
                                     bcast_inner(gif[:], N_GROUPS), ALU.is_equal))
            dve.tensor_tensor(ge_[:], lg[:, :, 0:N_GROUPS], bcast_inner(gm[:, :, 0], N_GROUPS), ALU.subtract).then_inc(gexp, 1)
            dve.wait_ge(gexp, 2)
            c.link(dve.tensor_reduce(pg[:], ge_[:], AX, ALU.add))
            c.link(dve.tensor_scalar(neg[:], ohg[:], -1.0, 3.0e38, ALU.add, ALU.mult))
            e4 = lambda x: x.rearrange("p t (g e) -> p t g e", g=N_GROUPS)
            c.link(dve.tensor_tensor(e4(el[:]), e4(lg[:, :, N_GROUPS:ROUTES]), bcast_inner(ohg[:], EPG), ALU.mult))
            c.link(dve.tensor_tensor(e4(el[:]), e4(el[:]), bcast_inner(neg[:], EPG), ALU.add))
            for i in range(T_):
                last = dve.max(em[:, i, :], el[:, i, :])
            c.link(last)
            for i in range(T_):
                last = dve.max_index(ei[:, i, :], em[:, i, :], el[:, i, :])
            c.link(last)
            c.link(dve.tensor_copy(eif[:], ei[:, :, 0:2]))
            dve.tensor_tensor(dd[:], em[:, :, 1], em[:, :, 0], ALU.subtract).then_inc(texp, 1)
            dve.wait_ge(texp, 2)
            c.link(dve.tensor_scalar(one_p[:], dd[:], 1.0, None, ALU.add))
            c.link(dve.tensor_tensor(one_p[:], one_p[:], pg[:], ALU.mult))
            c.link(dve.reciprocal(g["weight"][0][:], one_p[:]))
            dve.tensor_tensor(g["weight"][1][:], g["weight"][0][:], dd[:], ALU.mult)
            for k in range(2):
                last = dve.tensor_tensor(oh[k][:], iota32[:].unsqueeze(1).to_broadcast([P, T_, EXPERTS]),
                                         bcast_inner(eif[:, :, k], EXPERTS), ALU.is_equal)
            c.link(last)
            c.link(dve.tensor_tensor(both[:], oh[0][:], oh[1][:], ALU.add))
            for i in range(T_):
                ins = dve.tensor_tensor(pre[:, i + 1, :], pre[:, i, :], both[:, i, :], ALU.add)
                if i < T_ - 1:
                    c.link(ins)
                else:
                    ins.then_inc(both_done, 1)
            dve.wait_ge(pos_mm, 1)
            c.link(dve.tensor_tensor(over[:], bcast_inner(cnt_ps[:, 0:EXPERTS], J),
                                     iotaJ[:].unsqueeze(1).to_broadcast([P, EXPERTS, J]), ALU.is_gt))
            c.link(dve.tensor_reduce(nwin[:], over[:], AX, ALU.add))
            c.link(dve.tensor_tensor_scan(pend[:], g["ones"][:, 0:EXPERTS], nwin[:], 0.0, ALU.mult, ALU.add))
            c.link(dve.tensor_tensor(start[:], pend[:], nwin[:], ALU.subtract))
            c.link(dve.tensor_scalar(start[:], start[:], float(P), None, ALU.mult))
            c.link(dve.tensor_tensor(pos[:], pos_ps[:], start[:].unsqueeze(1).to_broadcast([P, T_, EXPERTS]), ALU.add))
            for k in range(2):
                c.link(dve.tensor_tensor(picked[:], pos[:], oh[k][:], ALU.mult))
                c.link(dve.tensor_reduce(dest_f[:], picked[:], AX, ALU.add))
                c.link(dve.tensor_copy(g["dest"][k][:], dest_f[:]))
            dve.wait_ge(chain, c.n)
            c.link(dve.tensor_tensor(wle[:], pend[0:1, :].unsqueeze(1).to_broadcast([1, WINDOWS + 1, EXPERTS]),
                                     bcast_inner(iotaW[0:1, :], EXPERTS), ALU.is_le))
            c.link(dve.tensor_reduce(wexp[:], wle[:], AX, ALU.add))
            c.link(dve.tensor_scalar(wexp[:], wexp[:], float(EXPERTS - 1), None, ALU.min))
            c.link(dve.tensor_scalar(wexp[:, WINDOWS:WINDOWS + 1], pend[0:1, EXPERTS - 1:EXPERTS], -1.0, None, ALU.add))
            dve.tensor_copy(g["window"][:], wexp[:]).then_inc(scat_ready, 1)

        @block.tensor
        def _(pe):
            pe.wait_ge(both_done, 1)
            pe.matmul(pos_ps[:].rearrange("p t e -> p (t e)"), tri[:], both[:].rearrange("p t e -> p (t e)"), start=True, stop=False)
            pe.matmul(pos_ps[:].rearrange("p t e -> p (t e)"), g["ones"][:],
                      pre[:, 0:T_, :].rearrange("p t e -> p (t e)"), start=False, stop=True)
            pe.matmul(cnt_ps[:, 0:EXPERTS], g["ones"][:], pre[:, T_, :], start=True, stop=True).then_inc(pos_mm, 1)


def phase_experts(nc, t, g):
    with ExitStack() as ctx:
        sb = lambda n, s, d=F32: ctx.enter_context(nc.sbuf_tensor(n, s, d))
        sem = ctx.enter_context(semaphores(nc))
        FT = F_EXP // P
        xt_ps = ctx.enter_context(nc.psum_tensor("e_xt_ps", [P, D], F32))
        gate_ps = ctx.enter_context(nc.psum_tensor("e_gate_ps", [P, BANK], F32))
        up_ps = ctx.enter_context(nc.psum_tensor("e_up_ps", [P, BANK], F32))
        at_ps = ctx.enter_context(nc.psum_tensor("e_at_ps", [P, BANK], F32))
        y_ps = ctx.enter_context(nc.psum_tensor("e_y_ps", [P, D], F32))
        wg = sb("e_wg", [P, 2, KD, F_EXP])
        wu = sb("e_wu", [P, 2, KD, F_EXP])
        wd = sb("e_wd", [P, 2, FT, D])
        idx = sb("e_idx", [P, 1], I32)
        xrow = sb("e_xrow", [P, D])
        xt = sb("e_xt", [P, KD, P])
        sg = sb("e_sg", [P, F_EXP])
        prod = sb("e_prod", [P, F_EXP])
        prodT = sb("e_prodT", [P, FT, P])
        y = sb("e_y", [P, D])
        gin, uin, din = ([sem(f"e_{n}_in{b}") for b in range(2)] for n in ("wg", "wu", "wd"))
        idx_in, x_in, xt_mm, xt_act, xt_dve, gu_mm, sg_done, prod_done, at_mm, at_done, y_mm, y_act, y_dve, y_out, passed = (
            sem(n) for n in ("e_idx_in", "e_x_in", "e_xt_mm", "e_xt_act", "e_xt_dve", "e_gu_mm", "e_sg_done", "e_prod_done",
                             "e_at_mm", "e_at_done", "e_y_mm", "e_y_act", "e_y_dve", "e_y_out", "e_passed"))
        block = ctx.enter_context(nc.Block())

        def windows(eng, body):
            body(0, 0, True)
            body(0, 1, False)
            with eng.Fori(1, SURE // 2) as i:
                body(i, 0, False)
                body(i, 1, False)
            last = eng.value_load(g["window"][0:1, WINDOWS:WINDOWS + 1], min_val=SURE - 1, max_val=WINDOWS - 1)
            with eng.Fori(SURE // 2, (WINDOWS + 1) // 2) as i:
                for r in range(2):
                    with eng.If(i * 2 + r < last + 1):
                        body(i, r, False)
                    with eng.Else():
                        eng.sem_inc(passed, 1)
            return last

        @block.sync
        def _(q):
            def body(i, r, first):
                w = i * 2 + r
                e = q.value_load(g["window"][0:1, ds(w, 1)], min_val=0, max_val=EXPERTS - 1)
                src = lambda name: t[name][0][ds(e, 1), :, :].rearrange("e (k p) n -> p (e k) n", p=P)
                if not (isinstance(i, int) and i == 0):
                    wait_apart(q, gu_mm, w - 1, passed)
                q.dma_start(wg[:, r, :, :], src("expert_w_gate")).then_inc(gin[r], 16)
                q.dma_start(wu[:, r, :, :], src("expert_w_up")).then_inc(uin[r], 16)
                if not (isinstance(i, int) and i == 0):
                    wait_apart(q, y_mm, w - 1, passed)
                q.dma_start(wd[:, r, :, :], src("expert_w_down")).then_inc(din[r], 16)

            windows(q, body)

        @block.gpsimd
        def _(pool):
            def gather(v):
                pool.dma_start(idx[:], t["slot_tok"][ds(v * P, P), :]).then_inc(idx_in, 16)
                pool.wait_ge(idx_in, v * 16 + 16)
                wait_apart(pool, xt_mm, v, passed)
                pool.indirect_dma_start(xrow[:], None, t["xh"], bass.IndirectOffsetOnAxis(ap=idx[:], axis=0)).then_inc(x_in, 16)
                wait_apart(pool, x_in, v * 16 + 16, passed)

            gather(0)
            windows(pool, lambda i, r, first: gather(i * 2 + r + 1))

        @block.scalar
        def _(act):
            def turn(v):
                for k in range(KD // 2):
                    if k == 0:
                        act.wait_ge(gu_mm, v)
                        act.wait_ge(xt_mm, v + 1)
                    ins = nc.scalar.activation(xt[:, k, :], xt_ps[:, k * P:(k + 1) * P], ACT.Identity,
                                               bias=g["shift_ffn"][:, k:k + 1], scale=g["scale_ffn"][:, k:k + 1])
                ins.then_inc(xt_act, 1)

            def store(v):
                act.wait_ge(y_mm, v + 1)
                act.wait_ge(y_out, v * 16)
                nc.scalar.activation(y[:, 0:BANK], y_ps[:, 0:BANK], ACT.Copy).then_inc(y_act, 1)
                act.wait_ge(y_act, v + 1)
                act.wait_ge(y_dve, v + 1)
                act.dma_start(t["ybuf"][ds(v * P, P), :], y[:]).then_inc(y_out, 16)

            def body(i, r, first):
                w = i * 2 + r
                act.wait_ge(gu_mm, w + 1)
                act.wait_ge(prod_done, w)
                nc.scalar.activation(sg[:], gate_ps[:], ACT.Silu).then_inc(sg_done, 1)
                turn(w + 1)
                if not first:
                    store(w - 1)
                act.wait_ge(at_mm, w + 1)
                act.wait_ge(y_mm, w)
                nc.scalar.activation(prodT[:].rearrange("p k n -> p (k n)"), at_ps[:], ACT.Copy).then_inc(at_done, 1)

            turn(0)
            last = windows(act, body)
            store(last)
            act.wait_ge(y_out, last * 16 + 16)
            act.sem_inc(passed, 1)

        @block.vector
        def _(dve):
            def turn(v):
                for k in range(KD // 2, KD):
                    if k == KD // 2:
                        dve.wait_ge(gu_mm, v)
                        dve.wait_ge(xt_mm, v + 1)
                    ins = dve.tensor_scalar(xt[:, k, :], xt_ps[:, k * P:(k + 1) * P], g["scale_ffn"][:, k:k + 1],
                                            g["shift_ffn"][:, k:k + 1], ALU.mult, ALU.add)
                ins.then_inc(xt_dve, 1)

            def store(v):
                dve.wait_ge(y_mm, v + 1)
                dve.wait_ge(y_out, v * 16)
                dve.tensor_copy(y[:, BANK:D], y_ps[:, BANK:D]).then_inc(y_dve, 1)

            def body(i, r, first):
                w = i * 2 + r
                dve.wait_ge(sg_done, w + 1)
                dve.wait_ge(at_mm, w)
                dve.tensor_tensor(prod[:], up_ps[:], sg[:], ALU.mult).then_inc(prod_done, 1)
                turn(w + 1)
                if not first:
                    store(w - 1)

            turn(0)
            last = windows(dve, body)
            store(last)

        @block.tensor
        def _(pe):
            def turn(v):
                pe.wait_ge(x_in, v * 16 + 16)
                pe.wait_ge(xt_act, v)
                pe.wait_ge(xt_dve, v)
                for k in range(KD):
                    tr = pe.transpose(xt_ps[:, k * P:(k + 1) * P], xrow[:, k * P:(k + 1) * P], g["ident"][:])
                tr.then_inc(xt_mm, 1)

            def down(v, weights):
                pe.wait_ge(at_done, v + 1)
                pe.wait_ge(y_act, v)
                pe.wait_ge(y_dve, v)
                for k in range(FT):
                    for h in range(2):
                        mm = pe.matmul(y_ps[:, h * BANK:(h + 1) * BANK], prodT[:, k, :], weights(k, h), start=(k == 0),
                                       stop=(k == FT - 1), skip_group_check=True)
                mm.then_inc(y_mm, 1)

            def body(i, r, first):
                w = i * 2 + r
                pe.wait_ge(xt_act, w + 1)
                pe.wait_ge(xt_dve, w + 1)
                pe.wait_ge(prod_done, w)
                pe.wait_ge(gin[r], i * 16 + 16)
                pe.wait_ge(uin[r], i * 16 + 16)
                for k in range(KD):
                    pe.matmul(gate_ps[:], xt[:, k, :], wg[:, r, k, :], start=(k == 0), stop=(k == KD - 1))
                    mm = pe.matmul(up_ps[:], xt[:, k, :], wu[:, r, k, :], start=(k == 0), stop=(k == KD - 1))
                mm.then_inc(gu_mm, 1)
                turn(w + 1)
                if not first:
                    down(w - 1, lambda k, h: wd[:, 1 - r, k, h * BANK:(h + 1) * BANK])
                pe.wait_ge(prod_done, w + 1)
                pe.wait_ge(at_done, w)
                for k in range(FT):
                    tr = pe.transpose(at_ps[:, k * P:(k + 1) * P], prod[:, k * P:(k + 1) * P], g["ident"][:])
                tr.then_inc(at_mm, 1)
                wait_apart(pe, din[r], i * 16 + 16, passed)

            turn(0)
            last = windows(pe, body)
            slot = pe.snap(last & 1)
            down(last, lambda k, h: wd[:, ds(slot, 1), k, h * BANK:(h + 1) * BANK])


def phase_combine(nc, t, g):
    with ExitStack() as ctx:
        sb = lambda n, s, d=F32: ctx.enter_context(nc.sbuf_tensor(n, s, d))
        sem = ctx.enter_context(semaphores(nc))
        sem2 = lambda n: [sem(f"{n}{b}") for b in range(2)]
        buf = lambda n, s, d=F32: [sb(f"{n}{b}", s, d) for b in range(2)]
        row = [buf(f"c_idx{k}_", [P, 1], U32) for k in range(2)]
        yr = [buf(f"c_y{k}_", [P, D]) for k in range(2)]
        wt, x2, acc, sq, st, out = (buf(n, s) for n, s in (
            ("c_wt", [P, 2]), ("c_x2", [P, D]), ("c_acc", [P, D]), ("c_sq", [P, D]), ("c_st", [P, 4]), ("c_out", [P, D])))
        x2_in, y_in, outs = sem2("c_x2_in"), [sem2(f"c_y{k}_in") for k in range(2)], sem2("c_outs")
        row_set, wt_set, chain, summed, squared, root, done, used = (sem(n) for n in (
            "c_row_set", "c_wt_set", "c_chain", "c_summed", "c_squared", "c_root", "c_done", "c_used"))
        block = ctx.enter_context(nc.Block())
        N = 3

        @block.sync
        def _(q):
            with q.Fori(0, TOK_TILES // 2) as i:
                for r in range(2):
                    wait_apart(q, summed, i * 2, used)
                    q.dma_start(x2[r][:], t["x2"][ds(i * (2 * P) + r * P, P), :]).then_inc(x2_in[r], 16)
                for r in range(2):
                    wait_apart(q, done, i * 2 + r + 1, used)
                    q.dma_start(t["out"][0][ds(i * (2 * P) + r * P, P), :], out[r][:]).then_inc(outs[r], 16)
            for r in range(2):
                q.wait_ge(outs[r], 16 * (TOK_TILES // 2))

        @block.gpsimd
        def _(pool):
            with pool.Fori(0, TOK_TILES // 2) as i:
                for r in range(2):
                    n = i * 2 + r
                    wait_apart(pool, summed, i * 2, used)
                    for k in range(2):
                        ins = pool.tensor_copy(row[k][r][:], g["dest"][k][:, ds(n, 1)])
                    ins.then_inc(row_set, 1)
                    wait_apart(pool, row_set, n + 1, used)
                    for k in range(2):
                        pool.indirect_dma_start(yr[k][r][:], None, t["ybuf"],
                                                bass.IndirectOffsetOnAxis(ap=row[k][r][:], axis=0)).then_inc(y_in[k][r], 16)

        @block.scalar
        def _(act):
            with act.Fori(0, TOK_TILES // 2) as i:
                for r in range(2):
                    n = i * 2 + r
                    act.wait_ge(summed, n + 1)
                    nc.scalar.activation(sq[r][:], acc[r][:], ACT.Square, accum_out=st[r][:, 0:1]).then_inc(squared, 1)
                    act.wait_ge(squared, n + 1)
                    nc.scalar.activation(st[r][:, 1:2], st[r][:, 0:1], ACT.Sqrt, bias=g["eps"][:], scale=1.0 / D).then_inc(root, 1)

        @block.vector
        def _(dve):
            with dve.Fori(0, TOK_TILES // 2) as i:
                for r in range(2):
                    n = i * 2 + r
                    c = Chain(dve, chain, n * 5)
                    dve.tensor_copy(wt[r][:, 0:1], g["weight"][0][:, ds(n, 1)])
                    c.link(dve.tensor_copy(wt[r][:, 1:2], g["weight"][1][:, ds(n, 1)]))
                    dve.wait_ge(y_in[0][r], i * 16 + 16)
                    c.link(dve.tensor_scalar(acc[r][:], yr[0][r][:], wt[r][:, 0:1], None, ALU.mult))
                    dve.wait_ge(y_in[1][r], i * 16 + 16)
                    c.link(dve.scalar_tensor_tensor(out=acc[r][:], in0=yr[1][r][:], scalar=wt[r][:, 1:2], in1=acc[r][:],
                                                    op0=ALU.mult, op1=ALU.add))
                    c.link(dve.tensor_tensor(acc[r][:], acc[r][:], g["gates"][:, 1, :], ALU.mult))
                    dve.wait_ge(x2_in[r], i * 16 + 16)
                    dve.tensor_tensor(acc[r][:], acc[r][:], x2[r][:], ALU.add).then_inc(summed, 1)
                    dve.wait_ge(root, n + 1)
                    c.link(dve.reciprocal(st[r][:, 2:3], st[r][:, 1:2]))
                    dve.wait_ge(outs[r], i * 16)
                    dve.scalar_tensor_tensor(out=out[r][:], in0=acc[r][:], scalar=st[r][:, 2:3], in1=g["final_w"][:],
                                             op0=ALU.mult, op1=ALU.mult).then_inc(done, 1)


_INS = ['x', 'c', 'ada_w', 'ada_b', 'norm_mix_w', 'w_in', 'conv_w', 'conv_b', 'lru_wa', 'lru_ba', 'lru_wx', 'lru_bx',
        'lru_lambda', 'norm_lru_w', 'hgrn_lb', 'norm_hgrn_w', 'w_out', 'norm_ffn_w', 'router_group_w', 'router_group_b',
        'router_expert_w', 'router_expert_b', 'expert_w_gate', 'expert_w_up', 'expert_w_down', 'final_norm_w']
_SCRATCH = [("projT", (GROUPS * CH, SEQ), F32), ("mergedT", (D, SEQ), F32), ("x2", (SEQ, D), F32), ("xh", (SEQ, D), F32),
            ("slot_tok", ((WINDOWS + 2) * P, 1), I32), ("ybuf", ((WINDOWS + 1) * P, D), F32)]


def build(nc, t):
    for name, shape, dt in _SCRATCH:
        t[name] = nc.dram_tensor(name, shape, dt, kind="Internal").ap()
    with ExitStack() as ctx:
        g = persistent(nc, ctx)
        with ExitStack() as own:
            g["hT"] = own.enter_context(nc.sbuf_tensor("hT", [P, KD, SEQ], F32))
            phase_modulate(nc, t, g)
            phase_project(nc, t, g)
        phase_hgrn(nc, t, g)
        persistent2(nc, ctx, g)
        phase_output(nc, t, g)
        phase_route(nc, t, g)
        phase_experts(nc, t, g)
        phase_combine(nc, t, g)


def kernel(**inputs):
    import numpy as np
    import concourse.bacc as bacc
    from concourse.bass_utils import run_bass_kernel_spmd

    nc = bacc.Bacc("TRN2", target_bir_lowering=False, num_devices=1)
    arrays, t = {}, {}
    for name in _INS:
        a = np.ascontiguousarray(inputs[name])
        arrays[f"in_{name}"] = a
        t[name] = nc.dram_tensor(f"in_{name}", a.shape, mybir.dt.from_np(a.dtype), kind="ExternalInput").ap()
    t["out"] = nc.dram_tensor("out", (1, SEQ, D), F32, kind="ExternalOutput").ap()
    build(nc, t)
    r = run_bass_kernel_spmd(nc, [arrays], core_ids=[0])
    return r.results[0]["out"]
```

```python
from contextlib import ExitStack, contextmanager

import concourse.bass as bass
from concourse import mybir

F32 = mybir.dt.float32
F32R = mybir.dt.float32r
I32 = mybir.dt.int32
U32 = mybir.dt.uint32
ALU = mybir.AluOpType
ACT = mybir.ActivationFunctionType
AX = mybir.AxisListType.X

P = 128
BANK = 512
SEQ = 2048
D = 1024
KD = D // P
CH = 512
CT = CH // P
GROUPS = 7
TOK_TILES = SEQ // P
TOK_CHUNKS = SEQ // BANK
HEAD = 64
EPS = 1e-6
N_GROUPS = 4
EPG = 8
EXPERTS = N_GROUPS * EPG
F_EXP = 512
LRU_C = 8.0
ROUTES = N_GROUPS + EXPERTS
ASSIGN = 2 * SEQ
WINDOWS = EXPERTS + (ASSIGN - EXPERTS) // P
ADA_CHUNKS = 6 * D // BANK
SURE = ASSIGN // P
W_EXPERT, W_NEW, W_COUNT, W_BEFORE = range(4)
ds = bass.ds

V_ADA_B, V_NORM_MIX, V_NORM_FFN, V_CONV_W, V_CONV_B, V_BA, V_BX, V_LAM, V_NORM_LRU, V_LB, V_NORM_HG, V_END = (
    0, 48, 56, 64, 80, 84, 92, 100, 108, 112, 116, 120)


class Chain:

    def __init__(self, eng, sem, base=0):
        self.eng, self.sem, self.base, self.n = eng, sem, base, 0

    def link(self, ins):
        ins.then_inc(self.sem, 1)
        self.n += 1
        self.eng.wait_ge(self.sem, self.base + self.n)


@contextmanager
def semaphores(nc):
    made = []

    def take(name):
        made.append(nc.alloc_semaphore(name))
        return made[-1]

    yield take
    nc.clear_and_free_semaphores(made)
    nc.all_engine_barrier()


def bcast_inner(ap, n):
    return ap.unsqueeze(ap.ndim).to_broadcast(list(ap.shape) + [n])


def phase_modulate(nc, t, g):
    with ExitStack() as ctx:
        sb = lambda n, s, d=F32: ctx.enter_context(nc.sbuf_tensor(n, s, d))
        sem = ctx.enter_context(semaphores(nc))
        bank = [ctx.enter_context(nc.psum_tensor(f"m_bank{i}", [P, BANK], F32)) for i in range(8)]
        cond = sb("cond", [P, KD])
        cond_in = sb("cond_in", [P, KD])
        cond_rep = sb("cond_rep", [P, KD, P])
        rows = sb("rows", [P, P])
        lines = sb("lines", [P, 2 * D])
        mod_row, fin_row, bias_row = lines[0:1, :], lines[32:33, 0:D], lines[HEAD:HEAD + 1, :]
        ada = [sb(f"ada{i}", [P, KD, BANK]) for i in range(3)]
        mod_raw = sb("mod_raw", [P, 2, 16])
        shift = sb("shift_mix", [P, KD])
        scale = sb("scale_mix", [P, KD])
        xg = [sb(f"xg{i}", [P, 4, D]) for i in range(2)]
        xn = sb("xn", [P, 4, D])
        junk = sb("junk", [P, 4, D])
        ssq = sb("ssq", [P, 4])
        std = sb("std", [P, 4])
        rstd = sb("rstd", [P, 4])
        c_in, rows_in, row_in, x_in = sem("c_in"), sem("rows_in"), sem("row_in"), [sem(f"x_in{i}") for i in range(2)]
        ada_in = [sem(f"ada_in{i}") for i in range(3)]
        consts, cond_done, rep_done, rows_zero = sem("consts"), sem("cond_done"), sem("rep_done"), sem("rows_zero")
        cols_ps, cols_sb = sem("cols_ps"), sem("cols_sb")
        mod_ps, mod_sb, chunk_mm, chunk_sb = sem("mod_ps"), sem("mod_sb"), sem("chunk_mm"), sem("chunk_sb")
        affine, fin_ps, dve_chain, pool_chain, act_chain = (
            sem("affine"), sem("fin_ps"), sem("m_dve_chain"), sem("m_pool_chain"), sem("m_act_chain"))
        sq_done, std_done, xn_done, tr_done, h_act, h_dve = (
            sem("sq_done"), sem("std_done"), sem("xn_done"), sem("tr_done"), sem("h_act"), sem("h_dve"))
        block = ctx.enter_context(nc.Block())

        @block.sync
        def _(sp):
            sp.dma_start(cond_in[:], t["c"].rearrange("a (p j) -> (a p) j", j=KD)).then_inc(c_in, 16)
            sp.wait_ge(rows_zero, 1)
            for at, src in (
                (V_ADA_B, t["ada_b"].rearrange("a (r p) -> (a r) p", p=P)),
                (V_NORM_MIX, t["norm_mix_w"].rearrange("a (r p) -> (a r) p", p=P)),
                (V_NORM_FFN, t["norm_ffn_w"].rearrange("a (r p) -> (a r) p", p=P)),
                (V_CONV_W, t["conv_w"].rearrange("a j (r p) -> (a j r) p", p=P)),
                (V_CONV_B, t["conv_b"].rearrange("a (r p) -> (a r) p", p=P)),
                (V_BA, t["lru_ba"].rearrange("a d (r p) -> (a d r) p", p=P)),
                (V_BX, t["lru_bx"].rearrange("a d (r p) -> (a d r) p", p=P)),
                (V_LAM, t["lru_lambda"].rearrange("a d (r p) -> (a d r) p", p=P)),
                (V_NORM_LRU, t["norm_lru_w"].rearrange("a (r p) -> (a r) p", p=P)),
                (V_LB, t["hgrn_lb"].rearrange("a (r p) -> (a r) p", p=P)),
                (V_NORM_HG, t["norm_hgrn_w"].rearrange("a (r p) -> (a r) p", p=P)),
            ):
                sp.dma_start(rows[at:at + src.shape[0], :], src).then_inc(rows_in, 16)
            sp.dma_start(bias_row.rearrange("a (h n) -> a h n", h=2), t["ada_b"].rearrange("a (h v n) -> a h v n", h=2, v=3)[:, :, 2, :]).then_inc(row_in, 16)
            sp.dma_start(fin_row, t["final_norm_w"].rearrange("(a n) -> a n", a=1)).then_inc(row_in, 16)
            sp.dma_start(g["route_bias"][0:1, 0:N_GROUPS], t["router_group_b"]).then_inc(row_in, 16)
            sp.dma_start(g["route_bias"][0:1, N_GROUPS:ROUTES], t["router_expert_b"]).then_inc(row_in, 16)

            def ada_chunks(i):
                for b in range(3):
                    if not (isinstance(i, int) and i == 0):
                        sp.wait_ge(chunk_mm, i * 3 + b - 2)
                    sp.dma_start(ada[b][:], t["ada_w"][0].rearrange("(p j) n -> p j n", j=KD)[
                        :, :, ds(i * (3 * BANK) + b * BANK, BANK)]).then_inc(ada_in[b], 16)

            rounds(sp, ADA_CHUNKS // 3, ada_chunks)

        @block.gpsimd
        def _(pool):
            pc = Chain(pool, pool_chain)
            pool.memset(rows[:], 0.0).then_inc(rows_zero, 1)
            pool.memset(g["ones"][:], 1.0).then_inc(consts, 1)
            pool.memset(g["eps"][:], EPS).then_inc(consts, 1)
            pc.link(pool.memset(g["ident"][:], 0.0))
            pool.affine_select(out=g["ident"][:], in_=g["ident"][:], compare_op=ALU.not_equal, fill=1.0, base=0,
                               pattern=[[-1, P]], channel_multiplier=1).then_inc(consts, 1)
            for i in range(TOK_CHUNKS):
                if i >= 2:
                    pool.wait_ge(xn_done, i - 1)
                    pool.wait_ge(sq_done, i - 1)
                pool.dma_start(xg[i % 2][:], t["x"][0].rearrange("(a p) d -> p a d", p=P)[:, i * 4:i * 4 + 4, :]).then_inc(
                    x_in[i % 2], 16)

        @block.scalar
        def _(act):
            act.wait_ge(c_in, 16)
            nc.scalar.activation(cond[:], cond_in[:], ACT.Silu).then_inc(cond_done, 1)
            act.wait_ge(consts, 3)
            for i in range(TOK_CHUNKS):
                act.wait_ge(x_in[i % 2], (i // 2) * 16 + 16)
                if i > 0:
                    act.wait_ge(std_done, i * 2)
                for a in range(4):
                    last = nc.scalar.activation(junk[:, a, :], xg[i % 2][:, a, :], ACT.Square, accum_out=ssq[:, a:a + 1])
                last.then_inc(sq_done, 1)
                act.wait_ge(sq_done, i + 1)
                nc.scalar.activation(std[:], ssq[:], ACT.Sqrt, bias=g["eps"][:], scale=1.0 / D).then_inc(std_done, 1)
                act.wait_ge(affine, 2)
                for k in range(0, KD, 2):
                    act.wait_ge(tr_done, i * KD + k + 1)
                    nc.scalar.activation(g["hT"][:, k, i * BANK:(i + 1) * BANK], bank[k % 4][:], ACT.Identity,
                                         bias=shift[:, k:k + 1], scale=scale[:, k:k + 1]).then_inc(h_act, 1)

        @block.vector
        def _(dve):
            dve.wait_ge(cond_done, 1)
            dve.tensor_copy(cond_rep[:], bcast_inner(cond[:], P)).then_inc(rep_done, 1)
            dve.wait_ge(cols_ps, 1)
            dve.tensor_copy(g["cols"][:], bank[7][:, 0:P]).then_inc(cols_sb, 1)
            dc = Chain(dve, dve_chain)
            for q in range(2):
                dve.wait_ge(fin_ps, q + 1)
                dve.tensor_copy(g["final_w"][:, q * BANK:(q + 1) * BANK], bank[5 + q][:]).then_inc(cols_sb, 1)

            def chunk_out(n):
                h, q = n // 6, n % 6
                dve.wait_ge(chunk_mm, n + 1)
                if q < 4:
                    if h > 0:
                        dve.wait_ge(mod_ps, h)
                    ins = dve.tensor_copy(mod_row[:, q * BANK:(q + 1) * BANK], bank[5 + n % 2][0:1, :])
                else:
                    ins = dve.tensor_copy(g["gates"][:, h, (q - 4) * BANK:(q - 3) * BANK], bank[5 + n % 2][:])
                ins.then_inc(chunk_sb, 1)

            for n in range(4):
                chunk_out(n)
            dve.wait_ge(mod_ps, 1)
            dve.tensor_copy(mod_raw[:, 0, :], bank[4][:, 0:16]).then_inc(mod_sb, 1)
            dve.wait_ge(mod_sb, 1)
            dve.wait_ge(cols_sb, 1)
            dve.tensor_tensor(shift[:], mod_raw[:, 0, 0:8], g["cols"][:, 0:8], ALU.add).then_inc(affine, 1)
            dc.link(dve.tensor_tensor(scale[:], mod_raw[:, 0, 8:16], g["cols"][:, 8:16], ALU.add))
            dve.scalar_tensor_tensor(out=scale[:], in0=scale[:], scalar=1.0, in1=g["cols"][:, V_NORM_MIX:V_NORM_MIX + 8],
                                     op0=ALU.add, op1=ALU.mult).then_inc(affine, 1)
            dve.wait_ge(affine, 2)

            for i in range(TOK_CHUNKS):
                dve.wait_ge(std_done, i * 2 + 1)
                dve.reciprocal(rstd[:], std[:]).then_inc(std_done, 1)
                dve.wait_ge(std_done, i * 2 + 2)
                if i > 0:
                    dve.wait_ge(tr_done, i * KD)
                dve.wait_ge(x_in[i % 2], (i // 2) * 16 + 16)
                for a in range(4):
                    last = dve.tensor_scalar(xn[:, a, :], xg[i % 2][:, a, :], rstd[:, a:a + 1], None, ALU.mult)
                last.then_inc(xn_done, 1)
                for k in range(1, KD, 2):
                    dve.wait_ge(tr_done, i * KD + k + 1)
                    dve.tensor_scalar(g["hT"][:, k, i * BANK:(i + 1) * BANK], bank[k % 4][:], scale[:, k:k + 1],
                                      shift[:, k:k + 1], ALU.mult, ALU.add).then_inc(h_dve, 1)
                if i == 3:
                    dve.wait_ge(mod_ps, 2)
                    dve.tensor_copy(mod_raw[:, 1, :], bank[4][:, 0:16]).then_inc(mod_sb, 1)
                    dve.wait_ge(mod_sb, 2)
                    dve.tensor_tensor(g["shift_ffn"][:], mod_raw[:, 1, 0:8], g["cols"][:, 24:32], ALU.add)
                    dc.link(dve.tensor_tensor(g["scale_ffn"][:], mod_raw[:, 1, 8:16], g["cols"][:, 32:40], ALU.add))
                    dve.scalar_tensor_tensor(out=g["scale_ffn"][:], in0=g["scale_ffn"][:], scalar=1.0,
                                             in1=g["cols"][:, V_NORM_FFN:V_NORM_FFN + 8], op0=ALU.add, op1=ALU.mult)
                for n in (4 + 2 * i, 5 + 2 * i):
                    chunk_out(n)

        @block.tensor
        def _(pe):
            pe.wait_ge(consts, 3)
            pe.wait_ge(rows_in, 16 * 11)
            pe.transpose(bank[7][:, 0:P], rows[:], g["ident"][:]).then_inc(cols_ps, 1)
            pe.wait_ge(row_in, 64)
            for q in range(2):
                pe.matmul(bank[5 + q][:], g["ones"][32:33, :], fin_row[:, q * BANK:(q + 1) * BANK],
                          start=True, stop=True).then_inc(fin_ps, 1)
            pe.wait_ge(rep_done, 1)
            pe.wait_ge(cond_done, 1)
            pe.wait_ge(cols_sb, 1)

            def modulation(n):
                h, q = n // 6, n % 6
                w, out = ada[n % 3], bank[5 + n % 2]
                pe.wait_ge(ada_in[n % 3], n // 3 * 16 + 16)
                pe.wait_ge(*((cols_sb, 3) if n < 2 else (chunk_sb, n - 1)))
                if q < 4:
                    for j in range(KD):
                        mm = pe.matmul(out[0:1, :], cond[:, j:j + 1], w[:, j, :], start=(j == 0), stop=(j == KD - 1))
                else:
                    for j in range(KD):
                        pe.matmul(out[:], cond_rep[:, j, :], w[:, j, :], start=(j == 0), stop=False)
                    mm = pe.matmul(out[:], g["ones"][HEAD:HEAD + 1, :], bias_row[:, h * D + (q - 4) * BANK:h * D + (q - 3) * BANK],
                                   start=False, stop=True)
                mm.then_inc(chunk_mm, 1)

            def columns(h):
                pe.wait_ge(chunk_sb, 6 * h + 4)
                if h > 0:
                    pe.wait_ge(mod_sb, h)
                for m in range(2 * KD):
                    mm = pe.matmul(bank[4][:, m:m + 1], mod_row[:, m * P:(m + 1) * P], g["ones"][0:1, 0:1], start=True, stop=True)
                mm.then_inc(mod_ps, 1)

            for n in range(4):
                modulation(n)
            columns(0)
            for i in range(TOK_CHUNKS):
                pe.wait_ge(xn_done, i + 1)
                for k in range(KD):
                    before = i * (KD // 2) + k // 2 - 1
                    if before > 0:
                        pe.wait_ge(h_dve if k % 2 else h_act, before)
                    for a in range(4):
                        tr = pe.transpose(bank[k % 4][:, a * P:(a + 1) * P], xn[:, a, k * P:(k + 1) * P], g["ident"][:])
                    tr.then_inc(tr_done, 1)
                if i == 3:
                    columns(1)
                for n in (4 + 2 * i, 5 + 2 * i):
                    modulation(n)


def persistent(nc, ctx):
    sb = lambda n, s, d=F32: ctx.enter_context(nc.sbuf_tensor(n, s, d))
    return dict(
        ident=sb("ident", [P, P]), ones=sb("ones", [P, P]), eps=sb("eps", [P, 1]),
        cols=sb("cols", [P, P]), gates=sb("gates", [P, 2, D]), final_w=sb("final_w", [P, D]),
        shift_ffn=sb("shift_ffn", [P, KD]), scale_ffn=sb("scale_ffn", [P, KD]), route_bias=sb("route_bias", [1, ROUTES]),
    )


def persistent2(nc, ctx, g):
    sb = lambda n, s, d=F32: ctx.enter_context(nc.sbuf_tensor(n, s, d))
    g["logits"] = sb("logits", [P, TOK_TILES, ROUTES])
    g["weight"] = [sb(f"weight{k}", [P, TOK_TILES]) for k in range(2)]
    g["dest"] = [sb(f"dest{k}", [P, TOK_TILES], U32) for k in range(2)]
    g["window"] = sb("window", [1, 4, WINDOWS + 3], I32)


def pos(value):
    return max(value, 0) if isinstance(value, int) else value


def rounds(eng, n, body):
    body(0)
    with eng.Fori(1, n) as i:
        body(i)


def wait_apart(eng, sem, value, passed):
    eng.wait_ge(sem, value)
    eng.sem_inc(passed, 1)


def phase_project(nc, t, g):
    with ExitStack() as ctx:
        sb = lambda n, s, d=F32: ctx.enter_context(nc.sbuf_tensor(n, s, d))
        sem = ctx.enter_context(semaphores(nc))
        bank = [ctx.enter_context(nc.psum_tensor(f"p_bank{i}", [P, BANK], F32)) for i in range(8)]
        hT = g["hT"]
        w = [sb(f"w_in{m}", [P, KD, P]) for m in range(CT)]
        stage = [sb(f"proj_stage{i}", [P, SEQ]) for i in range(2)]
        xin = sb("lru_x", [P, SEQ + 3])
        xc = sb("lru_xc", [P, SEQ])
        y = sb("lru_y", [P, SEQ])
        R = [sb(f"lru_r{d}", [P, SEQ]) for d in range(2)]
        I = [sb(f"lru_i{d}", [P, SEQ]) for d in range(2)]
        T = [sb(f"lru_t{d}", [P, SEQ]) for d in range(2)]
        gw = sb("lru_gate_w", [P, 4, P])
        par = sb("lru_par", [P, 12])
        neg = sb("lru_neg", [P, 2])
        sp = [sb(f"softplus{i}", [P, 8]) for i in range(5)]
        tmp = xin[:, 2:2 + SEQ]
        w_in = [sem(f"w_in_s{m}") for m in range(CT)]
        mm_done, evac, stored = sem("mm_done"), sem("evac"), [sem(f"stored{i}") for i in range(2)]
        x_in, y_in, gw_in, gw_zero = sem("lru_x_in"), sem("lru_y_in"), sem("gw_in"), sem("gw_zero")
        conv_done, gate_mm, gate_act = sem("conv_done"), sem("gate_mm"), sem("gate_act")
        ea, tanh_done, exp_done, pre_root, root_done, gelu_done = (
            sem("softplus_exp"), sem("tanh_done"), sem("exp_done"), sem("pre_root"), sem("root_done"), sem("gelu_done"))
        lru_done, lru_stored, chain, par_done = sem("lru_done"), sem("lru_stored"), sem("lru_chain"), sem("par_done")
        zero_out = sem("zero_out")
        zeros = sb("zeros", [P, D])
        CHAIN = 11
        block = ctx.enter_context(nc.Block())
        src_w = t["w_in"][0].rearrange("(k p) n -> p k n", p=P)

        def over_groups(eng, body):
            body(0, None)
            body(1, None)
            body(2, 0)
            with eng.Fori(1, CT) as i:
                body(i + 2, i)
            body(GROUPS - 1, None)

        @block.sync
        def _(q):
            for m in range(CT):
                q.dma_start(w[m][:], src_w[:, :, m * P:(m + 1) * P]).then_inc(w_in[m], 16)

            def body(gr, i):
                if i is not None:
                    q.wait_ge(lru_stored, i * 16)
                    q.wait_ge(gw_zero, 1)
                    for s in range(2):
                        q.wait_ge(stored[s], 64)
                    q.dma_start(xin[:, 2:2 + SEQ], t["projT"][ds(i * P, P), :]).then_inc(x_in, 16)
                    q.dma_start(y[:], t["projT"][ds(i * P + CH, P), :]).then_inc(y_in, 16)
                    for half in range(2):
                        at = slice(half * HEAD, (half + 1) * HEAD)
                        for gate, name in ((0, "lru_wa"), (2, "lru_wx")):
                            q.dma_start(gw[at, gate:gate + 2, at], t[name][0].rearrange("d h i j -> h i d j")[
                                ds(i * 2 + half, 1), :, :, :].rearrange("h i d j -> (h i) d j")).then_inc(gw_in, 16)
                for m in range(CT):
                    q.wait_ge(evac, gr * 16 + m * 4 + 4)
                    q.dma_start(t["projT"][ds(gr * CH + m * P, P), :], stage[m % 2][:]).then_inc(stored[m % 2], 16)
                    if not (isinstance(gr, int) and gr == GROUPS - 1):
                        q.wait_ge(mm_done, gr * 16 + m * 4 + 4)
                        q.dma_start(w[m][:], src_w[:, :, ds((gr + 1) * CH + m * P, P)]).then_inc(w_in[m], 16)
                if i is not None:
                    q.wait_ge(lru_done, i + 1)
                    q.dma_start(t["mergedT"][ds(i * P, P), :], tmp).then_inc(lru_stored, 16)

            over_groups(q, body)
            q.wait_ge(lru_stored, 16 * CT)
            for s in range(2):
                q.wait_ge(stored[s], 16 * 2 * GROUPS)

        @block.gpsimd
        def _(pool):
            pool.memset(xin[:], 0.0)
            pool.memset(zeros[:], 0.0)
            pool.memset(gw[:], 0.0).then_inc(gw_zero, 1)
            pool.wait_ge(gw_zero, 1)
            with pool.Fori(SURE, WINDOWS + 1) as i:
                pool.dma_start(t["ybuf"][ds(i * P, P), :], zeros[:]).then_inc(zero_out, 16)
            pool.wait_ge(zero_out, 16 * (WINDOWS + 1 - SURE))

        @block.scalar
        def _(act):
            nc.scalar.activation(sp[0][:], g["cols"][:, V_LAM:V_LAM + 8], ACT.Abs).then_inc(ea, 1)
            act.wait_ge(ea, 1)
            nc.scalar.activation(sp[1][:], sp[0][:], ACT.Exp, scale=-1.0).then_inc(ea, 1)

            def body(gr, i):
                for m in range(CT):
                    for c in range(TOK_CHUNKS):
                        act.wait_ge(mm_done, gr * 16 + m * 4 + c + 1)
                        if c == 0:
                            act.wait_ge(stored[m % 2], gr * 32 if m < 2 else gr * 32 + 16)
                        nc.scalar.activation(stage[m % 2][:, c * BANK:(c + 1) * BANK], bank[c][:],
                                             ACT.Copy).then_inc(evac, 1)
                    if i is None:
                        continue
                    if m == 0:
                        act.wait_ge(par_done, i + 1)
                        for k in range(4):
                            dst = (R[0], R[1], I[0], I[1])[k]
                            for c in range(TOK_CHUNKS):
                                act.wait_ge(gate_mm, i * 16 + k * 4 + c + 1)
                                nc.scalar.activation(dst[:, c * BANK:(c + 1) * BANK], bank[4 + c][:], ACT.Sigmoid,
                                                     bias=par[:, 5 + k:6 + k]).then_inc(gate_act, 1)
                    if m == 1:
                        act.wait_ge(gate_act, i * 16 + 16)
                        for d in range(2):
                            nc.scalar.activation(T[d][:], R[d][:], ACT.Tanh, scale=par[:, 9 + d:10 + d]).then_inc(tanh_done, 1)
                        act.wait_ge(tanh_done, i * 2 + 2)
                        for d in range(2):
                            nc.scalar.activation(R[d][:], R[d][:], ACT.Exp, scale=neg[:, d:d + 1]).then_inc(exp_done, 1)
                    if m == 2:
                        for d in range(2):
                            act.wait_ge(pre_root, i * 2 + d + 1)
                            nc.scalar.activation(T[d][:], T[d][:], ACT.Sqrt).then_inc(root_done, 1)
                        act.wait_ge(y_in, i * 16 + 16)
                        nc.scalar.activation(y[:], y[:], ACT.Gelu_apprx_tanh).then_inc(gelu_done, 1)

            over_groups(act, body)

        @block.vector
        def _(dve):
            dc = Chain(dve, chain)
            lam = g["cols"][:, V_LAM:V_LAM + 8]
            dve.wait_ge(ea, 2)
            e, u, z, z2, s = sp[1][:], sp[2][:], sp[3][:], sp[0][:], sp[4][:]
            dc.link(dve.tensor_scalar(u, e, 2.0, None, ALU.add))
            dc.link(dve.reciprocal(u, u))
            dc.link(dve.tensor_tensor(z, e, u, ALU.mult))
            dc.link(dve.tensor_tensor(z2, z, z, ALU.mult))
            dc.link(dve.tensor_scalar(s, z2, 1.0 / 17, 1.0 / 15, ALU.mult, ALU.add))
            for n in (13, 11, 9, 7, 5, 3, 1):
                dc.link(dve.tensor_tensor(s, s, z2, ALU.mult))
                dc.link(dve.tensor_scalar(s, s, 1.0 / n, None, ALU.add))
            dc.link(dve.tensor_tensor(s, s, z, ALU.mult))
            dc.link(dve.tensor_scalar(u, lam, -1.0, 0.0, ALU.mult, ALU.max))
            dc.link(dve.tensor_scalar(u, u, LRU_C, None, ALU.mult))
            dc.link(dve.scalar_tensor_tensor(out=lam, in0=s, scalar=2.0 * LRU_C, in1=u, op0=ALU.mult, op1=ALU.add))
            first = dc.n
            table = g["cols"][:, V_CONV_W:V_LB].rearrange("p (r k) -> p r k", k=CT)
            with dve.Fori(0, CT) as i:
                dc = Chain(dve, chain, i * CHAIN + first)
                dc.link(dve.tensor_copy(par[:].unsqueeze(2), table[:, :, ds(i, 1)]))
                dve.tensor_scalar(neg[:], par[:, 9:11], -1.0, None, ALU.mult).then_inc(par_done, 1)
                dve.wait_ge(x_in, i * 16 + 16)
                dc.link(dve.tensor_scalar(xc[:], xin[:, 0:SEQ], par[:, 0:1], par[:, 4:5], ALU.mult, ALU.add))
                for j in range(1, 4):
                    ins = dve.scalar_tensor_tensor(out=xc[:], in0=xin[:, j:j + SEQ], scalar=par[:, j:j + 1], in1=xc[:],
                                                   op0=ALU.mult, op1=ALU.add)
                    if j < 3:
                        dc.link(ins)
                    else:
                        ins.then_inc(conv_done, 1)
                dve.wait_ge(conv_done, i + 1)
                dve.wait_ge(gate_act, i * 16 + 16)
                for d in range(2):
                    dve.tensor_tensor(I[d][:], I[d][:], xc[:], ALU.mult)
                for d in range(2):
                    dve.wait_ge(exp_done, i * 2 + d + 1)
                    dc.link(dve.tensor_tensor(tmp, R[d][:], R[d][:], ALU.mult))
                    dve.scalar_tensor_tensor(out=T[d][:], in0=tmp, scalar=1.0, in1=T[d][:],
                                             op0=ALU.add, op1=ALU.mult).then_inc(pre_root, 1)
                    dve.wait_ge(pre_root, i * 2 + d + 1)
                for d in range(2):
                    dve.wait_ge(root_done, i * 2 + d + 1)
                    dc.link(dve.tensor_tensor(I[d][:], I[d][:], T[d][:], ALU.mult))
                    if d == 0:
                        dc.link(dve.tensor_tensor_scan(T[0][:], R[0][:], I[0][:], 0.0, ALU.mult, ALU.add))
                    else:
                        dc.link(dve.tensor_tensor_scan(T[1][:, ::-1], R[1][:, ::-1], I[1][:, ::-1], 0.0,
                                                       ALU.mult, ALU.add))
                dc.link(dve.tensor_tensor(T[0][:], T[0][:], T[1][:], ALU.add))
                dve.wait_ge(gelu_done, i + 1)
                dve.tensor_tensor(tmp, T[0][:], y[:], ALU.mult).then_inc(lru_done, 1)
                assert dc.n == CHAIN

        @block.tensor
        def _(pe):
            def body(gr, i):
                for m in range(CT):
                    pe.wait_ge(w_in[m], gr * 16 + 16)
                    for c in range(TOK_CHUNKS):
                        if m == 0:
                            pe.wait_ge(evac, gr * 16)
                        else:
                            pe.wait_ge(evac, gr * 16 + m * 4 + c - 3)
                        for k in range(KD):
                            mm = pe.matmul(bank[c][:], w[m][:, k, :], hT[:, k, c * BANK:(c + 1) * BANK],
                                           start=(k == 0), stop=(k == KD - 1))
                        mm.then_inc(mm_done, 1)
                    if i is not None and m == 0:
                        pe.wait_ge(conv_done, i + 1)
                        pe.wait_ge(gw_in, i * 64 + 64)
                        for k in range(4):
                            for c in range(TOK_CHUNKS):
                                n = k * 4 + c - 3
                                pe.wait_ge(gate_act, i * 16 + n if n > 0 else i * 16)
                                pe.matmul(bank[4 + c][:], gw[:, k, :], xc[:, c * BANK:(c + 1) * BANK],
                                          start=True, stop=True).then_inc(gate_mm, 1)

            over_groups(pe, body)


LEVELS = 7
CHUNKS = TOK_TILES


def phase_hgrn(nc, t, g):
    with ExitStack() as ctx:
        sb = lambda n, s, d=F32: ctx.enter_context(nc.sbuf_tensor(n, s, d))
        sem = ctx.enter_context(semaphores(nc))
        sem2 = lambda n: [sem(f"{n}{i}") for i in range(2)]
        bank = [ctx.enter_context(nc.psum_tensor(f"h_bank{i}", [P, BANK], F32)) for i in range(8)]
        W = [P, CT, P]
        v_tok = sb("v_tok", [P, CHUNKS, CH])
        s_bwd = sb("s_bwd", [P, CHUNKS + 1, CT, P])
        s_fwd = [sb(f"s_fwd{i}", W) for i in range(2)]
        decayed = sb("decayed", W)
        masks = sb("masks", [P, LEVELS, P], I32)
        xor_i = sb("xor_i", [P, 2, P], I32)
        xor_f = sb("xor_f", [P, P])
        ge = sb("ge", [P, LEVELS + 1, P])
        lbt = sb("lbt", [P, 4, CT])
        ones_row = sb("ones_row", [P, P])
        a_f = [sb(f"a_f{i}", W) for i in range(2)]
        a_v = [sb(f"a_v{i}", W) for i in range(2)]
        a_k = [sb(f"a_k{i}", W) for i in range(2)]
        a_e = [sb(f"a_e{i}", W) for i in range(2)]
        a_ktok = [sb(f"a_ktok{i}", [P, CH]) for i in range(2)]
        a_p = [sb(f"a_p{i}", [P, CT]) for i in range(2)]
        sem_names = ("f_in", "v_in", "a_sig", "a_gate", "a_keys", "a_kd", "a_ktr", "a_vtr", "a_kev", "a_vev", "a_kv")
        f_in, v_in, a_sig, a_gate, a_keys, a_kd, a_ktr, a_vtr, a_kev, a_vev, a_kv = (sem2(n) for n in sem_names)
        a_state, a_chain, zeroed, lb_done, lb_exp, mask_chain, iota_done = (
            sem("a_state"), sem("a_chain"), sem("zeroed"), sem("lb_done"), sem("lb_exp"), sem("mask_chain"), sem("iota_done"))
        passed = sem("passed")
        g["masks"], g["v_tok"], g["s_bwd"], g["lbt"] = masks, v_tok, s_bwd, lbt
        src = lambda group, c: t["projT"][group * CH:(group + 1) * CH, :].rearrange("(j p) n -> p j n", p=P)[:, :, ds(c, P)]
        A_CHAIN = 7

        with nc.Block() as block:
            @block.sync
            def _(q):
                def body(i):
                    for r in range(2):
                        c = q.snap((CHUNKS - 1 - r) * P - i * (2 * P))
                        wait_apart(q, a_keys[r], i, passed)
                        q.dma_start(a_f[r][:], src(4, c)).then_inc(f_in[r], 16)
                        q.wait_ge(a_vtr[r], i)
                        q.dma_start(a_v[r][:], src(5, c)).then_inc(v_in[r], 16)

                rounds(q, CHUNKS // 2, body)

            @block.gpsimd
            def _(pool):
                for x in (s_bwd[:], s_fwd[0][:], s_fwd[1][:]):
                    pool.memset(x, 0.0)
                pool.memset(ones_row[:], 1.0)
                for r in range(2):
                    last = pool.memset(a_e[r][:], 1.0)
                last.then_inc(zeroed, 1)
                pool.iota(xor_i[:, 0, :], [[0, P]], base=0, channel_multiplier=1)
                pool.iota(xor_i[:, 1, :], [[1, P]], base=0, channel_multiplier=0).then_inc(iota_done, 1)
                pool.wait_ge(lb_done, 1)
                def body(i):
                    for r in range(2):
                        wait_apart(pool, a_sig[r], i + 1, passed)
                        for j in range(CT):
                            last = pool.tensor_scalar(a_f[r][:, j, :], a_f[r][:, j, :], lbt[:, 3, j:j + 1], lbt[:, 2, j:j + 1],
                                                      ALU.mult, ALU.add)
                        last.then_inc(a_gate[r], 1)
                        pool.wait_ge(a_gate[r], i + 1)
                        wait_apart(pool, a_ktr[r], i, passed)
                        pool.tensor_scalar(a_k[r][:], a_f[r][:], -1.0, 1.0, ALU.mult, ALU.add).then_inc(a_kd[r], 1)

                rounds(pool, CHUNKS // 2, body)

            @block.scalar
            def _(act):
                act.wait_ge(lb_exp, 1)
                nc.scalar.activation(lbt[:, 0, :], lbt[:, 1, :], ACT.Exp).then_inc(lb_exp, 1)
                def body(i):
                    for r in range(2):
                        act.wait_ge(f_in[r], i * 16 + 16)
                        nc.scalar.activation(a_f[r][:], a_f[r][:], ACT.Sigmoid).then_inc(a_sig[r], 1)
                        act.wait_ge(a_ktr[r], i + 1)
                        act.wait_ge(a_kv[r], i)
                        nc.scalar.activation(a_ktok[r][:], bank[r][:], ACT.Copy).then_inc(a_kev[r], 1)

                rounds(act, CHUNKS // 2, body)

            @block.vector
            def _(dve):
                mc = Chain(dve, mask_chain)
                dve.wait_ge(iota_done, 1)
                mc.link(dve.tensor_tensor(xor_i[:, 0, :], xor_i[:, 0, :], xor_i[:, 1, :], ALU.bitwise_xor))
                mc.link(dve.tensor_copy(xor_f[:], xor_i[:, 0, :]))
                for l in range(LEVELS + 1):
                    last = dve.tensor_scalar(ge[:, l, :], xor_f[:], float(1 << l), None, ALU.is_ge)
                mc.link(last)
                dve.tensor_tensor(masks[:], ge[:, 0:LEVELS, :], ge[:, 1:LEVELS + 1, :], ALU.subtract)
                raw = g["cols"][:, V_LB:V_LB + CT]
                dve.tensor_tensor(lbt[:, 1, :], raw, raw, ALU.subtract).then_inc(lb_exp, 1)
                dve.wait_ge(lb_exp, 2)
                mc.link(dve.reciprocal(lbt[:, 1, :], lbt[:, 0, :]))
                mc.link(dve.tensor_tensor(lbt[:, 1, :], lbt[:, 1, :], lbt[:, 0, :], ALU.mult))
                mc.link(dve.tensor_tensor(lbt[:, 2, :], lbt[:, 1, :], lbt[:, 1, :], ALU.subtract))
                dve.tensor_scalar(lbt[:, 3, :], lbt[:, 2, :], -1.0, 1.0, ALU.mult, ALU.add).then_inc(lb_done, 1)
                dve.wait_ge(zeroed, 1)
                def body(i):
                    for r in range(2):
                        dc = Chain(dve, a_chain, i * 4 + r * 2)
                        c = dve.snap((CHUNKS - 1 - r) - i * 2)
                        dve.wait_ge(a_gate[r], i + 1)
                        dve.wait_ge(a_keys[r], i)
                        for j in range(CT):
                            last = dve.tensor_tensor_scan(a_e[r][:, j, 1:P], a_f[r][:, j, 0:P - 1], ones_row[:, 0:P - 1], 1.0,
                                                          ALU.mult, ALU.mult)
                        dc.link(last)
                        dve.tensor_tensor(a_p[r][:], a_e[r][:, :, P - 1], a_f[r][:, :, P - 1], ALU.mult)
                        dve.wait_ge(a_kd[r], i + 1)
                        dve.tensor_tensor(a_k[r][:], a_k[r][:], a_e[r][:], ALU.mult).then_inc(a_keys[r], 1)
                        dve.wait_ge(a_keys[r], i + 1)
                        wait_apart(dve, a_vtr[r], i + 1, passed)
                        dve.tensor_copy(v_tok[:, ds(c, 1), :], bank[2 + r][:].unsqueeze(1)).then_inc(a_vev[r], 1)
                        dve.wait_ge(a_state, i * 4 + r * 2)
                        dc.link(dve.tensor_tensor(decayed[:].unsqueeze(1), s_bwd[:, ds(c + 1, 1), :, :],
                                                  bcast_inner(a_p[r][:], P).unsqueeze(1), ALU.mult))
                        dve.wait_ge(a_kv[r], i + 1)
                        for half in range(2):
                            at = slice(half * HEAD, (half + 1) * HEAD)
                            kv = bank[4 + r][at, :].rearrange("p (j n) -> p j n", j=CT)[:, :, at]
                            dve.tensor_tensor(s_bwd[at, ds(c, 1), :, at], decayed[at, :, at].unsqueeze(1), kv.unsqueeze(1),
                                              ALU.add).then_inc(a_state, 1)

                rounds(dve, CHUNKS // 2, body)

            @block.tensor
            def _(pe):
                def body(i):
                    for r in range(2):
                        c = pe.snap((CHUNKS - 1 - r) - i * 2)
                        pe.wait_ge(v_in[r], i * 16 + 16)
                        pe.wait_ge(a_vev[r], i)
                        for j in range(CT):
                            tr = pe.transpose(bank[2 + r][:, j * P:(j + 1) * P], a_v[r][:, j, :], g["ident"][:])
                        tr.then_inc(a_vtr[r], 1)
                        pe.wait_ge(a_keys[r], i + 1)
                        pe.wait_ge(a_kev[r], i)
                        for j in range(CT):
                            tr = pe.transpose(bank[r][:, j * P:(j + 1) * P], a_k[r][:, j, :], g["ident"][:])
                        tr.then_inc(a_ktr[r], 1)
                        pe.wait_ge(a_vev[r], i + 1)
                        pe.wait_ge(a_state, i * 4)
                        wait_apart(pe, a_kev[r], i + 1, passed)
                        for j in range(CT):
                            mm = pe.matmul(bank[4 + r][:, j * P:(j + 1) * P], a_ktok[r][:, j * P:(j + 1) * P],
                                           v_tok[:, ds(c, 1), j * P:(j + 1) * P], start=True, stop=True)
                        mm.then_inc(a_kv[r], 1)

                rounds(pe, CHUNKS // 2, body)

        names = ("q", "ff", "fb", "gate")
        inp = {n: [sb(f"b_{n}{i}", W) for i in range(2)] for n in names}
        gate_sig = sb("b_gate_sig", W)
        first = [sb(f"{n}_first", W) for n in ("qf", "kf", "qb", "kb")]
        mid = [[sb(f"{n}_mid{i}", W) for i in range(2)] for n in ("qf", "kf", "qb", "kb")]
        end = [sb(f"{n}_end", W) for n in ("qf", "kf", "qb")]
        kd = sb("k_diag", W)
        PF, PB = ([sb(f"{n}{l}", [P, CT, P >> l]) for l in range(1, LEVELS + 1)] for n in ("pf", "pb"))
        score = [sb(f"score{i}", [P, 2, CT, P]) for i in range(2)]
        ktok = sb("ktok", [P, CH])
        sq = sb("o_sq", [P, CH])
        ss, rs, rinv = sb("o_ss", [P, 8]), sb("o_rms", [P, 8]), sb("o_rinv", [P, 8])
        on = sb("o_norm", [P, CH])
        mrg = [sb(f"mrg{i}", W) for i in range(2)]
        loaded = {n: sem2(f"in_{n}") for n in names}
        mrg_out = sem2("mrg_stored")
        (sig, gsig, gate_v, gate_p, init_v, init_p, up_v, up_p, up_a, lvl, taken, ktr, kev, kvs, st, inter, o_mm, o_sqd, o_ss,
         o_rms, o_n, o_tr, mrg_done, vch, gate_done) = (sem(n) for n in (
            "b_sig", "b_gsig", "b_gate_v", "b_gate_p", "b_init_v", "b_init_p", "up_v", "up_p", "up_a", "lvl", "taken", "b_ktr",
            "b_kev", "b_kv", "b_state", "b_inter", "o_mm", "o_sqd", "o_ssd", "o_rmsd", "o_nd", "o_tr", "mrg_done", "b_vch", "b_gate_done"))
        QF, KF, QB, KB = range(4)
        L1 = LEVELS + 1

        def arr(x, l):
            return first[x] if l == 0 else end[x] if l == LEVELS else mid[x][l % 2]

        def halves(x, l):
            return x.rearrange("p j (n two a) -> p (j n) two a", two=2, a=1 << l)

        def whole(x):
            return x.rearrange("p j (n two) -> p (j n) two", two=2)

        def target_free(eng, n, l):
            eng.wait_ge(lvl, pos(n * L1 - 1 if l == 0 else n * L1 if l == 1 else n * L1 + l + 1))
            eng.wait_ge(up_a, n * LEVELS + l)
            if l == LEVELS - 1:
                eng.wait_ge(inter, n)
                eng.wait_ge(ktr, n)

        def chunks(eng, body):
            body(0, 0, 0)
            body(1, 1, 0)
            with eng.Fori(1, CHUNKS // 2 - 1) as i:
                body(i * 2, 0, i)
                body(i * 2 + 1, 1, i)
            body(CHUNKS - 2, 0, CHUNKS // 2 - 1)
            body(CHUNKS - 1, 1, CHUNKS // 2 - 1)

        is_first = lambda n: isinstance(n, int) and n == 0
        is_last = lambda n: isinstance(n, int) and n == CHUNKS - 1

        with nc.Block() as block:
            @block.sync
            def _(q):
                def load(name, group, c, r):
                    q.dma_start(inp[name][r][:], src(group, c)).then_inc(loaded[name][r], 16)

                def store(n, r):
                    q.wait_ge(mrg_done, n + 1)
                    q.dma_start(t["mergedT"][CH:2 * CH, :].rearrange("(j p) n -> p j n", p=P)[:, :, ds(n * P, P)],
                                mrg[r][:]).then_inc(mrg_out[r], 16)

                for name, group in (("ff", 3), ("fb", 4), ("q", 2), ("gate", 6)):
                    load(name, group, 0, 0)

                def body(n, r, i):
                    if not is_last(n):
                        wait_apart(q, lvl, n * L1, passed)
                        wait_apart(q, up_v, n * LEVELS, passed)
                        wait_apart(q, up_p, n * LEVELS, passed)
                        for name, group in (("ff", 3), ("fb", 4), ("q", 2)):
                            load(name, group, n * P + P, 1 - r)
                    if not is_first(n):
                        wait_apart(q, mrg_done, n, passed)
                        store(n - 1, 1 - r)
                    if not is_last(n):
                        load("gate", 6, n * P + P, 1 - r)

                chunks(q, body)
                store(CHUNKS - 1, 1)
                for r in range(2):
                    q.wait_ge(mrg_out[r], 16 * (CHUNKS // 2))

            @block.gpsimd
            def _(pool):
                def init(n, r, i):
                    f, b, q = inp["ff"][r], inp["fb"][r], inp["q"][r]
                    wait_apart(pool, sig, n * 2 + 2, passed)
                    for j in range(CT):
                        last = pool.tensor_scalar(b[:, j, :], b[:, j, :], lbt[:, 3, j:j + 1], lbt[:, 2, j:j + 1], ALU.mult, ALU.add)
                    last.then_inc(gate_p, 1)
                    pool.wait_ge(lvl, pos((n - 1) * L1 + 2))
                    pool.wait_ge(up_v, pos((n - 1) * LEVELS + 1))
                    pool.wait_ge(up_a, pos((n - 1) * LEVELS + 1))
                    pool.wait_ge(gate_v, n + 1)
                    wait_apart(pool, gate_p, n + 1, passed)
                    pool.tensor_scalar(first[KF][:], f[:], -1.0, 1.0, ALU.mult, ALU.add)
                    pool.tensor_scalar(first[KB][:], b[:], -1.0, 1.0, ALU.mult, ALU.add).then_inc(init_p, 1)
                    pool.wait_ge(loaded["q"][r], i * 16 + 16)
                    pool.tensor_tensor(first[QB][:], q[:], b[:], ALU.mult).then_inc(init_p, 1)

                init(0, 0, 0)

                def body(n, r, i):
                    pool.wait_ge(init_p, n * 2 + 2)
                    b = inp["fb"][r]
                    for l in range(LEVELS):
                        pb = whole(b[:] if l == 0 else PB[l - 1][:])
                        target_free(pool, n, l)
                        pool.wait_ge(up_p, n * LEVELS + l)
                        ins = pool.tensor_tensor(halves(arr(QB, l + 1)[:], l)[:, :, 0, :], halves(arr(QB, l)[:], l)[:, :, 0, :],
                                                 bcast_inner(pb[:, :, 1], 1 << l), ALU.mult)
                        if l < LEVELS - 1:
                            pool.tensor_tensor(halves(arr(KB, l + 1)[:], l)[:, :, 1, :], halves(arr(KB, l)[:], l)[:, :, 1, :],
                                               bcast_inner(pb[:, :, 0], 1 << l), ALU.mult)
                            ins = pool.tensor_tensor(PB[l][:].rearrange("p j n -> p (j n)"), pb[:, :, 0], pb[:, :, 1], ALU.mult)
                        ins.then_inc(up_p, 1)
                        if l == 3 and not is_last(n):
                            init(n + 1, 1 - r, i + r)
                    pool.wait_ge(gsig, n + 1)
                    pool.tensor_tensor(inp["gate"][r][:], inp["gate"][r][:], gate_sig[:], ALU.mult).then_inc(gate_done, 1)

                chunks(pool, body)

            @block.scalar
            def _(act):
                def init(n, r, i):
                    for name in ("ff", "fb"):
                        act.wait_ge(loaded[name][r], i * 16 + 16)
                        nc.scalar.activation(inp[name][r][:], inp[name][r][:], ACT.Sigmoid).then_inc(sig, 1)

                def turn_keys(n):
                    act.wait_ge(ktr, n + 1)
                    act.wait_ge(kvs, n)
                    nc.scalar.activation(ktok[:], bank[5][:], ACT.Copy).then_inc(kev, 1)

                def square(n):
                    act.wait_ge(o_mm, n + 1)
                    act.wait_ge(o_ss, n)
                    nc.scalar.activation(sq[:], bank[4][:], ACT.Square).then_inc(o_sqd, 1)

                def root(n):
                    act.wait_ge(o_ss, n + 1)
                    nc.scalar.activation(rs[:], ss[:], ACT.Sqrt, bias=g["eps"][:], scale=1.0 / HEAD).then_inc(o_rms, 1)

                init(0, 0, 0)

                def body(n, r, i):
                    act.wait_ge(init_v, n * 2 + 2)
                    act.wait_ge(init_p, n * 2 + 2)
                    for l in range(LEVELS):
                        target_free(act, n, l)
                        act.wait_ge(up_v, n * LEVELS + l)
                        act.wait_ge(up_p, n * LEVELS + l)
                        for x, h in ((QF, 0), (KF, 1), (QB, 1), (KB, 0)):
                            if x == KB and l == LEVELS - 1:
                                continue
                            last = nc.scalar.activation(halves(arr(x, l + 1)[:], l)[:, :, h, :], halves(arr(x, l)[:], l)[:, :, h, :],
                                                        ACT.Copy)
                        last.then_inc(up_a, 1)
                        if not is_first(n):
                            if l == 1:
                                turn_keys(n - 1)
                            if l == 2:
                                square(n - 1)
                            if l == 3:
                                root(n - 1)
                        if l == 4:
                            if not is_last(n):
                                init(n + 1, 1 - r, i + r)
                            act.wait_ge(loaded["gate"][r], i * 16 + 16)
                            act.wait_ge(gate_done, n)
                            nc.scalar.activation(gate_sig[:], inp["gate"][r][:], ACT.Sigmoid).then_inc(gsig, 1)

                chunks(act, body)
                n = CHUNKS - 1
                square(n)
                root(n)

            @block.vector
            def _(dve):
                def init_gate(n, r):
                    f = inp["ff"][r]
                    dve.wait_ge(sig, n * 2 + 1)
                    for j in range(CT):
                        last = dve.tensor_scalar(f[:, j, :], f[:, j, :], lbt[:, 3, j:j + 1], lbt[:, 2, j:j + 1], ALU.mult, ALU.add)
                    last.then_inc(gate_v, 1)

                def init_queries(n, r, i):
                    dve.wait_ge(gate_v, n + 1)
                    dve.wait_ge(loaded["q"][r], i * 16 + 16)
                    dve.wait_ge(lvl, pos((n - 1) * L1 + 2))
                    dve.wait_ge(up_a, pos((n - 1) * LEVELS + 1))
                    dve.tensor_tensor(first[QF][:], inp["q"][r][:], inp["ff"][r][:], ALU.mult).then_inc(init_v, 1)
                    dve.wait_ge(init_p, n * 2 + 1)
                    dve.tensor_tensor(kd[:], first[KF][:], first[KB][:], ALU.add).then_inc(init_v, 1)

                def take(n, r, l):
                    base = n * L1 + l + 2
                    if l < 0:
                        dve.wait_ge(o_mm, pos(n - 1))
                    dve.wait_ge(taken, base - 1)
                    wait_apart(dve, lvl, base, passed)
                    for half in range(2):
                        b = bank[2 * ((l + 1) % 2) + half][:].rearrange("p (j n) -> p j n", j=CT)
                        if l < 0:
                            ins = dve.tensor_tensor(score[r][:, half, :, :], b,
                                                    g["ident"][:].unsqueeze(1).to_broadcast([P, CT, P]), ALU.mult)
                        else:
                            ins = dve.copy_predicated(score[r][:, half, :, :],
                                                      masks[:, l, :].unsqueeze(1).to_broadcast([P, CT, P]), b)
                    ins.then_inc(taken, 1)

                def head_sums(n):
                    dve.wait_ge(o_sqd, n + 1)
                    dve.wait_ge(o_rms, n)
                    dve.tensor_reduce(ss[:], sq[:].rearrange("p (h e) -> p h e", e=HEAD), AX, ALU.add).then_inc(o_ss, 1)

                def state(n, r):
                    dc = Chain(dve, vch, n * 2)
                    dve.wait_ge(st, n * 2)
                    dc.link(dve.tensor_tensor(decayed[:], s_fwd[r][:], bcast_inner(PF[LEVELS - 1][:, :, 0], P), ALU.mult))
                    dve.wait_ge(kvs, n + 1)
                    dve.wait_ge(inter, n)
                    for half in range(2):
                        at = slice(half * HEAD, (half + 1) * HEAD)
                        kv = bank[6][at, :].rearrange("p (j n) -> p j n", j=CT)[:, :, at]
                        dve.tensor_tensor(s_fwd[1 - r][at, :, at], decayed[at, :, at], kv, ALU.add).then_inc(st, 1)

                def normalise(n, links):
                    dc = Chain(dve, vch, links)
                    dve.wait_ge(o_rms, n + 1)
                    dc.link(dve.reciprocal(rinv[:], rs[:]))
                    dve.wait_ge(o_tr, n)
                    dve.tensor_tensor(on[:].rearrange("p (h e) -> p h e", e=HEAD), bank[4][:].rearrange("p (h e) -> p h e", e=HEAD),
                                      bcast_inner(rinv[:], HEAD), ALU.mult).then_inc(o_n, 1)

                def merge(n, r, i):
                    dve.wait_ge(o_tr, n + 1)
                    dve.wait_ge(gate_done, n + 1)
                    dve.wait_ge(mrg_out[r], i * 16)
                    dve.tensor_tensor(mrg[r][:], bank[7][:].rearrange("p (j n) -> p j n", j=CT), inp["gate"][r][:],
                                      ALU.mult).then_inc(mrg_done, 1)

                init_gate(0, 0)
                init_queries(0, 0, 0)

                def body(n, r, i):
                    f = inp["ff"][r]
                    dve.wait_ge(init_v, n * 2 + 2)
                    for l in range(LEVELS):
                        pf = whole(f[:] if l == 0 else PF[l - 1][:])
                        target_free(dve, n, l)
                        dve.wait_ge(up_v, n * LEVELS + l)
                        dve.tensor_tensor(halves(arr(QF, l + 1)[:], l)[:, :, 1, :], halves(arr(QF, l)[:], l)[:, :, 1, :],
                                          bcast_inner(pf[:, :, 0], 1 << l), ALU.mult)
                        dve.tensor_tensor(halves(arr(KF, l + 1)[:], l)[:, :, 0, :], halves(arr(KF, l)[:], l)[:, :, 0, :],
                                          bcast_inner(pf[:, :, 1], 1 << l), ALU.mult)
                        dve.tensor_tensor(PF[l][:].rearrange("p j n -> p (j n)"), pf[:, :, 0], pf[:, :, 1],
                                          ALU.mult).then_inc(up_v, 1)
                        take(n, r, l - 1)
                        if not is_first(n):
                            if l == 2:
                                head_sums(n - 1)
                            if l == 3:
                                state(n - 1, 1 - r)
                            if l == 4:
                                normalise(n - 1, n * 2 - 1)
                            if l == 6:
                                merge(n - 1, 1 - r, i - 1 + r)
                        if not is_last(n):
                            if l == 4:
                                init_gate(n + 1, 1 - r)
                            if l == 6:
                                init_queries(n + 1, 1 - r, i + r)
                    take(n, r, LEVELS - 1)

                chunks(dve, body)
                n = CHUNKS - 1
                head_sums(n)
                normalise(n, n * 2)
                merge(n, 1, CHUNKS // 2 - 1)

            @block.tensor
            def _(pe):
                def products(n, r, l):
                    q = inp["q"][r]
                    if l >= 1:
                        pe.wait_ge(up_v, n * LEVELS + l)
                        pe.wait_ge(up_p, n * LEVELS + l)
                        pe.wait_ge(up_a, n * LEVELS + l)
                    if l < LEVELS - 2:
                        pe.wait_ge(taken, pos(n * L1 + l))
                    else:
                        wait_apart(pe, taken, n * L1 + l, passed)
                    for half in range(2):
                        at = slice(half * HEAD, (half + 1) * HEAD)
                        for j in range(CT):
                            out = bank[2 * ((l + 1) % 2) + half][:, j * P:(j + 1) * P]
                            if l < 0:
                                mm = pe.matmul(out, kd[at, j, :], q[at, j, :], start=True, stop=True)
                                continue
                            if l >= LEVELS - 2:
                                L = 1 << l
                                for b in range(0, P, 2 * L):
                                    lo, hi = slice(b, b + L), slice(b + L, b + 2 * L)
                                    pe.matmul(out[lo, hi], arr(KF, l)[at, j, lo], arr(QF, l)[at, j, hi], start=True, stop=True)
                                    mm = pe.matmul(out[hi, lo], arr(KB, l)[at, j, hi], arr(QB, l)[at, j, lo], start=True,
                                                   stop=True)
                                continue
                            two = lambda x, w: x.rearrange("p (n two a) -> p n two a", two=2, a=1 << l)[:, :, w, :]
                            pe.matmul(two(out, 1), arr(KF, l)[at, j, :], two(arr(QF, l)[at, j, :], 1), start=True, stop=True)
                            mm = pe.matmul(two(out, 0), arr(KB, l)[at, j, :], two(arr(QB, l)[at, j, :], 0), start=True, stop=True)
                    mm.then_inc(lvl, 1)

                def across(n, r):
                    pe.wait_ge(up_v, (n + 1) * LEVELS)
                    pe.wait_ge(up_p, (n + 1) * LEVELS)
                    pe.wait_ge(up_a, (n + 1) * LEVELS)
                    pe.wait_ge(kev, n)
                    for j in range(CT):
                        tr = pe.transpose(bank[5][:, j * P:(j + 1) * P], end[KF][:, j, :], g["ident"][:])
                    tr.then_inc(ktr, 1)
                    pe.wait_ge(o_n, n)
                    wait_apart(pe, st, n * 2, passed)
                    for j in range(CT):
                        at = slice(j * P, (j + 1) * P)
                        pe.matmul(bank[4][:, at], end[QF][:, j, :], s_fwd[r][:, j, :], start=(j == 0), stop=False,
                                  skip_group_check=True)
                        mm = pe.matmul(bank[4][:, at], end[QB][:, j, :], s_bwd[:, ds(n + 1, 1), j, :], start=False, stop=False,
                                       skip_group_check=True)
                    mm.then_inc(inter, 1)

                def within(n, r):
                    pe.wait_ge(taken, (n + 1) * L1)
                    for j in range(CT):
                        for half in range(2):
                            at = slice(j * P + half * HEAD, j * P + (half + 1) * HEAD)
                            mm = pe.matmul(bank[4][:, at], score[r][:, half, j, :], v_tok[:, ds(n, 1), at], start=False,
                                           stop=(j == CT - 1 and half == 1), skip_group_check=True)
                    mm.then_inc(o_mm, 1)

                def keys_values(n):
                    pe.wait_ge(kev, n + 1)
                    pe.wait_ge(st, n * 2)
                    for j in range(CT):
                        mm = pe.matmul(bank[6][:, j * P:(j + 1) * P], ktok[:, j * P:(j + 1) * P],
                                       v_tok[:, ds(n, 1), j * P:(j + 1) * P], start=True, stop=True)
                    mm.then_inc(kvs, 1)

                def turn_back(n):
                    pe.wait_ge(o_n, n + 1)
                    pe.wait_ge(mrg_done, n)
                    for j in range(CT):
                        tr = pe.transpose(bank[7][:, j * P:(j + 1) * P], on[:, j * P:(j + 1) * P], g["ident"][:])
                    tr.then_inc(o_tr, 1)

                def body(n, r, i):
                    pe.wait_ge(init_v, n * 2 + 2)
                    pe.wait_ge(init_p, n * 2 + 2)
                    for l in range(-1, LEVELS):
                        products(n, r, l)
                        if not is_first(n):
                            if l == 0:
                                across(n - 1, 1 - r)
                            if l == 1:
                                within(n - 1, 1 - r)
                            if l == 2:
                                keys_values(n - 1)
                            if l == 5:
                                turn_back(n - 1)

                chunks(pe, body)
                n = CHUNKS - 1
                across(n, 1)
                within(n, 1)
                turn_back(n)


def phase_output(nc, t, g):
    with ExitStack() as ctx:
        sb = lambda n, s, d=F32: ctx.enter_context(nc.sbuf_tensor(n, s, d))
        sem = ctx.enter_context(semaphores(nc))
        sem2 = lambda n: [sem(f"{n}{i}") for i in range(2)]
        lru_ps = ctx.enter_context(nc.psum_tensor("lru_ps", [P, D], F32))
        hg_ps = ctx.enter_context(nc.psum_tensor("hg_ps", [P, D], F32))
        tr_ps = ctx.enter_context(nc.psum_tensor("tr_ps", [P, D], F32))
        sum_ps = ctx.enter_context(nc.psum_tensor("sum_ps", [P, BANK], F32))
        rt_ps = ctx.enter_context(nc.psum_tensor("rt_ps", [P, BANK], F32))
        wo = sb("wo", [P, KD, D])
        wr = sb("wr", [P, KD, ROUTES])
        wrs = sb("wrs", [P, KD, ROUTES])
        bias = sb("route_bias_all", [1, ROUTES])
        m = [sb(f"merged{i}", [P, KD, P]) for i in range(2)]
        xr = [sb(f"x_row{i}", [P, D]) for i in range(2)]
        x2 = [sb(f"x2_{i}", [P, D]) for i in range(2)]
        xh = [sb(f"xh_{i}", [P, D]) for i in range(2)]
        sq = [sb(f"lru_sq{i}", [P, CT, P]) for i in range(2)]
        junk = [sb(f"x2_sq{i}", [P, D]) for i in range(2)]
        xt = [sb(f"xh_t{i}", [P, KD, P]) for i in range(2)]
        st = [sb(f"stat{i}", [P, 8]) for i in range(2)]
        wo_in, wr_in, wo_done, wr_done, bias_ps, bias_done = (sem(n) for n in (
            "wo_in", "wr_in", "wo_done", "wr_done", "bias_ps", "bias_done"))
        m_in, xr_in, x2_out, xh_out = sem2("m_in"), sem2("xr_in"), sem2("x2_out"), sem2("xh_out")
        sq_done, sum_mm, lru_rms, lru_r, y_mm, acc, x2_done, x2_sq, x2_rms, x2_r, xh_done, xt_mm, xt_done, rt_mm, lg = (
            sem(n) for n in ("sq_d", "sum_mm", "lru_rms", "lru_r", "y_mm", "acc", "x2_done", "x2_sqd", "x2_rms", "x2_r",
                             "xh_done", "xt_mm", "xt_done", "rt_mm", "lg"))
        lru_mm, passed = sem("lru_mm"), sem("o_passed")
        block = ctx.enter_context(nc.Block())

        def tiles(eng, body):
            body(0, 0, 0)
            body(1, 1, 0)
            with eng.Fori(1, TOK_TILES // 2) as i:
                body(i * 2, 0, i)
                body(i * 2 + 1, 1, i)

        @block.sync
        def _(q):
            q.dma_start(wo[:], t["w_out"][0].rearrange("(k p) n -> p k n", p=P)).then_inc(wo_in, 16)
            q.dma_start(wr[:, :, 0:N_GROUPS], t["router_group_w"][0].rearrange("(k p) n -> p k n", p=P)).then_inc(wr_in, 16)
            q.dma_start(wr[:, :, N_GROUPS:ROUTES], t["router_expert_w"][0].rearrange("(k p) n -> p k n", p=P)).then_inc(wr_in, 16)

            def load(n, r):
                wait_apart(q, y_mm, pos(n - 1), passed)
                wait_apart(q, x2_done, pos(n - 1), passed)
                q.dma_start(m[r][:], t["mergedT"].rearrange("(k p) n -> p k n", p=P)[:, :, ds(n * P, P)]).then_inc(m_in[r], 16)
                q.dma_start(xr[r][:], t["x"][0][ds(n * P, P), :]).then_inc(xr_in[r], 16)

            def store(n, r):
                wait_apart(q, x2_done, n + 1, passed)
                q.dma_start(t["x2"][ds(n * P, P), :], x2[r][:]).then_inc(x2_out[r], 16)
                wait_apart(q, xh_done, n + 1, passed)
                q.dma_start(t["xh"][ds(n * P, P), :], xh[r][:]).then_inc(xh_out[r], 16)

            def body(n, r, i):
                load(n, r)
                if not (isinstance(n, int) and n == 0):
                    store(n - 1, 1 - r)

            tiles(q, body)
            store(TOK_TILES - 1, 1)
            for s in (*x2_out, *xh_out):
                q.wait_ge(s, 16 * (TOK_TILES // 2))

        @block.gpsimd
        def _(pool):
            def body(n, r, i):
                wait_apart(pool, m_in[r], i * 16 + 16, passed)
                pool.wait_ge(sum_mm, pos(n - 1))
                pool.tensor_tensor(sq[r][:], m[r][:, 0:CT, :], m[r][:, 0:CT, :], ALU.mult).then_inc(sq_done, 1)

            tiles(pool, body)

        @block.scalar
        def _(act):
            def turned(n, r):
                act.wait_ge(xt_mm, n + 1)
                act.wait_ge(rt_mm, pos(n - 1))
                nc.scalar.activation(xt[r][:].rearrange("p k n -> p (k n)"), tr_ps[:], ACT.Copy).then_inc(xt_done, 1)

            def body(n, r, i):
                act.wait_ge(sum_mm, n + 1)
                nc.scalar.activation(st[r][:, 0:1], sum_ps[:, 0:1], ACT.Sqrt, bias=g["eps"][:], scale=1.0 / CH).then_inc(lru_rms, 1)
                if not (isinstance(n, int) and n == 0):
                    turned(n - 1, 1 - r)
                act.wait_ge(x2_done, n + 1)
                nc.scalar.activation(junk[r][:], x2[r][:], ACT.Square, accum_out=st[r][:, 2:3]).then_inc(x2_sq, 1)
                act.wait_ge(x2_sq, n + 1)
                nc.scalar.activation(st[r][:, 3:4], st[r][:, 2:3], ACT.Sqrt, bias=g["eps"][:], scale=1.0 / D).then_inc(x2_rms, 1)

            tiles(act, body)
            turned(TOK_TILES - 1, 1)

        @block.vector
        def _(dve):
            dve.wait_ge(wo_in, 16)
            for k in range(KD):
                at = (V_NORM_LRU + k) if k < CT else (V_NORM_HG + k - CT)
                ins = dve.scalar_tensor_tensor(out=wo[:, k, :], in0=wo[:, k, :], scalar=g["cols"][:, at:at + 1],
                                               in1=g["gates"][:, 0, :], op0=ALU.mult, op1=ALU.mult)
            ins.then_inc(wo_done, 1)
            dve.wait_ge(wr_in, 32)
            dve.tensor_tensor(wrs[:], wr[:], bcast_inner(g["scale_ffn"][:], ROUTES), ALU.mult).then_inc(wr_done, 1)
            dve.wait_ge(bias_ps, 1)
            dve.tensor_tensor(bias[:], rt_ps[0:1, 0:ROUTES], g["route_bias"][:], ALU.add).then_inc(bias_done, 1)

            def logits(n):
                dve.wait_ge(rt_mm, n + 1)
                dve.tensor_copy(g["logits"][:, ds(n, 1), :], rt_ps[:, 0:ROUTES].unsqueeze(1)).then_inc(lg, 1)

            def body(n, r, i):
                dve.wait_ge(lru_rms, n + 1)
                dve.reciprocal(st[r][:, 1:2], st[r][:, 0:1]).then_inc(lru_r, 1)
                dve.wait_ge(lru_mm, n + 1)
                dve.wait_ge(lru_r, n + 1)
                dve.wait_ge(xr_in[r], i * 16 + 16)
                dve.wait_ge(x2_out[r], i * 16)
                dve.scalar_tensor_tensor(out=x2[r][:], in0=lru_ps[:], scalar=st[r][:, 1:2], in1=xr[r][:],
                                         op0=ALU.mult, op1=ALU.add).then_inc(acc, 1)
                dve.wait_ge(y_mm, n + 1)
                dve.wait_ge(acc, n + 1)
                dve.tensor_tensor(x2[r][:], x2[r][:], hg_ps[:], ALU.add).then_inc(x2_done, 1)
                dve.wait_ge(x2_rms, n + 1)
                dve.reciprocal(st[r][:, 4:5], st[r][:, 3:4]).then_inc(x2_r, 1)
                dve.wait_ge(x2_r, n + 1)
                dve.wait_ge(xh_out[r], i * 16)
                dve.wait_ge(xt_mm, pos(n - 1))
                dve.tensor_scalar(xh[r][:], x2[r][:], st[r][:, 4:5], None, ALU.mult).then_inc(xh_done, 1)
                if not (isinstance(n, int) and n == 0):
                    logits(n - 1)

            tiles(dve, body)
            logits(TOK_TILES - 1)

        @block.tensor
        def _(pe):
            pe.wait_ge(wr_in, 32)
            for k in range(KD):
                mm = pe.matmul(rt_ps[0:1, 0:ROUTES], g["shift_ffn"][:, k:k + 1], wr[:, k, :], start=(k == 0), stop=(k == KD - 1))
            mm.then_inc(bias_ps, 1)
            pe.wait_ge(wo_done, 1)

            def turn(n, r):
                pe.wait_ge(xh_done, n + 1)
                pe.wait_ge(xt_done, n)
                for k in range(KD):
                    tr = pe.transpose(tr_ps[:, k * P:(k + 1) * P], xh[r][:, k * P:(k + 1) * P], g["ident"][:])
                tr.then_inc(xt_mm, 1)

            def route(n, r):
                pe.wait_ge(xt_done, n + 1)
                pe.wait_ge(lg, n)
                for k in range(KD):
                    pe.matmul(rt_ps[:, 0:ROUTES], xt[r][:, k, :], wrs[:, k, :], start=(k == 0), stop=False)
                pe.matmul(rt_ps[:, 0:ROUTES], g["ones"][0:1, :], bias[:], start=False, stop=True).then_inc(rt_mm, 1)

            def products(r, ps, first):
                for k in range(CT):
                    for h in range(2):
                        mm = pe.matmul(ps[:, h * BANK:(h + 1) * BANK], m[r][:, first + k, :],
                                       wo[:, first + k, h * BANK:(h + 1) * BANK], start=(k == 0), stop=(k == CT - 1),
                                       skip_group_check=True)
                return mm

            pe.wait_ge(wr_done, 1)
            pe.wait_ge(bias_done, 1)

            def body(n, r, i):
                is_first = isinstance(n, int) and n == 0
                pe.wait_ge(sq_done, n + 1)
                pe.wait_ge(lru_rms, n)
                for k in range(CT):
                    mm = pe.matmul(sum_ps[:, 0:1], sq[r][:, k, :], g["ones"][:, 0:1], start=(k == 0), stop=(k == CT - 1))
                mm.then_inc(sum_mm, 1)
                pe.wait_ge(acc, n)
                products(r, lru_ps, 0).then_inc(lru_mm, 1)
                if not is_first:
                    turn(n - 1, 1 - r)
                pe.wait_ge(x2_done, n)
                products(r, hg_ps, CT).then_inc(y_mm, 1)
                if not is_first:
                    route(n - 1, 1 - r)

            tiles(pe, body)
            turn(TOK_TILES - 1, 1)
            route(TOK_TILES - 1, 1)


def phase_route(nc, t, g):
    J = ASSIGN // 2 // P
    with ExitStack() as ctx:
        sb = lambda n, s, d=F32: ctx.enter_context(nc.sbuf_tensor(n, s, d))
        sem = ctx.enter_context(semaphores(nc))
        pos_ps = ctx.enter_context(nc.psum_tensor("pos_ps", [P, TOK_TILES, EXPERTS], F32))
        cnt_ps = ctx.enter_context(nc.psum_tensor("cnt_ps", [P, BANK], F32))
        T_, lg = TOK_TILES, g["logits"]
        g8 = sb("g8", [P, T_, 8])
        gm, em = sb("gm", [P, T_, 8]), sb("em", [P, T_, 8])
        gi, ei = sb("gi", [P, T_, 8], U32), sb("ei", [P, T_, 8], U32)
        gif, eif = sb("gif", [P, T_]), sb("eif", [P, T_, 2])
        ohg = sb("ohg", [P, T_, N_GROUPS])
        neg = sb("neg", [P, T_, N_GROUPS])
        ge_ = sb("g_exp", [P, T_, N_GROUPS])
        pg, dd, one_p = sb("p_group", [P, T_]), sb("top_gap", [P, T_]), sb("one_plus", [P, T_])
        el = sb("el", [P, T_, EXPERTS])
        oh = [sb(f"oh{k}", [P, T_, EXPERTS]) for k in range(2)]
        both = sb("both", [P, T_, EXPERTS])
        pre = sb("pre", [P, T_ + 1, EXPERTS])
        tri = sb("tri", [P, P])
        iota32, iotaJ, iotaW, tokid = sb("iota32", [P, EXPERTS]), sb("iotaJ", [P, J]), sb("iotaW", [P, WINDOWS + 3]), sb("tokid", [P, T_], I32)
        over = sb("over", [P, EXPERTS, J])
        nwin, pend, start = sb("nwin", [P, EXPERTS]), sb("pend", [P, EXPERTS]), sb("start_row", [P, EXPERTS])
        pos, picked, dest_f = sb("pos", [P, T_, EXPERTS]), sb("picked", [P, T_, EXPERTS]), sb("dest_f", [P, T_])
        wle, table = sb("wle", [1, WINDOWS + 3, EXPERTS]), sb("table", [1, 4, WINDOWS + 3])
        live = sb("live", [1, WINDOWS + 3])
        zero_i = sb("zero_i", [P, WINDOWS + 3], I32)
        cst, chain, tri_set, gexp, texp, both_done, pos_mm, scat_ready, zero_in, scat = (sem(n) for n in (
            "r_consts", "r_chain", "tri_set", "g_expd", "t_expd", "both_done", "pos_mm", "scat_ready", "zero_stored", "scattered"))
        block = ctx.enter_context(nc.Block())

        @block.gpsimd
        def _(pool):
            pool.iota(iota32[:], [[1, EXPERTS]], base=0, channel_multiplier=0, allow_small_or_imprecise_dtypes=True)
            pool.iota(iotaJ[:], [[P, J]], base=0, channel_multiplier=0, allow_small_or_imprecise_dtypes=True)
            pool.iota(iotaW[:], [[1, WINDOWS + 3]], base=0, channel_multiplier=0, allow_small_or_imprecise_dtypes=True)
            pool.iota(tokid[:], [[P, T_]], base=0, channel_multiplier=1)
            pool.memset(zero_i[:], 0)
            pool.memset(g8[:], -3.0e38)
            pool.memset(pre[:, 0, :], 0.0)
            pool.memset(tri[:], 1.0).then_inc(tri_set, 1)
            pool.wait_ge(tri_set, 1)
            pool.affine_select(out=tri[:], in_=tri[:], compare_op=ALU.is_gt, fill=0.0, base=0, pattern=[[1, P]],
                               channel_multiplier=-1).then_inc(cst, 1)
            pool.wait_ge(cst, 1)
            pool.dma_start(t["slot_tok"].rearrange("(p w) a -> p (w a)", p=P), zero_i[:]).then_inc(zero_in, 16)
            pool.wait_ge(zero_in, 16)
            pool.wait_ge(scat_ready, 1)
            for i in range(T_):
                for k in range(2):
                    pool.indirect_dma_start(t["slot_tok"], bass.IndirectOffsetOnAxis(ap=g["dest"][k][:, i:i + 1], axis=0),
                                            tokid[:, i:i + 1], None).then_inc(scat, 16)
            pool.wait_ge(scat, 16 * 2 * T_)

        @block.scalar
        def _(act):
            act.wait_ge(gexp, 1)
            nc.scalar.activation(ge_[:], ge_[:], ACT.Exp).then_inc(gexp, 1)
            act.wait_ge(texp, 1)
            nc.scalar.activation(dd[:], dd[:], ACT.Exp).then_inc(texp, 1)

        @block.vector
        def _(dve):
            c = Chain(dve, chain)
            dve.wait_ge(cst, 1)
            c.link(dve.tensor_copy(g8[:, :, 0:N_GROUPS], lg[:, :, 0:N_GROUPS]))
            for i in range(T_):
                last = dve.max(gm[:, i, :], g8[:, i, :])
            c.link(last)
            for i in range(T_):
                last = dve.max_index(gi[:, i, :], gm[:, i, :], g8[:, i, :])
            c.link(last)
            c.link(dve.tensor_copy(gif[:], gi[:, :, 0]))
            c.link(dve.tensor_tensor(ohg[:], iota32[:, 0:N_GROUPS].unsqueeze(1).to_broadcast([P, T_, N_GROUPS]),
                                     bcast_inner(gif[:], N_GROUPS), ALU.is_equal))
            dve.tensor_tensor(ge_[:], lg[:, :, 0:N_GROUPS], bcast_inner(gm[:, :, 0], N_GROUPS), ALU.subtract).then_inc(gexp, 1)
            dve.wait_ge(gexp, 2)
            c.link(dve.tensor_reduce(pg[:], ge_[:], AX, ALU.add))
            c.link(dve.tensor_scalar(neg[:], ohg[:], -1.0, 3.0e38, ALU.add, ALU.mult))
            e4 = lambda x: x.rearrange("p t (g e) -> p t g e", g=N_GROUPS)
            c.link(dve.tensor_tensor(e4(el[:]), e4(lg[:, :, N_GROUPS:ROUTES]), bcast_inner(ohg[:], EPG), ALU.mult))
            c.link(dve.tensor_tensor(e4(el[:]), e4(el[:]), bcast_inner(neg[:], EPG), ALU.add))
            for i in range(T_):
                last = dve.max(em[:, i, :], el[:, i, :])
            c.link(last)
            for i in range(T_):
                last = dve.max_index(ei[:, i, :], em[:, i, :], el[:, i, :])
            c.link(last)
            c.link(dve.tensor_copy(eif[:], ei[:, :, 0:2]))
            dve.tensor_tensor(dd[:], em[:, :, 1], em[:, :, 0], ALU.subtract).then_inc(texp, 1)
            dve.wait_ge(texp, 2)
            c.link(dve.tensor_scalar(one_p[:], dd[:], 1.0, None, ALU.add))
            c.link(dve.tensor_tensor(one_p[:], one_p[:], pg[:], ALU.mult))
            c.link(dve.reciprocal(g["weight"][0][:], one_p[:]))
            dve.tensor_tensor(g["weight"][1][:], g["weight"][0][:], dd[:], ALU.mult)
            for k in range(2):
                last = dve.tensor_tensor(oh[k][:], iota32[:].unsqueeze(1).to_broadcast([P, T_, EXPERTS]),
                                         bcast_inner(eif[:, :, k], EXPERTS), ALU.is_equal)
            c.link(last)
            c.link(dve.tensor_tensor(both[:], oh[0][:], oh[1][:], ALU.add))
            for i in range(T_):
                ins = dve.tensor_tensor(pre[:, i + 1, :], pre[:, i, :], both[:, i, :], ALU.add)
                if i < T_ - 1:
                    c.link(ins)
                else:
                    ins.then_inc(both_done, 1)
            dve.wait_ge(pos_mm, 1)
            c.link(dve.tensor_tensor(over[:], bcast_inner(cnt_ps[:, 0:EXPERTS], J),
                                     iotaJ[:].unsqueeze(1).to_broadcast([P, EXPERTS, J]), ALU.is_gt))
            c.link(dve.tensor_reduce(nwin[:], over[:], AX, ALU.add))
            c.link(dve.tensor_tensor_scan(pend[:], g["ones"][:, 0:EXPERTS], nwin[:], 0.0, ALU.mult, ALU.add))
            c.link(dve.tensor_tensor(start[:], pend[:], nwin[:], ALU.subtract))
            c.link(dve.tensor_scalar(start[:], start[:], float(P), None, ALU.mult))
            c.link(dve.tensor_tensor(pos[:], pos_ps[:], start[:].unsqueeze(1).to_broadcast([P, T_, EXPERTS]), ALU.add))
            for k in range(2):
                c.link(dve.tensor_tensor(picked[:], pos[:], oh[k][:], ALU.mult))
                c.link(dve.tensor_reduce(dest_f[:], picked[:], AX, ALU.add))
                c.link(dve.tensor_copy(g["dest"][k][:], dest_f[:]))
            dve.wait_ge(chain, c.n)
            c.link(dve.tensor_tensor(wle[:], pend[0:1, :].unsqueeze(1).to_broadcast([1, WINDOWS + 3, EXPERTS]),
                                     bcast_inner(iotaW[0:1, :], EXPERTS), ALU.is_le))
            c.link(dve.tensor_reduce(table[:, W_EXPERT, :], wle[:], AX, ALU.add))
            c.link(dve.tensor_scalar(table[:, W_EXPERT, :], table[:, W_EXPERT, :], float(EXPERTS - 1), None, ALU.min))
            dve.tensor_scalar(live[:], iotaW[0:1, :], pend[0:1, EXPERTS - 1:EXPERTS], None, ALU.is_lt)
            dve.memset(table[:, W_NEW, 0:1], 1.0)
            c.link(dve.tensor_tensor(table[:, W_NEW, 1:], table[:, W_EXPERT, 1:], table[:, W_EXPERT, 0:WINDOWS + 2], ALU.not_equal))
            c.link(dve.tensor_tensor(table[:, W_NEW, :], table[:, W_NEW, :], live[:], ALU.mult))
            c.link(dve.tensor_tensor_scan(table[:, W_COUNT, :], g["ones"][0:1, 0:WINDOWS + 3], table[:, W_NEW, :], 0.0,
                                          ALU.mult, ALU.add))
            c.link(dve.tensor_scalar(table[:, W_BEFORE, :], table[:, W_COUNT, :], -1.0, None, ALU.add))
            c.link(dve.tensor_scalar(table[:, W_NEW, WINDOWS + 2:], pend[0:1, EXPERTS - 1:EXPERTS], -2.0, None, ALU.add))
            c.link(dve.tensor_scalar(table[:, W_EXPERT, WINDOWS + 2:], pend[0:1, EXPERTS - 1:EXPERTS], -1.0, None, ALU.add))
            dve.tensor_copy(g["window"][:], table[:]).then_inc(scat_ready, 1)

        @block.tensor
        def _(pe):
            pe.wait_ge(both_done, 1)
            pe.matmul(pos_ps[:].rearrange("p t e -> p (t e)"), tri[:], both[:].rearrange("p t e -> p (t e)"), start=True, stop=False)
            pe.matmul(pos_ps[:].rearrange("p t e -> p (t e)"), g["ones"][:],
                      pre[:, 0:T_, :].rearrange("p t e -> p (t e)"), start=False, stop=True)
            pe.matmul(cnt_ps[:, 0:EXPERTS], g["ones"][:], pre[:, T_, :], start=True, stop=True).then_inc(pos_mm, 1)


def phase_experts(nc, t, g):
    with ExitStack() as ctx:
        sb = lambda n, s, d=F32: ctx.enter_context(nc.sbuf_tensor(n, s, d))
        sem = ctx.enter_context(semaphores(nc))
        FT = F_EXP // P
        GU, DN = KD // 2, FT // 2
        PIECES = GU + DN
        xt_ps = ctx.enter_context(nc.psum_tensor("e_xt_ps", [P, D], F32))
        gate_ps = ctx.enter_context(nc.psum_tensor("e_gate_ps", [P, BANK], F32))
        up_ps = ctx.enter_context(nc.psum_tensor("e_up_ps", [P, BANK], F32))
        at_ps = ctx.enter_context(nc.psum_tensor("e_at_ps", [P, BANK], F32))
        y_ps = ctx.enter_context(nc.psum_tensor("e_y_ps", [P, D], F32))
        raw = [sb(f"e_raw{p}", [P, 2, D]) for p in range(PIECES)]
        w_hi = [sb(f"e_w_hi{p}", [P, 2, D], F32R) for p in range(PIECES)]
        w_lo = [sb(f"e_w_lo{p}", [P, 2, D], F32R) for p in range(PIECES)]
        idx = [sb(f"e_idx{r}", [P, 1], I32) for r in range(2)]
        xrow = [sb(f"e_xrow{r}", [P, D]) for r in range(2)]
        xt = sb("e_xt", [P, KD, P])
        x_hi = sb("e_x_hi", [P, KD, P], F32R)
        x_lo = sb("e_x_lo", [P, KD, P], F32R)
        sg = sb("e_sg", [P, F_EXP])
        prod = sb("e_prod", [P, F_EXP])
        p_hi = sb("e_p_hi", [P, FT, P], F32R)
        p_lo = sb("e_p_lo", [P, FT, P], F32R)
        y = sb("e_y", [P, D])
        raw_in, hi_done, lo_done, w_used = ([sem(f"e_{n}{p}") for p in range(PIECES)] for n in ("raw_in", "hi", "lo", "used"))
        idx_in, x_in = ([sem(f"e_{n}{r}") for r in range(2)] for n in ("idx_in", "x_in"))
        xt_mm, xf_act, xf_dve, xh_act, xh_dve, x_split, sg_done, prod_done, at_mm, ph_done, p_split = (
            sem(n) for n in ("e_xt_mm", "e_xf_act", "e_xf_dve", "e_xh_act", "e_xh_dve", "e_x_split", "e_sg_done",
                             "e_prod_done", "e_at_mm", "e_ph_done", "e_p_split"))
        gu_mm, y_mm = w_used[GU - 1], w_used[PIECES - 1]
        y_act, y_dve, y_out, passed = (sem(n) for n in ("e_y_act", "e_y_dve", "e_y_out", "e_passed"))
        block = ctx.enter_context(nc.Block())

        def windows(eng, body):
            body(0, 0, 0)
            body(1, 1, 0)
            with eng.Fori(1, SURE // 2) as i:
                body(i * 2, 0, i)
                body(i * 2 + 1, 1, i)
            last = eng.value_load(g["window"][0:1, W_EXPERT, WINDOWS + 2:], min_val=SURE - 1, max_val=WINDOWS - 1)
            with eng.Fori(SURE // 2, (WINDOWS + 1) // 2) as i:
                for r in range(2):
                    with eng.If(i * 2 + r < last + 1):
                        body(i * 2 + r, r, i)
                    with eng.Else():
                        eng.sem_inc(passed, 1)
            return last

        def look(eng, row, w, low, high):
            return eng.value_load(g["window"][0:1, row, ds(w, 1)], min_val=low, max_val=high)

        def if_new(eng, w, what):
            if isinstance(w, int) and w == 0:
                what(1)
                return
            with eng.If(look(eng, W_NEW, w, 0, 1) > 0):
                what(look(eng, W_COUNT, w, 1, EXPERTS))
            with eng.Else():
                eng.sem_inc(passed, 1)

        at_least = lambda w, n: not isinstance(w, int) or w >= n

        @block.sync
        def _(q):
            def load(w, pieces):
                def what(count):
                    e = look(q, W_EXPERT, w, 0, EXPERTS - 1)
                    if at_least(w, 1):
                        before = look(q, W_BEFORE, w, 1, EXPERTS)
                    src = lambda name: t[name][0][ds(e, 1), :, :].rearrange("e (k p) n -> p (e k) n", p=P)
                    for p in pieces:
                        if at_least(w, 1):
                            wait_apart(q, lo_done[p], before, passed)
                        if p < GU:
                            k = slice(2 * p, 2 * p + 2)
                            q.dma_start(raw[p][:, :, 0:F_EXP], src("expert_w_gate")[:, k, :]).then_inc(raw_in[p], 16)
                            q.dma_start(raw[p][:, :, F_EXP:D], src("expert_w_up")[:, k, :]).then_inc(raw_in[p], 16)
                        else:
                            k = slice(2 * (p - GU), 2 * (p - GU) + 2)
                            q.dma_start(raw[p][:], src("expert_w_down")[:, k, :]).then_inc(raw_in[p], 16)

                if_new(q, w, what)

            load(0, range(GU))
            load(1, range(GU))

            def body(w, r, i):
                load(w, range(GU, PIECES))
                load(w + 2, range(GU))

            windows(q, body)

        @block.gpsimd
        def _(pool):
            def fetch(v, r):
                pool.dma_start(idx[r][:], t["slot_tok"][ds(v * P, P), :]).then_inc(idx_in[r], 16)

            def gather(v, r, i):
                pool.wait_ge(idx_in[r], i * 16 + 16)
                wait_apart(pool, xt_mm, pos(v - 1), passed)
                pool.indirect_dma_start(xrow[r][:], None, t["xh"],
                                        bass.IndirectOffsetOnAxis(ap=idx[r][:], axis=0)).then_inc(x_in[r], 16)
                wait_apart(pool, x_in[r], i * 16 + 16, passed)

            def down_lo(w):
                def what(count):
                    for p in range(GU, PIECES):
                        wait_apart(pool, hi_done[p], count, passed)
                        pool.tensor_tensor(w_lo[p][:], raw[p][:], w_hi[p][:].bitcast(F32), ALU.subtract).then_inc(lo_done[p], 1)

                if_new(pool, w, what)

            fetch(0, 0)
            gather(0, 0, 0)
            fetch(1, 1)

            def body(w, r, i):
                gather(w + 1, 1 - r, i + r)
                fetch(w + 2, r)
                if at_least(w, 1):
                    down_lo(w - 1)

            last = windows(pool, body)
            down_lo(last)

        @block.scalar
        def _(act):
            def split(w, pieces):
                def what(count):
                    for p in pieces:
                        wait_apart(act, raw_in[p], count * (32 if p < GU else 16), passed)
                        if at_least(w, 1):
                            wait_apart(act, w_used[p], w, passed)
                        nc.scalar.activation(w_hi[p][:], raw[p][:], ACT.Copy).then_inc(hi_done[p], 1)

                if_new(act, w, what)

            def turned(v):
                act.wait_ge(xt_mm, v + 1)
                act.wait_ge(x_split, v)
                for k in range(KD // 2):
                    ins = nc.scalar.activation(xt[:, k, :], xt_ps[:, k * P:(k + 1) * P], ACT.Identity,
                                               bias=g["shift_ffn"][:, k:k + 1], scale=g["scale_ffn"][:, k:k + 1])
                ins.then_inc(xf_act, 1)
                act.wait_ge(xf_act, v + 1)
                act.wait_ge(gu_mm, v)
                nc.scalar.activation(x_hi[:, 0:KD // 2, :], xt[:, 0:KD // 2, :], ACT.Copy).then_inc(xh_act, 1)

            def prod_hi(w):
                act.wait_ge(at_mm, w + 1)
                act.wait_ge(y_mm, w)
                nc.scalar.activation(p_hi[:].rearrange("p k n -> p (k n)"), at_ps[:], ACT.Copy).then_inc(ph_done, 1)

            def store(v):
                act.wait_ge(y_mm, v + 1)
                act.wait_ge(y_out, v * 16)
                nc.scalar.activation(y[:, 0:BANK], y_ps[:, 0:BANK], ACT.Copy).then_inc(y_act, 1)
                act.wait_ge(y_act, v + 1)
                act.wait_ge(y_dve, v + 1)
                act.dma_start(t["ybuf"][ds(v * P, P), :], y[:]).then_inc(y_out, 16)

            split(0, range(GU))
            turned(0)

            def body(w, r, i):
                if at_least(w, 2):
                    store(w - 2)
                if at_least(w, 1):
                    prod_hi(w - 1)
                    split(w - 1, range(GU, PIECES))
                split(w + 1, range(GU - 1))
                act.wait_ge(gu_mm, w + 1)
                act.wait_ge(prod_done, w)
                nc.scalar.activation(sg[:], gate_ps[:], ACT.Silu).then_inc(sg_done, 1)
                turned(w + 1)
                split(w + 1, range(GU - 1, GU))

            last = windows(act, body)
            store(look(act, W_NEW, WINDOWS + 2, SURE - 2, WINDOWS - 2))
            prod_hi(last)
            split(last, range(GU, PIECES))
            store(last)
            act.wait_ge(y_out, last * 16 + 16)
            act.sem_inc(passed, 1)

        @block.vector
        def _(dve):
            def split(w, pieces):
                def what(count):
                    for p in pieces:
                        wait_apart(dve, hi_done[p], count, passed)
                        dve.tensor_tensor(w_lo[p][:], raw[p][:], w_hi[p][:].bitcast(F32), ALU.subtract).then_inc(lo_done[p], 1)

                if_new(dve, w, what)

            def turned(v):
                second = slice(KD // 2, KD)
                dve.wait_ge(xt_mm, v + 1)
                for k in range(KD // 2, KD):
                    ins = dve.tensor_scalar(xt[:, k, :], xt_ps[:, k * P:(k + 1) * P], g["scale_ffn"][:, k:k + 1],
                                            g["shift_ffn"][:, k:k + 1], ALU.mult, ALU.add)
                ins.then_inc(xf_dve, 1)
                dve.wait_ge(xf_dve, v + 1)
                dve.wait_ge(gu_mm, v)
                dve.tensor_copy(x_hi[:, second, :], xt[:, second, :]).then_inc(xh_dve, 1)
                dve.wait_ge(xh_dve, v + 1)
                dve.wait_ge(xh_act, v + 1)
                dve.tensor_tensor(x_lo[:], xt[:], x_hi[:].bitcast(F32), ALU.subtract).then_inc(x_split, 1)

            def prod_lo(w):
                dve.wait_ge(ph_done, w + 1)
                dve.tensor_tensor(p_lo[:].rearrange("p k n -> p (k n)"), at_ps[:],
                                  p_hi[:].rearrange("p k n -> p (k n)").bitcast(F32), ALU.subtract).then_inc(p_split, 1)

            def store(v):
                dve.wait_ge(y_mm, v + 1)
                dve.wait_ge(y_out, v * 16)
                dve.tensor_copy(y[:, BANK:D], y_ps[:, BANK:D]).then_inc(y_dve, 1)

            split(0, range(GU))
            turned(0)

            def body(w, r, i):
                if at_least(w, 2):
                    store(w - 2)
                if at_least(w, 1):
                    prod_lo(w - 1)
                split(w + 1, range(GU - 1))
                dve.wait_ge(sg_done, w + 1)
                dve.wait_ge(at_mm, w)
                dve.tensor_tensor(prod[:], up_ps[:], sg[:], ALU.mult).then_inc(prod_done, 1)
                turned(w + 1)
                split(w + 1, range(GU - 1, GU))

            last = windows(dve, body)
            store(look(dve, W_NEW, WINDOWS + 2, SURE - 2, WINDOWS - 2))
            prod_lo(last)
            store(last)

        @block.tensor
        def _(pe):
            def turn(v, r, i):
                pe.wait_ge(x_in[r], i * 16 + 16)
                pe.wait_ge(xf_act, v)
                pe.wait_ge(xf_dve, v)
                for k in range(KD):
                    tr = pe.transpose(xt_ps[:, k * P:(k + 1) * P], xrow[r][:, k * P:(k + 1) * P], g["ident"][:])
                tr.then_inc(xt_mm, 1)

            def down(v):
                count = 1 if isinstance(v, int) and v == 0 else look(pe, W_COUNT, v, 1, EXPERTS)
                pe.wait_ge(p_split, v + 1)
                pe.wait_ge(y_act, v)
                pe.wait_ge(y_dve, v)
                for p in range(GU, PIECES):
                    wait_apart(pe, lo_done[p], count, passed)
                    for k in range(2):
                        kk = 2 * (p - GU) + k
                        for a, b in ((p_hi, w_hi), (p_hi, w_lo), (p_lo, w_hi)):
                            for h in range(2):
                                mm = pe.matmul(y_ps[:, h * BANK:(h + 1) * BANK], a[:, kk, :], b[p][:, k, h * BANK:(h + 1) * BANK],
                                               start=(kk == 0 and a is p_hi and b is w_hi),
                                               stop=(kk == FT - 1 and a is p_lo), skip_group_check=True)
                    mm.then_inc(w_used[p], 1)

            def body(w, r, i):
                count = 1 if isinstance(w, int) and w == 0 else look(pe, W_COUNT, w, 1, EXPERTS)
                pe.wait_ge(x_split, w + 1)
                pe.wait_ge(prod_done, w)
                for p in range(GU):
                    wait_apart(pe, lo_done[p], count, passed)
                    for k in range(2):
                        kk = 2 * p + k
                        for a, b in ((x_hi, w_hi), (x_hi, w_lo), (x_lo, w_hi)):
                            for out, h in ((gate_ps, 0), (up_ps, 1)):
                                mm = pe.matmul(out[:], a[:, kk, :], b[p][:, k, h * BANK:(h + 1) * BANK],
                                               start=(kk == 0 and a is x_hi and b is w_hi), stop=(kk == KD - 1 and a is x_lo),
                                               skip_group_check=True)
                    mm.then_inc(w_used[p], 1)
                turn(w + 1, 1 - r, i + r)
                if at_least(w, 1):
                    down(w - 1)
                pe.wait_ge(prod_done, w + 1)
                pe.wait_ge(p_split, w)
                for k in range(FT):
                    tr = pe.transpose(at_ps[:, k * P:(k + 1) * P], prod[:, k * P:(k + 1) * P], g["ident"][:])
                tr.then_inc(at_mm, 1)

            turn(0, 0, 0)
            last = windows(pe, body)
            down(last)


def phase_combine(nc, t, g):
    with ExitStack() as ctx:
        sb = lambda n, s, d=F32: ctx.enter_context(nc.sbuf_tensor(n, s, d))
        sem = ctx.enter_context(semaphores(nc))
        SLOTS = 4
        buf = lambda n, s, d=F32: [sb(f"{n}{b}", s, d) for b in range(SLOTS)]
        sems = lambda n: [sem(f"{n}{b}") for b in range(SLOTS)]
        row = [buf(f"c_idx{k}_", [P, 1], U32) for k in range(2)]
        yr = [buf(f"c_y{k}_", [P, D]) for k in range(2)]
        wt, x2, acc, st, out = (buf(n, s) for n, s in (
            ("c_wt", [P, 2]), ("c_x2", [P, D]), ("c_acc", [P, D]), ("c_st", [P, 4]), ("c_out", [P, D])))
        sq = [sb(f"c_sq{b}", [P, D]) for b in range(2)]
        x2_in, y_in, outs = sems("c_x2_in"), [sems(f"c_y{k}_in") for k in range(2)], sems("c_outs")
        row_set, share, chain, summed, squared, root, done, used = (sem(n) for n in (
            "c_row_set", "c_share", "c_chain", "c_summed", "c_squared", "c_root", "c_done", "c_used"))
        block = ctx.enter_context(nc.Block())

        def tiles(eng, body):
            for r in range(SLOTS):
                body(r, r, 0)
            with eng.Fori(1, TOK_TILES // SLOTS) as i:
                for r in range(SLOTS):
                    body(i * SLOTS + r, r, i)

        is_first = lambda n: isinstance(n, int) and n == 0

        @block.sync
        def _(q):
            def body(n, r, i):
                if not isinstance(n, int):
                    wait_apart(q, summed, n - SLOTS + 1, used)
                q.dma_start(x2[r][:], t["x2"][ds(n * P, P), :]).then_inc(x2_in[r], 16)

            tiles(q, body)
            for r in range(SLOTS):
                q.wait_ge(outs[r], 16 * (TOK_TILES // SLOTS))

        @block.gpsimd
        def _(pool):
            def body(n, r, i):
                if not isinstance(n, int):
                    wait_apart(pool, summed, n - SLOTS + 1, used)
                for k in range(2):
                    pool.tensor_copy(wt[r][:, k:k + 1], g["weight"][k][:, ds(n, 1)])
                for k in range(2):
                    ins = pool.tensor_copy(row[k][r][:], g["dest"][k][:, ds(n, 1)])
                ins.then_inc(row_set, 1)
                wait_apart(pool, row_set, n + 1, used)
                for k in range(2):
                    pool.indirect_dma_start(yr[k][r][:], None, t["ybuf"],
                                            bass.IndirectOffsetOnAxis(ap=row[k][r][:], axis=0)).then_inc(y_in[k][r], 16)

            tiles(pool, body)

        @block.scalar
        def _(act):
            def norm(n, r):
                act.wait_ge(summed, n + 1)
                nc.scalar.activation(sq[r % 2][:], acc[r][:], ACT.Square, accum_out=st[r][:, 0:1]).then_inc(squared, 1)
                act.wait_ge(squared, n + 1)
                nc.scalar.activation(st[r][:, 1:2], st[r][:, 0:1], ACT.Sqrt, bias=g["eps"][:], scale=1.0 / D).then_inc(root, 1)

            def store(n, r):
                act.wait_ge(done, n + 1)
                act.dma_start(t["out"][0][ds(n * P, P), :], out[r][:]).then_inc(outs[r], 16)

            def body(n, r, i):
                act.wait_ge(y_in[0][r], i * 16 + 16)
                act.wait_ge(row_set, n + 1)
                if not isinstance(n, int):
                    act.wait_ge(done, n - SLOTS + 1)
                nc.scalar.activation(acc[r][:], yr[0][r][:], ACT.Copy, scale=wt[r][:, 0:1]).then_inc(share, 1)
                if not is_first(n):
                    norm(n - 1, (r - 1) % SLOTS)
                if not is_first(n) and not (isinstance(n, int) and n == 1):
                    store(n - 2, (r - 2) % SLOTS)

            tiles(act, body)
            norm(TOK_TILES - 1, SLOTS - 1)
            for n in (TOK_TILES - 2, TOK_TILES - 1):
                store(n, n % SLOTS)

        @block.vector
        def _(dve):
            def finish(n, r, i, links):
                c = Chain(dve, chain, links)
                dve.wait_ge(root, n + 1)
                c.link(dve.reciprocal(st[r][:, 2:3], st[r][:, 1:2]))
                if not (isinstance(i, int) and i == 0):
                    dve.wait_ge(outs[r], i * 16)
                dve.scalar_tensor_tensor(out=out[r][:], in0=acc[r][:], scalar=st[r][:, 2:3], in1=g["final_w"][:],
                                         op0=ALU.mult, op1=ALU.mult).then_inc(done, 1)

            def body(n, r, i):
                links = n * 3 - 1 if not is_first(n) else 0
                c = Chain(dve, chain, links)
                dve.wait_ge(share, n + 1)
                dve.wait_ge(y_in[1][r], i * 16 + 16)
                c.link(dve.scalar_tensor_tensor(out=acc[r][:], in0=yr[1][r][:], scalar=wt[r][:, 1:2], in1=acc[r][:],
                                                op0=ALU.mult, op1=ALU.add))
                c.link(dve.tensor_tensor(acc[r][:], acc[r][:], g["gates"][:, 1, :], ALU.mult))
                dve.wait_ge(x2_in[r], i * 16 + 16)
                dve.tensor_tensor(acc[r][:], acc[r][:], x2[r][:], ALU.add).then_inc(summed, 1)
                if not is_first(n):
                    finish(n - 1, (r - 1) % SLOTS, i if r > 0 else i - 1, n * 3 + 1)

            tiles(dve, body)
            finish(TOK_TILES - 1, SLOTS - 1, TOK_TILES // SLOTS - 1, TOK_TILES * 3 - 1)


_INS = ['x', 'c', 'ada_w', 'ada_b', 'norm_mix_w', 'w_in', 'conv_w', 'conv_b', 'lru_wa', 'lru_ba', 'lru_wx', 'lru_bx',
        'lru_lambda', 'norm_lru_w', 'hgrn_lb', 'norm_hgrn_w', 'w_out', 'norm_ffn_w', 'router_group_w', 'router_group_b',
        'router_expert_w', 'router_expert_b', 'expert_w_gate', 'expert_w_up', 'expert_w_down', 'final_norm_w']
_SCRATCH = [("projT", (GROUPS * CH, SEQ), F32), ("mergedT", (D, SEQ), F32), ("x2", (SEQ, D), F32), ("xh", (SEQ, D), F32),
            ("slot_tok", ((WINDOWS + 3) * P, 1), I32), ("ybuf", ((WINDOWS + 1) * P, D), F32)]


def build(nc, t):
    for name, shape, dt in _SCRATCH:
        t[name] = nc.dram_tensor(name, shape, dt, kind="Internal").ap()
    with ExitStack() as ctx:
        g = persistent(nc, ctx)
        with ExitStack() as own:
            g["hT"] = own.enter_context(nc.sbuf_tensor("hT", [P, KD, SEQ], F32))
            phase_modulate(nc, t, g)
            phase_project(nc, t, g)
        phase_hgrn(nc, t, g)
        persistent2(nc, ctx, g)
        phase_output(nc, t, g)
        phase_route(nc, t, g)
        phase_experts(nc, t, g)
        phase_combine(nc, t, g)


def kernel(**inputs):
    import numpy as np
    import concourse.bacc as bacc
    from concourse.bass_utils import run_bass_kernel_spmd

    nc = bacc.Bacc("TRN2", target_bir_lowering=False, num_devices=1)
    arrays, t = {}, {}
    for name in _INS:
        a = np.ascontiguousarray(inputs[name])
        arrays[f"in_{name}"] = a
        t[name] = nc.dram_tensor(f"in_{name}", a.shape, mybir.dt.from_np(a.dtype), kind="ExternalInput").ap()
    t["out"] = nc.dram_tensor("out", (1, SEQ, D), F32, kind="ExternalOutput").ap()
    build(nc, t)
    r = run_bass_kernel_spmd(nc, [arrays], core_ids=[0])
    return r.results[0]["out"]
```

```python
from contextlib import ExitStack, contextmanager

import concourse.bass as bass
from concourse import mybir

F32 = mybir.dt.float32
F32R = mybir.dt.float32r
I32 = mybir.dt.int32
U32 = mybir.dt.uint32
ALU = mybir.AluOpType
ACT = mybir.ActivationFunctionType
AX = mybir.AxisListType.X

P = 128
BANK = 512
SEQ = 2048
D = 1024
KD = D // P
CH = 512
CT = CH // P
GROUPS = 7
TOK_TILES = SEQ // P
TOK_CHUNKS = SEQ // BANK
HEAD = 64
EPS = 1e-6
N_GROUPS = 4
EPG = 8
EXPERTS = N_GROUPS * EPG
F_EXP = 512
LRU_C = 8.0
ROUTES = N_GROUPS + EXPERTS
ASSIGN = 2 * SEQ
WINDOWS = EXPERTS + (ASSIGN - EXPERTS) // P
ADA_CHUNKS = 6 * D // BANK
SURE = ASSIGN // P
W_EXPERT, W_NEW, W_COUNT, W_BEFORE = range(4)
ds = bass.ds

V_ADA_B, V_NORM_MIX, V_NORM_FFN, V_CONV_W, V_CONV_B, V_BA, V_BX, V_LAM, V_NORM_LRU, V_LB, V_NORM_HG, V_END = (
    0, 48, 56, 64, 80, 84, 92, 100, 108, 112, 116, 120)


class Chain:

    def __init__(self, eng, sem, base=0):
        self.eng, self.sem, self.base, self.n = eng, sem, base, 0

    def link(self, ins):
        ins.then_inc(self.sem, 1)
        self.n += 1
        self.eng.wait_ge(self.sem, self.base + self.n)


@contextmanager
def semaphores(nc):
    made = []

    def take(name):
        made.append(nc.alloc_semaphore(name))
        return made[-1]

    yield take
    nc.clear_and_free_semaphores(made)
    nc.all_engine_barrier()


def bcast_inner(ap, n):
    return ap.unsqueeze(ap.ndim).to_broadcast(list(ap.shape) + [n])


def phase_modulate(nc, t, g):
    with ExitStack() as ctx:
        sb = lambda n, s, d=F32: ctx.enter_context(nc.sbuf_tensor(n, s, d))
        sem = ctx.enter_context(semaphores(nc))
        bank = [ctx.enter_context(nc.psum_tensor(f"m_bank{i}", [P, BANK], F32)) for i in range(8)]
        cond = sb("cond", [P, KD])
        cond_in = sb("cond_in", [P, KD])
        cond_rep = sb("cond_rep", [P, KD, P])
        rows = sb("rows", [P, P])
        lines = sb("lines", [P, 2 * D])
        mod_row, fin_row, bias_row = lines[0:1, :], lines[32:33, 0:D], lines[HEAD:HEAD + 1, :]
        ada = [sb(f"ada{i}", [P, KD, BANK]) for i in range(3)]
        mod_raw = sb("mod_raw", [P, 2, 16])
        shift = sb("shift_mix", [P, KD])
        scale = sb("scale_mix", [P, KD])
        xg = [sb(f"xg{i}", [P, 4, D]) for i in range(2)]
        xn = sb("xn", [P, 4, D])
        junk = sb("junk", [P, 4, D])
        ssq = sb("ssq", [P, 4])
        std = sb("std", [P, 4])
        rstd = sb("rstd", [P, 4])
        c_in, rows_in, row_in, x_in = sem("c_in"), sem("rows_in"), sem("row_in"), [sem(f"x_in{i}") for i in range(2)]
        ada_in = [sem(f"ada_in{i}") for i in range(3)]
        consts, cond_done, rep_done, rows_zero = sem("consts"), sem("cond_done"), sem("rep_done"), sem("rows_zero")
        cols_ps, cols_sb = sem("cols_ps"), sem("cols_sb")
        mod_ps, mod_sb, chunk_mm, chunk_sb = sem("mod_ps"), sem("mod_sb"), sem("chunk_mm"), sem("chunk_sb")
        affine, fin_ps, dve_chain, pool_chain = (
            sem("affine"), sem("fin_ps"), sem("m_dve_chain"), sem("m_pool_chain"))
        sq_done, std_done, xn_done, tr_done, h_act, h_dve = (
            sem("sq_done"), sem("std_done"), sem("xn_done"), sem("tr_done"), sem("h_act"), sem("h_dve"))
        block = ctx.enter_context(nc.Block())

        @block.sync
        def _(sp):
            sp.dma_start(cond_in[:], t["c"].rearrange("a (p j) -> (a p) j", j=KD)).then_inc(c_in, 16)
            sp.wait_ge(rows_zero, 1)
            for at, src in (
                (V_ADA_B, t["ada_b"].rearrange("a (r p) -> (a r) p", p=P)),
                (V_NORM_MIX, t["norm_mix_w"].rearrange("a (r p) -> (a r) p", p=P)),
                (V_NORM_FFN, t["norm_ffn_w"].rearrange("a (r p) -> (a r) p", p=P)),
                (V_CONV_W, t["conv_w"].rearrange("a j (r p) -> (a j r) p", p=P)),
                (V_CONV_B, t["conv_b"].rearrange("a (r p) -> (a r) p", p=P)),
                (V_BA, t["lru_ba"].rearrange("a d (r p) -> (a d r) p", p=P)),
                (V_BX, t["lru_bx"].rearrange("a d (r p) -> (a d r) p", p=P)),
                (V_LAM, t["lru_lambda"].rearrange("a d (r p) -> (a d r) p", p=P)),
                (V_NORM_LRU, t["norm_lru_w"].rearrange("a (r p) -> (a r) p", p=P)),
                (V_LB, t["hgrn_lb"].rearrange("a (r p) -> (a r) p", p=P)),
                (V_NORM_HG, t["norm_hgrn_w"].rearrange("a (r p) -> (a r) p", p=P)),
            ):
                sp.dma_start(rows[at:at + src.shape[0], :], src).then_inc(rows_in, 16)
            sp.dma_start(bias_row.rearrange("a (h n) -> a h n", h=2), t["ada_b"].rearrange("a (h v n) -> a h v n", h=2, v=3)[:, :, 2, :]).then_inc(row_in, 16)
            sp.dma_start(fin_row, t["final_norm_w"].rearrange("(a n) -> a n", a=1)).then_inc(row_in, 16)
            sp.dma_start(g["route_bias"][0:1, 0:N_GROUPS], t["router_group_b"]).then_inc(row_in, 16)
            sp.dma_start(g["route_bias"][0:1, N_GROUPS:ROUTES], t["router_expert_b"]).then_inc(row_in, 16)

            def ada_chunks(i):
                for b in range(3):
                    if not (isinstance(i, int) and i == 0):
                        sp.wait_ge(chunk_mm, i * 3 + b - 2)
                    sp.dma_start(ada[b][:], t["ada_w"][0].rearrange("(p j) n -> p j n", j=KD)[
                        :, :, ds(i * (3 * BANK) + b * BANK, BANK)]).then_inc(ada_in[b], 16)

            rounds(sp, ADA_CHUNKS // 3, ada_chunks)

        @block.gpsimd
        def _(pool):
            pc = Chain(pool, pool_chain)
            pool.memset(rows[:], 0.0).then_inc(rows_zero, 1)
            pool.memset(g["ones"][:], 1.0).then_inc(consts, 1)
            pool.memset(g["eps"][:], EPS).then_inc(consts, 1)
            pc.link(pool.memset(g["ident"][:], 0.0))
            pool.affine_select(out=g["ident"][:], in_=g["ident"][:], compare_op=ALU.not_equal, fill=1.0, base=0,
                               pattern=[[-1, P]], channel_multiplier=1).then_inc(consts, 1)
            for i in range(TOK_CHUNKS):
                if i >= 2:
                    pool.wait_ge(xn_done, i - 1)
                    pool.wait_ge(sq_done, i - 1)
                pool.dma_start(xg[i % 2][:], t["x"][0].rearrange("(a p) d -> p a d", p=P)[:, i * 4:i * 4 + 4, :]).then_inc(
                    x_in[i % 2], 16)

        @block.scalar
        def _(act):
            act.wait_ge(c_in, 16)
            nc.scalar.activation(cond[:], cond_in[:], ACT.Silu).then_inc(cond_done, 1)
            act.wait_ge(consts, 3)
            for i in range(TOK_CHUNKS):
                act.wait_ge(x_in[i % 2], (i // 2) * 16 + 16)
                if i > 0:
                    act.wait_ge(std_done, i * 2)
                for a in range(4):
                    last = nc.scalar.activation(junk[:, a, :], xg[i % 2][:, a, :], ACT.Square, accum_out=ssq[:, a:a + 1])
                last.then_inc(sq_done, 1)
                act.wait_ge(sq_done, i + 1)
                nc.scalar.activation(std[:], ssq[:], ACT.Sqrt, bias=g["eps"][:], scale=1.0 / D).then_inc(std_done, 1)
                act.wait_ge(affine, 2)
                for k in range(0, KD, 2):
                    act.wait_ge(tr_done, i * KD + k + 1)
                    nc.scalar.activation(g["hT"][:, k, i * BANK:(i + 1) * BANK], bank[k % 4][:], ACT.Identity,
                                         bias=shift[:, k:k + 1], scale=scale[:, k:k + 1]).then_inc(h_act, 1)

        @block.vector
        def _(dve):
            dve.wait_ge(cond_done, 1)
            dve.tensor_copy(cond_rep[:], bcast_inner(cond[:], P)).then_inc(rep_done, 1)
            dve.wait_ge(cols_ps, 1)
            dve.tensor_copy(g["cols"][:], bank[7][:, 0:P]).then_inc(cols_sb, 1)
            dc = Chain(dve, dve_chain)
            for q in range(2):
                dve.wait_ge(fin_ps, q + 1)
                dve.tensor_copy(g["final_w"][:, q * BANK:(q + 1) * BANK], bank[5 + q][:]).then_inc(cols_sb, 1)

            def chunk_out(n):
                h, q = n // 6, n % 6
                dve.wait_ge(chunk_mm, n + 1)
                if q < 4:
                    if h > 0:
                        dve.wait_ge(mod_ps, h)
                    ins = dve.tensor_copy(mod_row[:, q * BANK:(q + 1) * BANK], bank[5 + n % 2][0:1, :])
                else:
                    ins = dve.tensor_copy(g["gates"][:, h, (q - 4) * BANK:(q - 3) * BANK], bank[5 + n % 2][:])
                ins.then_inc(chunk_sb, 1)

            for n in range(4):
                chunk_out(n)
            dve.wait_ge(mod_ps, 1)
            dve.tensor_copy(mod_raw[:, 0, :], bank[4][:, 0:16]).then_inc(mod_sb, 1)
            dve.wait_ge(mod_sb, 1)
            dve.wait_ge(cols_sb, 1)
            dve.tensor_tensor(shift[:], mod_raw[:, 0, 0:8], g["cols"][:, 0:8], ALU.add).then_inc(affine, 1)
            dc.link(dve.tensor_tensor(scale[:], mod_raw[:, 0, 8:16], g["cols"][:, 8:16], ALU.add))
            dve.scalar_tensor_tensor(out=scale[:], in0=scale[:], scalar=1.0, in1=g["cols"][:, V_NORM_MIX:V_NORM_MIX + 8],
                                     op0=ALU.add, op1=ALU.mult).then_inc(affine, 1)
            dve.wait_ge(affine, 2)

            for i in range(TOK_CHUNKS):
                dve.wait_ge(std_done, i * 2 + 1)
                dve.reciprocal(rstd[:], std[:]).then_inc(std_done, 1)
                dve.wait_ge(std_done, i * 2 + 2)
                if i > 0:
                    dve.wait_ge(tr_done, i * KD)
                dve.wait_ge(x_in[i % 2], (i // 2) * 16 + 16)
                for a in range(4):
                    last = dve.tensor_scalar(xn[:, a, :], xg[i % 2][:, a, :], rstd[:, a:a + 1], None, ALU.mult)
                last.then_inc(xn_done, 1)
                for k in range(1, KD, 2):
                    dve.wait_ge(tr_done, i * KD + k + 1)
                    dve.tensor_scalar(g["hT"][:, k, i * BANK:(i + 1) * BANK], bank[k % 4][:], scale[:, k:k + 1],
                                      shift[:, k:k + 1], ALU.mult, ALU.add).then_inc(h_dve, 1)
                if i == 3:
                    dve.wait_ge(mod_ps, 2)
                    dve.tensor_copy(mod_raw[:, 1, :], bank[4][:, 0:16]).then_inc(mod_sb, 1)
                    dve.wait_ge(mod_sb, 2)
                    dve.tensor_tensor(g["shift_ffn"][:], mod_raw[:, 1, 0:8], g["cols"][:, 24:32], ALU.add)
                    dc.link(dve.tensor_tensor(g["scale_ffn"][:], mod_raw[:, 1, 8:16], g["cols"][:, 32:40], ALU.add))
                    dve.scalar_tensor_tensor(out=g["scale_ffn"][:], in0=g["scale_ffn"][:], scalar=1.0,
                                             in1=g["cols"][:, V_NORM_FFN:V_NORM_FFN + 8], op0=ALU.add, op1=ALU.mult)
                for n in (4 + 2 * i, 5 + 2 * i):
                    chunk_out(n)

        @block.tensor
        def _(pe):
            pe.wait_ge(consts, 3)
            pe.wait_ge(rows_in, 16 * 11)
            pe.transpose(bank[7][:, 0:P], rows[:], g["ident"][:]).then_inc(cols_ps, 1)
            pe.wait_ge(row_in, 64)
            for q in range(2):
                pe.matmul(bank[5 + q][:], g["ones"][32:33, :], fin_row[:, q * BANK:(q + 1) * BANK],
                          start=True, stop=True).then_inc(fin_ps, 1)
            pe.wait_ge(rep_done, 1)
            pe.wait_ge(cond_done, 1)
            pe.wait_ge(cols_sb, 1)

            def modulation(n):
                h, q = n // 6, n % 6
                w, out = ada[n % 3], bank[5 + n % 2]
                pe.wait_ge(ada_in[n % 3], n // 3 * 16 + 16)
                pe.wait_ge(*((cols_sb, 3) if n < 2 else (chunk_sb, n - 1)))
                if q < 4:
                    for j in range(KD):
                        mm = pe.matmul(out[0:1, :], cond[:, j:j + 1], w[:, j, :], start=(j == 0), stop=(j == KD - 1))
                else:
                    for j in range(KD):
                        pe.matmul(out[:], cond_rep[:, j, :], w[:, j, :], start=(j == 0), stop=False)
                    mm = pe.matmul(out[:], g["ones"][HEAD:HEAD + 1, :], bias_row[:, h * D + (q - 4) * BANK:h * D + (q - 3) * BANK],
                                   start=False, stop=True)
                mm.then_inc(chunk_mm, 1)

            def columns(h):
                pe.wait_ge(chunk_sb, 6 * h + 4)
                if h > 0:
                    pe.wait_ge(mod_sb, h)
                for m in range(2 * KD):
                    mm = pe.matmul(bank[4][:, m:m + 1], mod_row[:, m * P:(m + 1) * P], g["ones"][0:1, 0:1], start=True, stop=True)
                mm.then_inc(mod_ps, 1)

            for n in range(4):
                modulation(n)
            columns(0)
            for i in range(TOK_CHUNKS):
                pe.wait_ge(xn_done, i + 1)
                for k in range(KD):
                    before = i * (KD // 2) + k // 2 - 1
                    if before > 0:
                        pe.wait_ge(h_dve if k % 2 else h_act, before)
                    for a in range(4):
                        tr = pe.transpose(bank[k % 4][:, a * P:(a + 1) * P], xn[:, a, k * P:(k + 1) * P], g["ident"][:])
                    tr.then_inc(tr_done, 1)
                if i == 3:
                    columns(1)
                for n in (4 + 2 * i, 5 + 2 * i):
                    modulation(n)


def persistent(nc, ctx):
    sb = lambda n, s, d=F32: ctx.enter_context(nc.sbuf_tensor(n, s, d))
    return dict(
        ident=sb("ident", [P, P]), ones=sb("ones", [P, P]), eps=sb("eps", [P, 1]),
        cols=sb("cols", [P, P]), gates=sb("gates", [P, 2, D]), final_w=sb("final_w", [P, D]),
        shift_ffn=sb("shift_ffn", [P, KD]), scale_ffn=sb("scale_ffn", [P, KD]), route_bias=sb("route_bias", [1, ROUTES]),
    )


def persistent2(nc, ctx, g):
    sb = lambda n, s, d=F32: ctx.enter_context(nc.sbuf_tensor(n, s, d))
    g["logits"] = sb("logits", [P, TOK_TILES, ROUTES])
    g["weight"] = [sb(f"weight{k}", [P, TOK_TILES]) for k in range(2)]
    g["dest"] = [sb(f"dest{k}", [P, TOK_TILES], U32) for k in range(2)]
    g["token"] = sb("token", [P, TOK_TILES], I32)
    g["window"] = sb("window", [1, 4, WINDOWS + 3], I32)


def pos(value):
    return max(value, 0) if isinstance(value, int) else value


def rounds(eng, n, body):
    body(0)
    with eng.Fori(1, n) as i:
        body(i)


def pairs(eng, n, body):
    for k in range(3):
        body(k, k % 2, k // 2)
    with eng.Fori(1, n // 2 - 1) as i:
        body(i * 2 + 1, 1, i)
        body(i * 2 + 2, 0, i + 1)
    body(n - 1, 1, n // 2 - 1)


def wait_apart(eng, sem, value, passed):
    eng.wait_ge(sem, value)
    eng.sem_inc(passed, 1)


def at_least(w, n):
    return not isinstance(w, int) or w >= n


def phase_project(nc, t, g):
    with ExitStack() as ctx:
        sb = lambda n, s, d=F32: ctx.enter_context(nc.sbuf_tensor(n, s, d))
        sem = ctx.enter_context(semaphores(nc))
        bank = [ctx.enter_context(nc.psum_tensor(f"p_bank{i}", [P, BANK], F32)) for i in range(8)]
        hT = g["hT"]
        w = [sb(f"w_in{m}", [P, KD, P]) for m in range(CT)]
        stage = [sb(f"proj_stage{i}", [P, SEQ]) for i in range(2)]
        xin = sb("lru_x", [P, SEQ + 3])
        xc = sb("lru_xc", [P, SEQ])
        y = sb("lru_y", [P, SEQ])
        R = [sb(f"lru_r{d}", [P, SEQ]) for d in range(2)]
        I = [sb(f"lru_i{d}", [P, SEQ]) for d in range(2)]
        T = [sb(f"lru_t{d}", [P, SEQ]) for d in range(2)]
        gw = sb("lru_gate_w", [P, 4, P])
        par = sb("lru_par", [P, 12])
        neg = sb("lru_neg", [P, 2])
        sp = [sb(f"softplus{i}", [P, 8]) for i in range(5)]
        tmp = xin[:, 2:2 + SEQ]
        w_in = [sem(f"w_in_s{m}") for m in range(CT)]
        mm_done, evac, stored = sem("mm_done"), sem("evac"), [sem(f"stored{i}") for i in range(2)]
        x_in, y_in, gw_in, gw_zero = sem("lru_x_in"), sem("lru_y_in"), sem("gw_in"), sem("gw_zero")
        conv_done, gate_mm, gate_act = sem("conv_done"), sem("gate_mm"), sem("gate_act")
        ea, tanh_done, exp_done, pre_root, root_done, gelu_done = (
            sem("softplus_exp"), sem("tanh_done"), sem("exp_done"), sem("pre_root"), sem("root_done"), sem("gelu_done"))
        lru_done, lru_stored, chain, par_done = sem("lru_done"), sem("lru_stored"), sem("lru_chain"), sem("par_done")
        zero_out = sem("zero_out")
        zeros = sb("zeros", [P, D])
        CHAIN = 11
        block = ctx.enter_context(nc.Block())
        src_w = t["w_in"][0].rearrange("(k p) n -> p k n", p=P)

        def over_groups(eng, body):
            body(0, None)
            body(1, None)
            body(2, 0)
            with eng.Fori(1, CT) as i:
                body(i + 2, i)
            body(GROUPS - 1, None)

        @block.sync
        def _(q):
            for m in range(CT):
                q.dma_start(w[m][:], src_w[:, :, m * P:(m + 1) * P]).then_inc(w_in[m], 16)

            def body(gr, i):
                if i is not None:
                    q.wait_ge(lru_stored, i * 16)
                    q.wait_ge(gw_zero, 1)
                    for s in range(2):
                        q.wait_ge(stored[s], 64)
                    q.dma_start(xin[:, 2:2 + SEQ], t["projT"][ds(i * P, P), :]).then_inc(x_in, 16)
                    q.dma_start(y[:], t["projT"][ds(i * P + CH, P), :]).then_inc(y_in, 16)
                    for half in range(2):
                        at = slice(half * HEAD, (half + 1) * HEAD)
                        for gate, name in ((0, "lru_wa"), (2, "lru_wx")):
                            q.dma_start(gw[at, gate:gate + 2, at], t[name][0].rearrange("d h i j -> h i d j")[
                                ds(i * 2 + half, 1), :, :, :].rearrange("h i d j -> (h i) d j")).then_inc(gw_in, 16)
                for m in range(CT):
                    q.wait_ge(evac, gr * 16 + m * 4 + 4)
                    q.dma_start(t["projT"][ds(gr * CH + m * P, P), :], stage[m % 2][:]).then_inc(stored[m % 2], 16)
                    if not (isinstance(gr, int) and gr == GROUPS - 1):
                        q.wait_ge(mm_done, gr * 16 + m * 4 + 4)
                        q.dma_start(w[m][:], src_w[:, :, ds((gr + 1) * CH + m * P, P)]).then_inc(w_in[m], 16)
                if i is not None:
                    q.wait_ge(lru_done, i + 1)
                    q.dma_start(t["mergedT"][ds(i * P, P), :], tmp).then_inc(lru_stored, 16)

            over_groups(q, body)
            q.wait_ge(lru_stored, 16 * CT)
            for s in range(2):
                q.wait_ge(stored[s], 16 * 2 * GROUPS)

        @block.gpsimd
        def _(pool):
            pool.memset(xin[:], 0.0)
            pool.memset(zeros[:], 0.0)
            pool.memset(gw[:], 0.0).then_inc(gw_zero, 1)
            pool.wait_ge(gw_zero, 1)
            with pool.Fori(SURE, WINDOWS + 1) as i:
                pool.dma_start(t["ybuf"][ds(i * P, P), :], zeros[:]).then_inc(zero_out, 16)
            pool.wait_ge(zero_out, 16 * (WINDOWS + 1 - SURE))

        @block.scalar
        def _(act):
            nc.scalar.activation(sp[0][:], g["cols"][:, V_LAM:V_LAM + 8], ACT.Abs).then_inc(ea, 1)
            act.wait_ge(ea, 1)
            nc.scalar.activation(sp[1][:], sp[0][:], ACT.Exp, scale=-1.0).then_inc(ea, 1)

            def body(gr, i):
                for m in range(CT):
                    for c in range(TOK_CHUNKS):
                        act.wait_ge(mm_done, gr * 16 + m * 4 + c + 1)
                        if c == 0:
                            act.wait_ge(stored[m % 2], gr * 32 if m < 2 else gr * 32 + 16)
                        nc.scalar.activation(stage[m % 2][:, c * BANK:(c + 1) * BANK], bank[c][:],
                                             ACT.Copy).then_inc(evac, 1)
                    if i is None:
                        continue
                    if m == 0:
                        act.wait_ge(par_done, i + 1)
                        for k in range(4):
                            dst = (R[0], R[1], I[0], I[1])[k]
                            for c in range(TOK_CHUNKS):
                                act.wait_ge(gate_mm, i * 16 + k * 4 + c + 1)
                                nc.scalar.activation(dst[:, c * BANK:(c + 1) * BANK], bank[4 + c][:], ACT.Sigmoid,
                                                     bias=par[:, 5 + k:6 + k]).then_inc(gate_act, 1)
                    if m == 1:
                        act.wait_ge(gate_act, i * 16 + 16)
                        for d in range(2):
                            nc.scalar.activation(T[d][:], R[d][:], ACT.Tanh, scale=par[:, 9 + d:10 + d]).then_inc(tanh_done, 1)
                        act.wait_ge(tanh_done, i * 2 + 2)
                        for d in range(2):
                            nc.scalar.activation(R[d][:], R[d][:], ACT.Exp, scale=neg[:, d:d + 1]).then_inc(exp_done, 1)
                    if m == 2:
                        for d in range(2):
                            act.wait_ge(pre_root, i * 2 + d + 1)
                            nc.scalar.activation(T[d][:], T[d][:], ACT.Sqrt).then_inc(root_done, 1)
                        act.wait_ge(y_in, i * 16 + 16)
                        nc.scalar.activation(y[:], y[:], ACT.Gelu_apprx_tanh).then_inc(gelu_done, 1)

            over_groups(act, body)

        @block.vector
        def _(dve):
            dc = Chain(dve, chain)
            lam = g["cols"][:, V_LAM:V_LAM + 8]
            dve.wait_ge(ea, 2)
            e, u, z, z2, s = sp[1][:], sp[2][:], sp[3][:], sp[0][:], sp[4][:]
            dc.link(dve.tensor_scalar(u, e, 2.0, None, ALU.add))
            dc.link(dve.reciprocal(u, u))
            dc.link(dve.tensor_tensor(z, e, u, ALU.mult))
            dc.link(dve.tensor_tensor(z2, z, z, ALU.mult))
            dc.link(dve.tensor_scalar(s, z2, 1.0 / 17, 1.0 / 15, ALU.mult, ALU.add))
            for n in (13, 11, 9, 7, 5, 3, 1):
                dc.link(dve.tensor_tensor(s, s, z2, ALU.mult))
                dc.link(dve.tensor_scalar(s, s, 1.0 / n, None, ALU.add))
            dc.link(dve.tensor_tensor(s, s, z, ALU.mult))
            dc.link(dve.tensor_scalar(u, lam, -1.0, 0.0, ALU.mult, ALU.max))
            dc.link(dve.tensor_scalar(u, u, LRU_C, None, ALU.mult))
            dc.link(dve.scalar_tensor_tensor(out=lam, in0=s, scalar=2.0 * LRU_C, in1=u, op0=ALU.mult, op1=ALU.add))
            first = dc.n
            table = g["cols"][:, V_CONV_W:V_LB].rearrange("p (r k) -> p r k", k=CT)
            with dve.Fori(0, CT) as i:
                dc = Chain(dve, chain, i * CHAIN + first)
                dc.link(dve.tensor_copy(par[:].unsqueeze(2), table[:, :, ds(i, 1)]))
                dve.tensor_scalar(neg[:], par[:, 9:11], -1.0, None, ALU.mult).then_inc(par_done, 1)
                dve.wait_ge(x_in, i * 16 + 16)
                dc.link(dve.tensor_scalar(xc[:], xin[:, 0:SEQ], par[:, 0:1], par[:, 4:5], ALU.mult, ALU.add))
                for j in range(1, 4):
                    ins = dve.scalar_tensor_tensor(out=xc[:], in0=xin[:, j:j + SEQ], scalar=par[:, j:j + 1], in1=xc[:],
                                                   op0=ALU.mult, op1=ALU.add)
                    if j < 3:
                        dc.link(ins)
                    else:
                        ins.then_inc(conv_done, 1)
                dve.wait_ge(conv_done, i + 1)
                dve.wait_ge(gate_act, i * 16 + 16)
                for d in range(2):
                    dve.tensor_tensor(I[d][:], I[d][:], xc[:], ALU.mult)
                for d in range(2):
                    dve.wait_ge(exp_done, i * 2 + d + 1)
                    dc.link(dve.tensor_tensor(tmp, R[d][:], R[d][:], ALU.mult))
                    dve.scalar_tensor_tensor(out=T[d][:], in0=tmp, scalar=1.0, in1=T[d][:],
                                             op0=ALU.add, op1=ALU.mult).then_inc(pre_root, 1)
                    dve.wait_ge(pre_root, i * 2 + d + 1)
                for d in range(2):
                    dve.wait_ge(root_done, i * 2 + d + 1)
                    dc.link(dve.tensor_tensor(I[d][:], I[d][:], T[d][:], ALU.mult))
                    if d == 0:
                        dc.link(dve.tensor_tensor_scan(T[0][:], R[0][:], I[0][:], 0.0, ALU.mult, ALU.add))
                    else:
                        dc.link(dve.tensor_tensor_scan(T[1][:, ::-1], R[1][:, ::-1], I[1][:, ::-1], 0.0,
                                                       ALU.mult, ALU.add))
                dc.link(dve.tensor_tensor(T[0][:], T[0][:], T[1][:], ALU.add))
                dve.wait_ge(gelu_done, i + 1)
                dve.tensor_tensor(tmp, T[0][:], y[:], ALU.mult).then_inc(lru_done, 1)
                assert dc.n == CHAIN

        @block.tensor
        def _(pe):
            def body(gr, i):
                for m in range(CT):
                    pe.wait_ge(w_in[m], gr * 16 + 16)
                    for c in range(TOK_CHUNKS):
                        if m == 0:
                            pe.wait_ge(evac, gr * 16)
                        else:
                            pe.wait_ge(evac, gr * 16 + m * 4 + c - 3)
                        for k in range(KD):
                            mm = pe.matmul(bank[c][:], w[m][:, k, :], hT[:, k, c * BANK:(c + 1) * BANK],
                                           start=(k == 0), stop=(k == KD - 1))
                        mm.then_inc(mm_done, 1)
                    if i is not None and m == 0:
                        pe.wait_ge(conv_done, i + 1)
                        pe.wait_ge(gw_in, i * 64 + 64)
                        for k in range(4):
                            for c in range(TOK_CHUNKS):
                                n = k * 4 + c - 3
                                pe.wait_ge(gate_act, i * 16 + n if n > 0 else i * 16)
                                pe.matmul(bank[4 + c][:], gw[:, k, :], xc[:, c * BANK:(c + 1) * BANK],
                                          start=True, stop=True).then_inc(gate_mm, 1)

            over_groups(pe, body)


LEVELS = 7
CHUNKS = TOK_TILES


def phase_hgrn(nc, t, g):
    with ExitStack() as ctx:
        sb = lambda n, s, d=F32: ctx.enter_context(nc.sbuf_tensor(n, s, d))
        sem = ctx.enter_context(semaphores(nc))
        sem2 = lambda n: [sem(f"{n}{i}") for i in range(2)]
        bank = [ctx.enter_context(nc.psum_tensor(f"h_bank{i}", [P, BANK], F32)) for i in range(8)]
        W = [P, CT, P]
        v_tok = sb("v_tok", [P, CHUNKS, CH])
        s_bwd = sb("s_bwd", [P, CHUNKS + 1, CT, P])
        s_fwd = [sb(f"s_fwd{i}", W) for i in range(2)]
        decayed = sb("decayed", W)
        masks = sb("masks", [P, LEVELS, P], I32)
        xor_i = sb("xor_i", [P, 2, P], I32)
        xor_f = sb("xor_f", [P, P])
        ge = sb("ge", [P, LEVELS + 1, P])
        lbt = sb("lbt", [P, 4, CT])
        ones_row = sb("ones_row", [P, P])
        a_f = [sb(f"a_f{i}", W) for i in range(2)]
        a_v = [sb(f"a_v{i}", W) for i in range(2)]
        a_k = [sb(f"a_k{i}", W) for i in range(2)]
        a_e = [sb(f"a_e{i}", W) for i in range(2)]
        a_ktok = [sb(f"a_ktok{i}", [P, CH]) for i in range(2)]
        a_p = [sb(f"a_p{i}", [P, CT]) for i in range(2)]
        sem_names = ("f_in", "v_in", "a_sig", "a_gate", "a_keys", "a_kd", "a_ktr", "a_vtr", "a_kev", "a_vev", "a_kv")
        f_in, v_in, a_sig, a_gate, a_keys, a_kd, a_ktr, a_vtr, a_kev, a_vev, a_kv = (sem2(n) for n in sem_names)
        a_state, a_chain, zeroed, lb_done, lb_exp, mask_chain, iota_done = (
            sem("a_state"), sem("a_chain"), sem("zeroed"), sem("lb_done"), sem("lb_exp"), sem("mask_chain"), sem("iota_done"))
        passed, by_head_zero = sem("passed"), sem("by_head_zero")
        g["masks"], g["v_tok"], g["s_bwd"], g["lbt"] = masks, v_tok, s_bwd, lbt
        src = lambda group, c: t["projT"][group * CH:(group + 1) * CH, :].rearrange("(j p) n -> p j n", p=P)[:, :, ds(c, P)]

        with nc.Block() as block:
            @block.sync
            def _(q):
                def body(n, r, i):
                    c = (CHUNKS - 1) * P - n * P if isinstance(n, int) else q.snap((CHUNKS - 1) * P - n * P)
                    wait_apart(q, a_keys[r], i, passed)
                    q.dma_start(a_f[r][:], src(4, c)).then_inc(f_in[r], 16)
                    q.wait_ge(a_vtr[r], i)
                    q.dma_start(a_v[r][:], src(5, c)).then_inc(v_in[r], 16)

                pairs(q, CHUNKS, body)

            @block.gpsimd
            def _(pool):
                for x in (s_bwd[:], s_fwd[0][:], s_fwd[1][:]):
                    pool.memset(x, 0.0)
                pool.memset(ones_row[:], 1.0)
                for r in range(2):
                    last = pool.memset(a_e[r][:], 1.0)
                last.then_inc(zeroed, 1)
                pool.iota(xor_i[:, 0, :], [[0, P]], base=0, channel_multiplier=1)
                pool.iota(xor_i[:, 1, :], [[1, P]], base=0, channel_multiplier=0).then_inc(iota_done, 1)
                pool.wait_ge(lb_done, 1)
                def body(n, r, i):
                    wait_apart(pool, a_sig[r], i + 1, passed)
                    for j in range(CT):
                        last = pool.tensor_scalar(a_f[r][:, j, :], a_f[r][:, j, :], lbt[:, 3, j:j + 1], lbt[:, 2, j:j + 1],
                                                  ALU.mult, ALU.add)
                    last.then_inc(a_gate[r], 1)
                    pool.wait_ge(a_gate[r], i + 1)
                    wait_apart(pool, a_ktr[r], i, passed)
                    pool.tensor_scalar(a_k[r][:], a_f[r][:], -1.0, 1.0, ALU.mult, ALU.add).then_inc(a_kd[r], 1)

                pairs(pool, CHUNKS, body)

            @block.scalar
            def _(act):
                act.wait_ge(lb_exp, 1)
                nc.scalar.activation(lbt[:, 0, :], lbt[:, 1, :], ACT.Exp).then_inc(lb_exp, 1)

                def keys_out(n, r, i):
                    act.wait_ge(a_ktr[r], i + 1)
                    act.wait_ge(a_kv[r], i)
                    nc.scalar.activation(a_ktok[r][:], bank[r][:], ACT.Copy).then_inc(a_kev[r], 1)

                def body(n, r, i):
                    act.wait_ge(f_in[r], i * 16 + 16)
                    nc.scalar.activation(a_f[r][:], a_f[r][:], ACT.Sigmoid).then_inc(a_sig[r], 1)
                    if at_least(n, 1):
                        keys_out(n - 1, 1 - r, i - 1 + r)

                pairs(act, CHUNKS, body)
                keys_out(CHUNKS - 1, 1, CHUNKS // 2 - 1)

            @block.vector
            def _(dve):
                mc = Chain(dve, mask_chain)
                dve.wait_ge(iota_done, 1)
                mc.link(dve.tensor_tensor(xor_i[:, 0, :], xor_i[:, 0, :], xor_i[:, 1, :], ALU.bitwise_xor))
                mc.link(dve.tensor_copy(xor_f[:], xor_i[:, 0, :]))
                for l in range(LEVELS + 1):
                    last = dve.tensor_scalar(ge[:, l, :], xor_f[:], float(1 << l), None, ALU.is_ge)
                mc.link(last)
                dve.tensor_tensor(masks[:], ge[:, 0:LEVELS, :], ge[:, 1:LEVELS + 1, :], ALU.subtract)
                raw = g["cols"][:, V_LB:V_LB + CT]
                dve.tensor_tensor(lbt[:, 1, :], raw, raw, ALU.subtract).then_inc(lb_exp, 1)
                dve.wait_ge(lb_exp, 2)
                mc.link(dve.reciprocal(lbt[:, 1, :], lbt[:, 0, :]))
                mc.link(dve.tensor_tensor(lbt[:, 1, :], lbt[:, 1, :], lbt[:, 0, :], ALU.mult))
                mc.link(dve.tensor_tensor(lbt[:, 2, :], lbt[:, 1, :], lbt[:, 1, :], ALU.subtract))
                dve.tensor_scalar(lbt[:, 3, :], lbt[:, 2, :], -1.0, 1.0, ALU.mult, ALU.add).then_inc(lb_done, 1)
                dve.wait_ge(zeroed, 1)

                def keys(n, r, i):
                    c = dve.snap((CHUNKS - 1) - n) if not isinstance(n, int) else CHUNKS - 1 - n
                    dc = Chain(dve, a_chain, n * 2 - 1 if at_least(n, 1) else 0)
                    dve.wait_ge(a_gate[r], i + 1)
                    dve.wait_ge(a_keys[r], i)
                    for j in range(CT):
                        last = dve.tensor_tensor_scan(a_e[r][:, j, 1:P], a_f[r][:, j, 0:P - 1], ones_row[:, 0:P - 1], 1.0,
                                                      ALU.mult, ALU.mult)
                    dc.link(last)
                    if at_least(n, 2):
                        dve.wait_ge(a_state, n * 2 - 2)
                    dve.tensor_tensor(a_p[r][:], a_e[r][:, :, P - 1], a_f[r][:, :, P - 1], ALU.mult)
                    dve.wait_ge(a_kd[r], i + 1)
                    dve.tensor_tensor(a_k[r][:], a_k[r][:], a_e[r][:], ALU.mult).then_inc(a_keys[r], 1)
                    dve.wait_ge(a_keys[r], i + 1)
                    wait_apart(dve, a_vtr[r], i + 1, passed)
                    dve.tensor_copy(v_tok[:, ds(c, 1), :], bank[2 + r][:].unsqueeze(1)).then_inc(a_vev[r], 1)

                def state(n, r, i):
                    c = dve.snap((CHUNKS - 1) - n) if not isinstance(n, int) else CHUNKS - 1 - n
                    dc = Chain(dve, a_chain, n * 2 + 2 if not (isinstance(n, int) and n == CHUNKS - 1) else n * 2 + 1)
                    wait_apart(dve, a_state, n * 2, passed)
                    dc.link(dve.tensor_tensor(decayed[:].unsqueeze(1), s_bwd[:, ds(c + 1, 1), :, :],
                                              bcast_inner(a_p[r][:], P).unsqueeze(1), ALU.mult))
                    dve.wait_ge(a_kv[r], i + 1)
                    for half in range(2):
                        at = slice(half * HEAD, (half + 1) * HEAD)
                        kv = bank[4 + r][at, :].rearrange("p (j n) -> p j n", j=CT)[:, :, at]
                        dve.tensor_tensor(s_bwd[at, ds(c, 1), :, at], decayed[at, :, at].unsqueeze(1), kv.unsqueeze(1),
                                          ALU.add).then_inc(a_state, 1)

                def body(n, r, i):
                    keys(n, r, i)
                    if at_least(n, 1):
                        state(n - 1, 1 - r, i - 1 + r)

                pairs(dve, CHUNKS, body)
                state(CHUNKS - 1, 1, CHUNKS // 2 - 1)

            @block.tensor
            def _(pe):
                def products(n, r, i):
                    c = pe.snap((CHUNKS - 1) - n) if not isinstance(n, int) else CHUNKS - 1 - n
                    pe.wait_ge(a_vev[r], i + 1)
                    pe.wait_ge(a_state, pos(n * 2 - 2))
                    wait_apart(pe, a_kev[r], i + 1, passed)
                    for j in range(CT):
                        mm = pe.matmul(bank[4 + r][:, j * P:(j + 1) * P], a_ktok[r][:, j * P:(j + 1) * P],
                                       v_tok[:, ds(c, 1), j * P:(j + 1) * P], start=True, stop=True)
                    mm.then_inc(a_kv[r], 1)

                def body(n, r, i):
                    pe.wait_ge(v_in[r], i * 16 + 16)
                    pe.wait_ge(a_vev[r], i)
                    for j in range(CT):
                        tr = pe.transpose(bank[2 + r][:, j * P:(j + 1) * P], a_v[r][:, j, :], g["ident"][:])
                    tr.then_inc(a_vtr[r], 1)
                    pe.wait_ge(a_keys[r], i + 1)
                    pe.wait_ge(a_kev[r], i)
                    for j in range(CT):
                        tr = pe.transpose(bank[r][:, j * P:(j + 1) * P], a_k[r][:, j, :], g["ident"][:])
                    tr.then_inc(a_ktr[r], 1)
                    if at_least(n, 1):
                        products(n - 1, 1 - r, i - 1 + r)

                pairs(pe, CHUNKS, body)
                products(CHUNKS - 1, 1, CHUNKS // 2 - 1)

        names = ("q", "ff", "fb", "gate")
        inp = {n: [sb(f"b_{n}{i}", W) for i in range(2)] for n in names}
        gate_sig = sb("b_gate_sig", W)
        BY_HEAD = [P, 2, CT, P]
        first = [sb(f"{n}_first", BY_HEAD if n[0] == "q" else W) for n in ("qf", "kf", "qb", "kb")]
        mid = [[sb(f"{n}_mid{i}", BY_HEAD if n[0] == "q" else W) for i in range(2)] for n in ("qf", "kf", "qb", "kb")]
        heads = sb("heads", [P, 2])
        end = [sb(f"{n}_end", W) for n in ("qf", "kf", "qb")]
        kd = sb("k_diag", W)
        PF, PB = ([sb(f"{n}{l}", [P, CT, P >> l]) for l in range(1, LEVELS + 1)] for n in ("pf", "pb"))
        score = [sb(f"score{i}", [P, CT * 2, P]) for i in range(2)]
        ktok = sb("ktok", [P, CH])
        sq = sb("o_sq", [P, CH])
        ss, rs, rinv = sb("o_ss", [P, 8]), sb("o_rms", [P, 8]), sb("o_rinv", [P, 8])
        on = sb("o_norm", [P, CH])
        mrg = [sb(f"mrg{i}", W) for i in range(2)]
        loaded = {n: sem2(f"in_{n}") for n in names}
        mrg_out = sem2("mrg_stored")
        (sig, gsig, gate_v, gate_p, init_v, init_p, up_v, up_p, up_a, lvl, taken, ktr, kev, kvs, st, inter, o_mm, o_sqd, o_ss,
         o_rms, o_n, o_tr, mrg_done, vch, gate_done) = (sem(n) for n in (
            "b_sig", "b_gsig", "b_gate_v", "b_gate_p", "b_init_v", "b_init_p", "up_v", "up_p", "up_a", "lvl", "taken", "b_ktr",
            "b_kev", "b_kv", "b_state", "b_inter", "o_mm", "o_sqd", "o_ssd", "o_rmsd", "o_nd", "o_tr", "mrg_done", "b_vch", "b_gate_done"))
        QF, KF, QB, KB = range(4)
        L1 = LEVELS + 1

        def arr(x, l):
            return first[x] if l == 0 else end[x] if l == LEVELS else mid[x][l % 2]

        def halves(x, l):
            return x.rearrange("p j (n two a) -> p (j n) two a", two=2, a=1 << l)

        def whole(x):
            return x.rearrange("p j (n two) -> p (j n) two", two=2)

        HALVES = [slice(half * HEAD, (half + 1) * HEAD) for half in range(2)]

        def parts(x, l):
            a = arr(x, l)[:]
            if x in (KF, KB):
                return [(slice(0, P), a)]
            return [(at, a[at, half, :, :] if l < LEVELS else a[at, :, :]) for half, at in enumerate(HALVES)]

        def raise_level(op, x, l, w):
            for (at, src), (_, dst) in zip(parts(x, l), parts(x, l + 1)):
                last = op(halves(dst, l)[:, :, w, :], halves(src, l)[:, :, w, :], at)
            return last

        def target_free(eng, n, l):
            eng.wait_ge(lvl, pos(n * L1 - 1 if l == 0 else n * L1 if l == 1 else n * L1 + l + 1))
            eng.wait_ge(up_a, n * LEVELS + l)
            if l == LEVELS - 1:
                eng.wait_ge(inter, n)
                eng.wait_ge(ktr, n)

        is_first = lambda n: isinstance(n, int) and n == 0
        is_last = lambda n: isinstance(n, int) and n == CHUNKS - 1

        with nc.Block() as block:
            @block.sync
            def _(q):
                def load(name, group, c, r):
                    q.dma_start(inp[name][r][:], src(group, c)).then_inc(loaded[name][r], 16)

                def store(n, r):
                    q.wait_ge(mrg_done, n + 1)
                    q.dma_start(t["mergedT"][CH:2 * CH, :].rearrange("(j p) n -> p j n", p=P)[:, :, ds(n * P, P)],
                                mrg[r][:]).then_inc(mrg_out[r], 16)

                for name, group in (("ff", 3), ("fb", 4), ("q", 2), ("gate", 6)):
                    load(name, group, 0, 0)

                def body(n, r, i):
                    if not is_last(n):
                        wait_apart(q, lvl, n * L1, passed)
                        wait_apart(q, up_v, n * LEVELS, passed)
                        wait_apart(q, up_p, n * LEVELS, passed)
                        for name, group in (("ff", 3), ("fb", 4), ("q", 2)):
                            load(name, group, n * P + P, 1 - r)
                    if not is_first(n):
                        wait_apart(q, mrg_done, n, passed)
                        store(n - 1, 1 - r)
                    if not is_last(n):
                        load("gate", 6, n * P + P, 1 - r)

                pairs(q, CHUNKS, body)
                store(CHUNKS - 1, 1)
                for r in range(2):
                    q.wait_ge(mrg_out[r], 16 * (CHUNKS // 2))

            @block.gpsimd
            def _(pool):
                def gates(n, r):
                    b = inp["fb"][r]
                    wait_apart(pool, sig, n * 2 + 2, passed)
                    for j in range(CT):
                        last = pool.tensor_scalar(b[:, j, :], b[:, j, :], lbt[:, 3, j:j + 1], lbt[:, 2, j:j + 1], ALU.mult, ALU.add)
                    last.then_inc(gate_p, 1)

                def keys(n, r, i):
                    f, b = inp["ff"][r], inp["fb"][r]
                    pool.wait_ge(lvl, pos((n - 1) * L1 + 2))
                    pool.wait_ge(up_v, pos((n - 1) * LEVELS + 1))
                    pool.wait_ge(up_a, pos((n - 1) * LEVELS + 1))
                    pool.wait_ge(gate_v, n + 1)
                    wait_apart(pool, gate_p, n + 1, passed)
                    pool.tensor_scalar(first[KF][:], f[:], -1.0, 1.0, ALU.mult, ALU.add)
                    pool.tensor_scalar(first[KB][:], b[:], -1.0, 1.0, ALU.mult, ALU.add).then_inc(init_p, 1)
                    pool.wait_ge(init_p, n * 3 + 1)
                    pool.tensor_tensor(kd[:], first[KF][:], first[KB][:], ALU.add).then_inc(init_p, 1)
                    pool.wait_ge(init_p, n * 3 + 2)
                    pool.wait_ge(loaded["q"][r], i * 16 + 16)
                    pool.tensor_tensor(kd[:], kd[:], inp["q"][r][:], ALU.mult).then_inc(init_p, 1)

                gates(0, 0)
                keys(0, 0, 0)

                def body(n, r, i):
                    pool.wait_ge(init_p, n * 3 + 3)
                    pool.wait_ge(init_v, n + 1)
                    f, b = inp["ff"][r], inp["fb"][r]
                    for l in range(LEVELS):
                        pf, pb = whole(f[:] if l == 0 else PF[l - 1][:]), whole(b[:] if l == 0 else PB[l - 1][:])
                        target_free(pool, n, l)
                        pool.wait_ge(up_p, n * LEVELS + l)
                        pool.tensor_tensor(halves(arr(KF, l + 1)[:], l)[:, :, 0, :], halves(arr(KF, l)[:], l)[:, :, 0, :],
                                           bcast_inner(pf[:, :, 1], 1 << l), ALU.mult)
                        if l < LEVELS - 1:
                            pool.tensor_tensor(halves(arr(KB, l + 1)[:], l)[:, :, 1, :], halves(arr(KB, l)[:], l)[:, :, 1, :],
                                               bcast_inner(pb[:, :, 0], 1 << l), ALU.mult)
                            pool.tensor_tensor(PB[l][:].rearrange("p j n -> p (j n)"), pb[:, :, 0], pb[:, :, 1], ALU.mult)
                        elif not is_first(n):
                            pool.wait_ge(st, n * 2)
                        ins = pool.tensor_tensor(PF[l][:].rearrange("p j n -> p (j n)"), pf[:, :, 0], pf[:, :, 1], ALU.mult)
                        ins.then_inc(up_p, 1)
                        if l == 2 and not is_last(n):
                            gates(n + 1, 1 - r)
                        if l == 4 and not is_last(n):
                            keys(n + 1, 1 - r, i + r)
                    pool.wait_ge(gsig, n + 1)
                    pool.tensor_tensor(inp["gate"][r][:], inp["gate"][r][:], gate_sig[:], ALU.mult).then_inc(gate_done, 1)

                pairs(pool, CHUNKS, body)

            @block.scalar
            def _(act):
                def init(n, r, i):
                    for name in ("ff", "fb"):
                        act.wait_ge(loaded[name][r], i * 16 + 16)
                        nc.scalar.activation(inp[name][r][:], inp[name][r][:], ACT.Sigmoid).then_inc(sig, 1)

                def turn_keys(n):
                    act.wait_ge(ktr, n + 1)
                    act.wait_ge(kvs, n)
                    nc.scalar.activation(ktok[:], bank[5][:], ACT.Copy).then_inc(kev, 1)

                def square(n):
                    act.wait_ge(o_mm, n + 1)
                    act.wait_ge(o_ss, n)
                    nc.scalar.activation(sq[:], bank[4][:], ACT.Square).then_inc(o_sqd, 1)

                def root(n):
                    act.wait_ge(o_ss, n + 1)
                    nc.scalar.activation(rs[:], ss[:], ACT.Sqrt, bias=g["eps"][:], scale=1.0 / HEAD).then_inc(o_rms, 1)

                init(0, 0, 0)

                def body(n, r, i):
                    act.wait_ge(init_v, n + 1)
                    act.wait_ge(init_p, n * 3 + 3)
                    for l in range(LEVELS):
                        target_free(act, n, l)
                        act.wait_ge(up_v, n * LEVELS + l)
                        act.wait_ge(up_p, n * LEVELS + l)
                        for x, h in ((QF, 0), (KF, 1), (QB, 1), (KB, 0)):
                            if x == KB and l == LEVELS - 1:
                                continue
                            last = raise_level(lambda dst, src, at: nc.scalar.activation(dst, src, ACT.Copy), x, l, h)
                        last.then_inc(up_a, 1)
                        if not is_first(n):
                            if l == 1:
                                turn_keys(n - 1)
                            if l == 2:
                                square(n - 1)
                            if l == 4:
                                root(n - 1)
                        if l == 2:
                            if not is_last(n):
                                init(n + 1, 1 - r, i + r)
                            act.wait_ge(loaded["gate"][r], i * 16 + 16)
                            if not is_first(n):
                                act.wait_ge(gate_done, n)
                            nc.scalar.activation(gate_sig[:], inp["gate"][r][:], ACT.Sigmoid).then_inc(gsig, 1)

                pairs(act, CHUNKS, body)
                n = CHUNKS - 1
                square(n)
                root(n)

            @block.vector
            def _(dve):
                def init_gate(n, r):
                    f = inp["ff"][r]
                    dve.wait_ge(sig, n * 2 + 1)
                    for j in range(CT):
                        last = dve.tensor_scalar(f[:, j, :], f[:, j, :], lbt[:, 3, j:j + 1], lbt[:, 2, j:j + 1], ALU.mult, ALU.add)
                    last.then_inc(gate_v, 1)

                def init_queries(n, r, i):
                    dve.wait_ge(gate_v, n + 1)
                    dve.wait_ge(loaded["q"][r], i * 16 + 16)
                    dve.wait_ge(lvl, pos((n - 1) * L1 + 2))
                    dve.wait_ge(up_a, pos((n - 1) * LEVELS + 1))
                    dve.wait_ge(gate_p, n + 1)
                    for x, gate in ((QF, "ff"), (QB, "fb")):
                        for half, at in enumerate(HALVES):
                            last = dve.tensor_tensor(first[x][at, half, :, :], inp["q"][r][at, :, :], inp[gate][r][at, :, :],
                                                     ALU.mult)
                    last.then_inc(init_v, 1)

                def take(n, r, l):
                    base = n * L1 + l + 2
                    if l < 0:
                        dve.wait_ge(o_mm, pos(n - 1))
                    dve.wait_ge(taken, base - 1)
                    wait_apart(dve, lvl, base, passed)
                    if l < 0:
                        ins = dve.tensor_tensor(score[r][:], g["ident"][:].unsqueeze(1).to_broadcast([P, 2 * CT, P]),
                                                bcast_inner(bank[0][:, 0:2 * CT], P), ALU.mult)
                    else:
                        for two in range(2):
                            ins = dve.copy_predicated(score[r][:, two * CT:(two + 1) * CT, :],
                                                      masks[:, l, :].unsqueeze(1).to_broadcast([P, CT, P]),
                                                      bank[2 * ((l + 1) % 2) + two][:].rearrange("p (j n) -> p j n", j=CT))
                    ins.then_inc(taken, 1)

                def head_sums(n):
                    dve.wait_ge(o_sqd, n + 1)
                    dve.wait_ge(o_rms, n)
                    dve.tensor_reduce(ss[:], sq[:].rearrange("p (h e) -> p h e", e=HEAD), AX, ALU.add).then_inc(o_ss, 1)

                def state(n, r):
                    dc = Chain(dve, vch, n * 2)
                    dve.wait_ge(up_p, (n + 1) * LEVELS)
                    dve.wait_ge(st, n * 2)
                    dc.link(dve.tensor_tensor(decayed[:], s_fwd[r][:], bcast_inner(PF[LEVELS - 1][:, :, 0], P), ALU.mult))
                    dve.wait_ge(kvs, n + 1)
                    dve.wait_ge(inter, n)
                    for half in range(2):
                        at = slice(half * HEAD, (half + 1) * HEAD)
                        kv = bank[6][at, :].rearrange("p (j n) -> p j n", j=CT)[:, :, at]
                        dve.tensor_tensor(s_fwd[1 - r][at, :, at], decayed[at, :, at], kv, ALU.add).then_inc(st, 1)

                def normalise(n, links):
                    dc = Chain(dve, vch, links)
                    dve.wait_ge(o_rms, n + 1)
                    dc.link(dve.reciprocal(rinv[:], rs[:]))
                    dve.wait_ge(o_tr, n)
                    dve.tensor_tensor(on[:].rearrange("p (h e) -> p h e", e=HEAD), bank[4][:].rearrange("p (h e) -> p h e", e=HEAD),
                                      bcast_inner(rinv[:], HEAD), ALU.mult).then_inc(o_n, 1)

                def merge(n, r, i):
                    dve.wait_ge(o_tr, n + 1)
                    dve.wait_ge(gate_done, n + 1)
                    dve.wait_ge(mrg_out[r], i * 16)
                    dve.tensor_tensor(mrg[r][:], bank[7][:].rearrange("p (j n) -> p j n", j=CT), inp["gate"][r][:],
                                      ALU.mult).then_inc(mrg_done, 1)

                for x in (QF, QB):
                    for a in (first[x], *mid[x]):
                        for half, at in enumerate(HALVES):
                            dve.memset(a[at, 1 - half, :, :], 0.0)
                dve.memset(heads[0:HEAD, 0:1], 1.0)
                dve.memset(heads[HEAD:P, 0:1], 0.0)
                dve.memset(heads[0:HEAD, 1:2], 0.0)
                dve.memset(heads[HEAD:P, 1:2], 1.0).then_inc(by_head_zero, 1)
                init_gate(0, 0)
                init_queries(0, 0, 0)

                def body(n, r, i):
                    f, b = inp["ff"][r], inp["fb"][r]
                    dve.wait_ge(init_v, n + 1)
                    for l in range(LEVELS):
                        pf, pb = whole(f[:] if l == 0 else PF[l - 1][:]), whole(b[:] if l == 0 else PB[l - 1][:])
                        target_free(dve, n, l)
                        dve.wait_ge(up_v, n * LEVELS + l)
                        dve.wait_ge(up_p, n * LEVELS + l)
                        raise_level(lambda dst, src, at: dve.tensor_tensor(
                            dst, src, bcast_inner(pf[at, :, 0], 1 << l), ALU.mult), QF, l, 1)
                        raise_level(lambda dst, src, at: dve.tensor_tensor(
                            dst, src, bcast_inner(pb[at, :, 1], 1 << l), ALU.mult), QB, l, 0).then_inc(up_v, 1)
                        take(n, r, l - 1)
                        if not is_first(n):
                            if l == 2:
                                head_sums(n - 1)
                            if l == 3:
                                state(n - 1, 1 - r)
                            if l == 5:
                                normalise(n - 1, n * 2 - 1)
                            if l == 6:
                                merge(n - 1, 1 - r, i - 1 + r)
                        if not is_last(n):
                            if l == 3:
                                init_gate(n + 1, 1 - r)
                            if l == 5:
                                init_queries(n + 1, 1 - r, i + r)
                    take(n, r, LEVELS - 1)

                pairs(dve, CHUNKS, body)
                n = CHUNKS - 1
                head_sums(n)
                normalise(n, n * 2)
                merge(n, 1, CHUNKS // 2 - 1)

            @block.tensor
            def _(pe):
                def products(n, r, l):
                    if l >= 1:
                        pe.wait_ge(up_v, n * LEVELS + l)
                        pe.wait_ge(up_p, n * LEVELS + l)
                        pe.wait_ge(up_a, n * LEVELS + l)
                    pe.wait_ge(taken, pos(n * L1 + l))
                    for j in range(CT):
                        if l < 0:
                            mm = pe.matmul(bank[0][:, 2 * j:2 * j + 2], kd[:, j, :], heads[:], start=True, stop=True)
                            continue
                        out = bank[2 * ((l + 1) % 2) + j // 2][:, (j % 2) * 2 * P:(j % 2 + 1) * 2 * P]
                        for keys, queries, w in ((KF, QF, 1), (KB, QB, 0)):
                            mm = pe.matmul(out.rearrange("p (h n two a) -> p h n two a", h=2, two=2, a=1 << l)[:, :, :, w, :],
                                           arr(keys, l)[:, j, :],
                                           arr(queries, l)[:, :, j, :].rearrange("p h (n two a) -> p h n two a", two=2,
                                                                                 a=1 << l)[:, :, :, w, :],
                                           start=True, stop=True)
                    mm.then_inc(lvl, 1)

                def across(n, r):
                    pe.wait_ge(up_v, (n + 1) * LEVELS)
                    pe.wait_ge(up_p, (n + 1) * LEVELS)
                    pe.wait_ge(up_a, (n + 1) * LEVELS)
                    pe.wait_ge(kev, n)
                    for j in range(CT):
                        tr = pe.transpose(bank[5][:, j * P:(j + 1) * P], end[KF][:, j, :], g["ident"][:])
                    tr.then_inc(ktr, 1)
                    pe.wait_ge(o_n, n)
                    wait_apart(pe, st, n * 2, passed)
                    for j in range(CT):
                        at = slice(j * P, (j + 1) * P)
                        pe.matmul(bank[4][:, at], end[QF][:, j, :], s_fwd[r][:, j, :], start=(j == 0), stop=False,
                                  skip_group_check=True)
                        mm = pe.matmul(bank[4][:, at], end[QB][:, j, :], s_bwd[:, ds(n + 1, 1), j, :], start=False, stop=False,
                                       skip_group_check=True)
                    mm.then_inc(inter, 1)

                def within(n, r):
                    pe.wait_ge(taken, (n + 1) * L1)
                    for j in range(CT):
                        for half in range(2):
                            at = slice(j * P + half * HEAD, j * P + (half + 1) * HEAD)
                            mm = pe.matmul(bank[4][:, at], score[r][:, 2 * j + half, :], v_tok[:, ds(n, 1), at], start=False,
                                           stop=(j == CT - 1 and half == 1), skip_group_check=True)
                    mm.then_inc(o_mm, 1)

                def keys_values(n):
                    pe.wait_ge(kev, n + 1)
                    pe.wait_ge(st, n * 2)
                    for j in range(CT):
                        mm = pe.matmul(bank[6][:, j * P:(j + 1) * P], ktok[:, j * P:(j + 1) * P],
                                       v_tok[:, ds(n, 1), j * P:(j + 1) * P], start=True, stop=True)
                    mm.then_inc(kvs, 1)

                def turn_back(n):
                    pe.wait_ge(o_n, n + 1)
                    pe.wait_ge(mrg_done, n)
                    for j in range(CT):
                        tr = pe.transpose(bank[7][:, j * P:(j + 1) * P], on[:, j * P:(j + 1) * P], g["ident"][:])
                    tr.then_inc(o_tr, 1)

                def body(n, r, i):
                    pe.wait_ge(init_v, n + 1)
                    pe.wait_ge(init_p, n * 3 + 3)
                    for l in range(-1, LEVELS):
                        products(n, r, l)
                        if not is_first(n):
                            if l == 0:
                                across(n - 1, 1 - r)
                            if l == 1:
                                within(n - 1, 1 - r)
                            if l == 2:
                                keys_values(n - 1)
                            if l == 6:
                                turn_back(n - 1)

                pe.wait_ge(by_head_zero, 1)
                pairs(pe, CHUNKS, body)
                n = CHUNKS - 1
                across(n, 1)
                within(n, 1)
                turn_back(n)


def phase_output(nc, t, g):
    with ExitStack() as ctx:
        sb = lambda n, s, d=F32: ctx.enter_context(nc.sbuf_tensor(n, s, d))
        sem = ctx.enter_context(semaphores(nc))
        sem2 = lambda n: [sem(f"{n}{i}") for i in range(2)]
        lru_ps = ctx.enter_context(nc.psum_tensor("lru_ps", [P, D], F32))
        hg_ps = ctx.enter_context(nc.psum_tensor("hg_ps", [P, D], F32))
        tr_ps = ctx.enter_context(nc.psum_tensor("tr_ps", [P, D], F32))
        sum_ps = ctx.enter_context(nc.psum_tensor("sum_ps", [P, BANK], F32))
        rt_ps = ctx.enter_context(nc.psum_tensor("rt_ps", [P, BANK], F32))
        wo = sb("wo", [P, KD, D])
        wo_hi, wo_lo = sb("wo_hi", [P, KD, D], F32R), sb("wo_lo", [P, KD, D], F32R)
        m_hi, m_lo = ([sb(f"merged_{part}{i}", [P, KD, P], F32R) for i in range(2)] for part in ("hi", "lo"))
        wr = sb("wr", [P, KD, ROUTES])
        wrs = sb("wrs", [P, KD, ROUTES])
        bias = sb("route_bias_all", [1, ROUTES])
        m = [sb(f"merged{i}", [P, KD, P]) for i in range(2)]
        xr = [sb(f"x_row{i}", [P, D]) for i in range(2)]
        x2 = [sb(f"x2_{i}", [P, D]) for i in range(2)]
        xh = [sb(f"xh_{i}", [P, D]) for i in range(2)]
        sq = [sb(f"lru_sq{i}", [P, CT, P]) for i in range(2)]
        junk = [sb(f"x2_sq{i}", [P, D]) for i in range(2)]
        xt = [sb(f"xh_t{i}", [P, KD, P]) for i in range(2)]
        st = [sb(f"stat{i}", [P, 8]) for i in range(2)]
        wo_in, wr_in, wo_done, wr_done, bias_ps, bias_done = (sem(n) for n in (
            "wo_in", "wr_in", "wo_done", "wr_done", "bias_ps", "bias_done"))
        m_in, xr_in, x2_out, xh_out = sem2("m_in"), sem2("xr_in"), sem2("x2_out"), sem2("xh_out")
        sq_done, sum_mm, lru_rms, lru_r, y_mm, acc, x2_done, x2_sq, x2_rms, x2_r, xh_done, xt_mm, xt_done, rt_mm, lg = (
            sem(n) for n in ("sq_d", "sum_mm", "lru_rms", "lru_r", "y_mm", "acc", "x2_done", "x2_sqd", "x2_rms", "x2_r",
                             "xh_done", "xt_mm", "xt_done", "rt_mm", "lg"))
        lru_mm, passed = sem("lru_mm"), sem("o_passed")
        wo_in2, wo_hi_done, wo_split, m_hi_done, m_split = (sem(n) for n in ("wo_in2", "wo_hi_done", "wo_split", "m_hi_done", "m_split"))
        block = ctx.enter_context(nc.Block())

        @block.sync
        def _(q):
            for k, done in ((slice(0, CT), wo_in), (slice(CT, KD), wo_in2)):
                q.dma_start(wo[:, k, :], t["w_out"][0].rearrange("(k p) n -> p k n", p=P)[:, k, :]).then_inc(done, 16)
            q.dma_start(wr[:, :, 0:N_GROUPS], t["router_group_w"][0].rearrange("(k p) n -> p k n", p=P)).then_inc(wr_in, 16)
            q.dma_start(wr[:, :, N_GROUPS:ROUTES], t["router_expert_w"][0].rearrange("(k p) n -> p k n", p=P)).then_inc(wr_in, 16)

            def load(n, r):
                wait_apart(q, m_split, pos(n - 1), passed)
                wait_apart(q, x2_done, pos(n - 1), passed)
                q.dma_start(m[r][:], t["mergedT"].rearrange("(k p) n -> p k n", p=P)[:, :, ds(n * P, P)]).then_inc(m_in[r], 16)
                q.dma_start(xr[r][:], t["x"][0][ds(n * P, P), :]).then_inc(xr_in[r], 16)

            def store(n, r):
                wait_apart(q, x2_done, n + 1, passed)
                q.dma_start(t["x2"][ds(n * P, P), :], x2[r][:]).then_inc(x2_out[r], 16)
                wait_apart(q, xh_done, n + 1, passed)
                q.dma_start(t["xh"][ds(n * P, P), :], xh[r][:]).then_inc(xh_out[r], 16)

            def body(n, r, i):
                load(n, r)
                if not (isinstance(n, int) and n == 0):
                    store(n - 1, 1 - r)

            pairs(q, TOK_TILES, body)
            store(TOK_TILES - 1, 1)
            for s in (*x2_out, *xh_out):
                q.wait_ge(s, 16 * (TOK_TILES // 2))

        @block.gpsimd
        def _(pool):
            def body(n, r, i):
                wait_apart(pool, m_in[r], i * 16 + 16, passed)
                pool.wait_ge(sum_mm, pos(n - 1))
                pool.tensor_tensor(sq[r][:], m[r][:, 0:CT, :], m[r][:, 0:CT, :], ALU.mult).then_inc(sq_done, 1)
                wait_apart(pool, y_mm, pos(n - 1), passed)
                pool.tensor_copy(m_hi[r][:], m[r][:]).then_inc(m_hi_done, 1)
                wait_apart(pool, m_hi_done, n + 1, passed)
                pool.tensor_tensor(m_lo[r][:], m[r][:], m_hi[r][:].bitcast(F32), ALU.subtract).then_inc(m_split, 1)

            pairs(pool, TOK_TILES, body)

        @block.scalar
        def _(act):
            for k in range(KD):
                act.wait_ge(wo_done, k + 1)
                nc.scalar.activation(wo_hi[:, k, :], wo[:, k, :], ACT.Copy).then_inc(wo_hi_done, 1)

            def turned(n, r):
                act.wait_ge(xt_mm, n + 1)
                act.wait_ge(rt_mm, pos(n - 1))
                nc.scalar.activation(xt[r][:].rearrange("p k n -> p (k n)"), tr_ps[:], ACT.Copy).then_inc(xt_done, 1)

            def body(n, r, i):
                act.wait_ge(sum_mm, n + 1)
                nc.scalar.activation(st[r][:, 0:1], sum_ps[:, 0:1], ACT.Sqrt, bias=g["eps"][:], scale=1.0 / CH).then_inc(lru_rms, 1)
                if not (isinstance(n, int) and n == 0):
                    turned(n - 1, 1 - r)
                act.wait_ge(x2_done, n + 1)
                nc.scalar.activation(junk[r][:], x2[r][:], ACT.Square, accum_out=st[r][:, 2:3]).then_inc(x2_sq, 1)
                act.wait_ge(x2_sq, n + 1)
                nc.scalar.activation(st[r][:, 3:4], st[r][:, 2:3], ACT.Sqrt, bias=g["eps"][:], scale=1.0 / D).then_inc(x2_rms, 1)

            pairs(act, TOK_TILES, body)
            turned(TOK_TILES - 1, 1)

        @block.vector
        def _(dve):
            for k in range(KD):
                dve.wait_ge(wo_in if k < CT else wo_in2, 16)
                at = (V_NORM_LRU + k) if k < CT else (V_NORM_HG + k - CT)
                dve.scalar_tensor_tensor(out=wo[:, k, :], in0=wo[:, k, :], scalar=g["cols"][:, at:at + 1],
                                               in1=g["gates"][:, 0, :], op0=ALU.mult, op1=ALU.mult).then_inc(wo_done, 1)
            for k in range(KD):
                dve.wait_ge(wo_hi_done, k + 1)
                dve.tensor_tensor(wo_lo[:, k, :], wo[:, k, :], wo_hi[:, k, :].bitcast(F32), ALU.subtract).then_inc(wo_split, 1)
            dve.wait_ge(wr_in, 32)
            dve.tensor_tensor(wrs[:], wr[:], bcast_inner(g["scale_ffn"][:], ROUTES), ALU.mult).then_inc(wr_done, 1)
            dve.wait_ge(bias_ps, 1)
            dve.tensor_tensor(bias[:], rt_ps[0:1, 0:ROUTES], g["route_bias"][:], ALU.add).then_inc(bias_done, 1)

            def logits(n):
                dve.wait_ge(rt_mm, n + 1)
                dve.tensor_copy(g["logits"][:, ds(n, 1), :], rt_ps[:, 0:ROUTES].unsqueeze(1)).then_inc(lg, 1)

            def body(n, r, i):
                dve.wait_ge(lru_rms, n + 1)
                dve.reciprocal(st[r][:, 1:2], st[r][:, 0:1]).then_inc(lru_r, 1)
                dve.wait_ge(lru_mm, n + 1)
                dve.wait_ge(lru_r, n + 1)
                dve.wait_ge(xr_in[r], i * 16 + 16)
                dve.wait_ge(x2_out[r], i * 16)
                dve.scalar_tensor_tensor(out=x2[r][:], in0=lru_ps[:], scalar=st[r][:, 1:2], in1=xr[r][:],
                                         op0=ALU.mult, op1=ALU.add).then_inc(acc, 1)
                dve.wait_ge(y_mm, n + 1)
                dve.wait_ge(acc, n + 1)
                dve.tensor_tensor(x2[r][:], x2[r][:], hg_ps[:], ALU.add).then_inc(x2_done, 1)
                dve.wait_ge(x2_rms, n + 1)
                dve.reciprocal(st[r][:, 4:5], st[r][:, 3:4]).then_inc(x2_r, 1)
                dve.wait_ge(x2_r, n + 1)
                dve.wait_ge(xh_out[r], i * 16)
                dve.wait_ge(xt_mm, pos(n - 1))
                dve.tensor_scalar(xh[r][:], x2[r][:], st[r][:, 4:5], None, ALU.mult).then_inc(xh_done, 1)
                if not (isinstance(n, int) and n == 0):
                    logits(n - 1)

            pairs(dve, TOK_TILES, body)
            logits(TOK_TILES - 1)

        @block.tensor
        def _(pe):
            pe.wait_ge(wr_in, 32)
            for k in range(KD):
                mm = pe.matmul(rt_ps[0:1, 0:ROUTES], g["shift_ffn"][:, k:k + 1], wr[:, k, :], start=(k == 0), stop=(k == KD - 1))
            mm.then_inc(bias_ps, 1)

            def turn(n, r):
                pe.wait_ge(xh_done, n + 1)
                pe.wait_ge(xt_done, n)
                for k in range(KD):
                    tr = pe.transpose(tr_ps[:, k * P:(k + 1) * P], xh[r][:, k * P:(k + 1) * P], g["ident"][:])
                tr.then_inc(xt_mm, 1)

            def route(n, r):
                pe.wait_ge(xt_done, n + 1)
                pe.wait_ge(lg, n)
                for k in range(KD):
                    pe.matmul(rt_ps[:, 0:ROUTES], xt[r][:, k, :], wrs[:, k, :], start=(k == 0), stop=False)
                pe.matmul(rt_ps[:, 0:ROUTES], g["ones"][0:1, :], bias[:], start=False, stop=True).then_inc(rt_mm, 1)

            def products(n, r, ps, first):
                for k in range(first, first + CT):
                    if isinstance(n, int) and n == 0:
                        pe.wait_ge(wo_split, k + 1)
                    for a, b in ((m_hi, wo_hi), (m_hi, wo_lo), (m_lo, wo_hi)):
                        for h in range(2):
                            mm = pe.matmul(ps[:, h * BANK:(h + 1) * BANK], a[r][:, k, :], b[:, k, h * BANK:(h + 1) * BANK],
                                           start=(k == first and a is m_hi and b is wo_hi),
                                           stop=(k == first + CT - 1 and a is m_lo), skip_group_check=True)
                return mm

            pe.wait_ge(wr_done, 1)
            pe.wait_ge(bias_done, 1)

            def body(n, r, i):
                is_first = isinstance(n, int) and n == 0
                pe.wait_ge(sq_done, n + 1)
                pe.wait_ge(lru_rms, n)
                for k in range(CT):
                    mm = pe.matmul(sum_ps[:, 0:1], sq[r][:, k, :], g["ones"][:, 0:1], start=(k == 0), stop=(k == CT - 1))
                mm.then_inc(sum_mm, 1)
                pe.wait_ge(acc, n)
                pe.wait_ge(m_split, n + 1)
                products(n, r, lru_ps, 0).then_inc(lru_mm, 1)
                if not is_first:
                    turn(n - 1, 1 - r)
                pe.wait_ge(x2_done, n)
                products(n, r, hg_ps, CT).then_inc(y_mm, 1)
                if not is_first:
                    route(n - 1, 1 - r)

            pairs(pe, TOK_TILES, body)
            turn(TOK_TILES - 1, 1)
            route(TOK_TILES - 1, 1)


def phase_route(nc, t, g):
    J = ASSIGN // 2 // P
    with ExitStack() as ctx:
        sb = lambda n, s, d=F32: ctx.enter_context(nc.sbuf_tensor(n, s, d))
        sem = ctx.enter_context(semaphores(nc))
        pos_ps = ctx.enter_context(nc.psum_tensor("pos_ps", [P, TOK_TILES, EXPERTS], F32))
        cnt_ps = ctx.enter_context(nc.psum_tensor("cnt_ps", [P, BANK], F32))
        T_, lg = TOK_TILES, g["logits"]
        g8 = sb("g8", [P, T_, 8])
        gm, em = sb("gm", [P, T_, 8]), sb("em", [P, T_, 8])
        gi, ei = sb("gi", [P, T_, 8], U32), sb("ei", [P, T_, 8], U32)
        gif, eif = sb("gif", [P, T_]), sb("eif", [P, T_, 2])
        ohg = sb("ohg", [P, T_, N_GROUPS])
        neg = sb("neg", [P, T_, N_GROUPS])
        ge_ = sb("g_exp", [P, T_, N_GROUPS])
        pg, dd, one_p = sb("p_group", [P, T_]), sb("top_gap", [P, T_]), sb("one_plus", [P, T_])
        el = sb("el", [P, T_, EXPERTS])
        oh = [sb(f"oh{k}", [P, T_, EXPERTS]) for k in range(2)]
        both = sb("both", [P, T_, EXPERTS])
        pre = sb("pre", [P, T_ + 1, EXPERTS])
        tri = sb("tri", [P, P])
        iota32, iotaJ, iotaW = sb("iota32", [P, EXPERTS]), sb("iotaJ", [P, J]), sb("iotaW", [P, WINDOWS + 3])
        over = sb("over", [P, EXPERTS, J])
        nwin, pend, start = sb("nwin", [P, EXPERTS]), sb("pend", [P, EXPERTS]), sb("start_row", [P, EXPERTS])
        pos, picked, dest_f = sb("pos", [P, T_, EXPERTS]), sb("picked", [P, T_, EXPERTS]), sb("dest_f", [P, T_])
        wle, table = sb("wle", [1, WINDOWS + 3, EXPERTS]), sb("table", [1, 4, WINDOWS + 3])
        live = sb("live", [1, WINDOWS + 3])
        zero_i = sb("zero_i", [P, WINDOWS + 3], I32)
        cst, chain, tri_set, gexp, texp, both_done, pos_mm, zero_in = (sem(n) for n in (
            "r_consts", "r_chain", "tri_set", "g_expd", "t_expd", "both_done", "pos_mm", "zero_stored"))
        block = ctx.enter_context(nc.Block())

        @block.gpsimd
        def _(pool):
            pool.iota(iota32[:], [[1, EXPERTS]], base=0, channel_multiplier=0, allow_small_or_imprecise_dtypes=True)
            pool.iota(iotaJ[:], [[P, J]], base=0, channel_multiplier=0, allow_small_or_imprecise_dtypes=True)
            pool.iota(iotaW[:], [[1, WINDOWS + 3]], base=0, channel_multiplier=0, allow_small_or_imprecise_dtypes=True)
            pool.iota(g["token"][:], [[P, T_]], base=0, channel_multiplier=1)
            pool.memset(zero_i[:], 0)
            pool.memset(g8[:], -3.0e38)
            pool.memset(pre[:, 0, :], 0.0)
            pool.memset(tri[:], 1.0).then_inc(tri_set, 1)
            pool.wait_ge(tri_set, 1)
            pool.affine_select(out=tri[:], in_=tri[:], compare_op=ALU.is_gt, fill=0.0, base=0, pattern=[[1, P]],
                               channel_multiplier=-1).then_inc(cst, 1)
            pool.wait_ge(cst, 1)
            pool.dma_start(t["slot_tok"].rearrange("(p w) a -> p (w a)", p=P), zero_i[:]).then_inc(zero_in, 16)
            pool.wait_ge(zero_in, 16)

        @block.scalar
        def _(act):
            act.wait_ge(gexp, 1)
            nc.scalar.activation(ge_[:], ge_[:], ACT.Exp).then_inc(gexp, 1)
            act.wait_ge(texp, 1)
            nc.scalar.activation(dd[:], dd[:], ACT.Exp).then_inc(texp, 1)

        @block.vector
        def _(dve):
            c = Chain(dve, chain)
            dve.wait_ge(cst, 1)
            c.link(dve.tensor_copy(g8[:, :, 0:N_GROUPS], lg[:, :, 0:N_GROUPS]))
            for i in range(T_):
                last = dve.max(gm[:, i, :], g8[:, i, :])
            c.link(last)
            for i in range(T_):
                last = dve.max_index(gi[:, i, :], gm[:, i, :], g8[:, i, :])
            c.link(last)
            c.link(dve.tensor_copy(gif[:], gi[:, :, 0]))
            c.link(dve.tensor_tensor(ohg[:], iota32[:, 0:N_GROUPS].unsqueeze(1).to_broadcast([P, T_, N_GROUPS]),
                                     bcast_inner(gif[:], N_GROUPS), ALU.is_equal))
            dve.tensor_tensor(ge_[:], lg[:, :, 0:N_GROUPS], bcast_inner(gm[:, :, 0], N_GROUPS), ALU.subtract).then_inc(gexp, 1)
            dve.wait_ge(gexp, 2)
            c.link(dve.tensor_reduce(pg[:], ge_[:], AX, ALU.add))
            c.link(dve.tensor_scalar(neg[:], ohg[:], -1.0, 3.0e38, ALU.add, ALU.mult))
            e4 = lambda x: x.rearrange("p t (g e) -> p t g e", g=N_GROUPS)
            c.link(dve.tensor_tensor(e4(el[:]), e4(lg[:, :, N_GROUPS:ROUTES]), bcast_inner(ohg[:], EPG), ALU.mult))
            c.link(dve.tensor_tensor(e4(el[:]), e4(el[:]), bcast_inner(neg[:], EPG), ALU.add))
            for i in range(T_):
                last = dve.max(em[:, i, :], el[:, i, :])
            c.link(last)
            for i in range(T_):
                last = dve.max_index(ei[:, i, :], em[:, i, :], el[:, i, :])
            c.link(last)
            c.link(dve.tensor_copy(eif[:], ei[:, :, 0:2]))
            dve.tensor_tensor(dd[:], em[:, :, 1], em[:, :, 0], ALU.subtract).then_inc(texp, 1)
            dve.wait_ge(texp, 2)
            c.link(dve.tensor_scalar(one_p[:], dd[:], 1.0, None, ALU.add))
            c.link(dve.tensor_tensor(one_p[:], one_p[:], pg[:], ALU.mult))
            c.link(dve.reciprocal(g["weight"][0][:], one_p[:]))
            dve.tensor_tensor(g["weight"][1][:], g["weight"][0][:], dd[:], ALU.mult)
            for k in range(2):
                last = dve.tensor_tensor(oh[k][:], iota32[:].unsqueeze(1).to_broadcast([P, T_, EXPERTS]),
                                         bcast_inner(eif[:, :, k], EXPERTS), ALU.is_equal)
            c.link(last)
            c.link(dve.tensor_tensor(both[:], oh[0][:], oh[1][:], ALU.add))
            for i in range(T_):
                ins = dve.tensor_tensor(pre[:, i + 1, :], pre[:, i, :], both[:, i, :], ALU.add)
                if i < T_ - 1:
                    c.link(ins)
                else:
                    ins.then_inc(both_done, 1)
            dve.wait_ge(pos_mm, 1)
            c.link(dve.tensor_tensor(over[:], bcast_inner(cnt_ps[:, 0:EXPERTS], J),
                                     iotaJ[:].unsqueeze(1).to_broadcast([P, EXPERTS, J]), ALU.is_gt))
            c.link(dve.tensor_reduce(nwin[:], over[:], AX, ALU.add))
            c.link(dve.tensor_tensor_scan(pend[:], g["ones"][:, 0:EXPERTS], nwin[:], 0.0, ALU.mult, ALU.add))
            c.link(dve.tensor_tensor(start[:], pend[:], nwin[:], ALU.subtract))
            c.link(dve.tensor_scalar(start[:], start[:], float(P), None, ALU.mult))
            c.link(dve.tensor_tensor(pos[:], pos_ps[:], start[:].unsqueeze(1).to_broadcast([P, T_, EXPERTS]), ALU.add))
            for k in range(2):
                c.link(dve.tensor_tensor(picked[:], pos[:], oh[k][:], ALU.mult))
                c.link(dve.tensor_reduce(dest_f[:], picked[:], AX, ALU.add))
                c.link(dve.tensor_copy(g["dest"][k][:], dest_f[:]))
            dve.wait_ge(chain, c.n)
            c.link(dve.tensor_tensor(wle[:], pend[0:1, :].unsqueeze(1).to_broadcast([1, WINDOWS + 3, EXPERTS]),
                                     bcast_inner(iotaW[0:1, :], EXPERTS), ALU.is_le))
            c.link(dve.tensor_reduce(table[:, W_EXPERT, :], wle[:], AX, ALU.add))
            c.link(dve.tensor_scalar(table[:, W_EXPERT, :], table[:, W_EXPERT, :], float(EXPERTS - 1), None, ALU.min))
            dve.tensor_scalar(live[:], iotaW[0:1, :], pend[0:1, EXPERTS - 1:EXPERTS], None, ALU.is_lt)
            dve.memset(table[:, W_NEW, 0:1], 1.0)
            c.link(dve.tensor_tensor(table[:, W_NEW, 1:], table[:, W_EXPERT, 1:], table[:, W_EXPERT, 0:WINDOWS + 2], ALU.not_equal))
            c.link(dve.tensor_tensor(table[:, W_NEW, :], table[:, W_NEW, :], live[:], ALU.mult))
            c.link(dve.tensor_tensor_scan(table[:, W_COUNT, :], g["ones"][0:1, 0:WINDOWS + 3], table[:, W_NEW, :], 0.0,
                                          ALU.mult, ALU.add))
            c.link(dve.tensor_scalar(table[:, W_BEFORE, :], table[:, W_COUNT, :], -1.0, None, ALU.add))
            c.link(dve.tensor_scalar(table[:, W_NEW, WINDOWS + 2:], pend[0:1, EXPERTS - 1:EXPERTS], -2.0, None, ALU.add))
            c.link(dve.tensor_scalar(table[:, W_EXPERT, WINDOWS + 2:], pend[0:1, EXPERTS - 1:EXPERTS], -1.0, None, ALU.add))
            dve.tensor_copy(g["window"][:], table[:])

        @block.tensor
        def _(pe):
            pe.wait_ge(both_done, 1)
            pe.matmul(pos_ps[:].rearrange("p t e -> p (t e)"), tri[:], both[:].rearrange("p t e -> p (t e)"), start=True, stop=False)
            pe.matmul(pos_ps[:].rearrange("p t e -> p (t e)"), g["ones"][:],
                      pre[:, 0:T_, :].rearrange("p t e -> p (t e)"), start=False, stop=True)
            pe.matmul(cnt_ps[:, 0:EXPERTS], g["ones"][:], pre[:, T_, :], start=True, stop=True).then_inc(pos_mm, 1)


def phase_experts(nc, t, g):
    with ExitStack() as ctx:
        sb = lambda n, s, d=F32: ctx.enter_context(nc.sbuf_tensor(n, s, d))
        sem = ctx.enter_context(semaphores(nc))
        FT = F_EXP // P
        GU, DN = KD // 2, FT // 2
        PIECES = GU + DN
        EARLY = GU // 2
        xt_ps = ctx.enter_context(nc.psum_tensor("e_xt_ps", [P, D], F32))
        gate_ps = ctx.enter_context(nc.psum_tensor("e_gate_ps", [P, BANK], F32))
        up_ps = ctx.enter_context(nc.psum_tensor("e_up_ps", [P, BANK], F32))
        at_ps = ctx.enter_context(nc.psum_tensor("e_at_ps", [P, BANK], F32))
        y_ps = ctx.enter_context(nc.psum_tensor("e_y_ps", [P, D], F32))
        raw = [sb(f"e_raw{p}", [P, 2, D]) for p in range(PIECES)]
        w_hi = [sb(f"e_w_hi{p}", [P, 2, D], F32R) for p in range(PIECES)]
        w_lo = [sb(f"e_w_lo{p}", [P, 2, D], F32R) for p in range(PIECES)]
        idx = [sb(f"e_idx{r}", [P, 1], I32) for r in range(2)]
        xrow = [sb(f"e_xrow{r}", [P, D]) for r in range(2)]
        xt = sb("e_xt", [P, KD, P])
        x_hi = sb("e_x_hi", [P, KD, P], F32R)
        x_lo = sb("e_x_lo", [P, KD, P], F32R)
        sg = sb("e_sg", [P, F_EXP])
        prod = sb("e_prod", [P, F_EXP])
        p_hi = sb("e_p_hi", [P, FT, P], F32R)
        p_lo = sb("e_p_lo", [P, FT, P], F32R)
        y = sb("e_y", [P, D])
        raw_in, hi_done, lo_done, w_used = ([sem(f"e_{n}{p}") for p in range(PIECES)] for n in ("raw_in", "hi", "lo", "used"))
        idx_in, x_in = ([sem(f"e_{n}{r}") for r in range(2)] for n in ("idx_in", "x_in"))
        xt_mm, xf_act, xf_dve, xh_act, xh_dve, x_split, sg_done, prod_done, at_mm, ph_done, p_split = (
            sem(n) for n in ("e_xt_mm", "e_xf_act", "e_xf_dve", "e_xh_act", "e_xh_dve", "e_x_split", "e_sg_done",
                             "e_prod_done", "e_at_mm", "e_ph_done", "e_p_split"))
        gu_mm, y_mm = w_used[GU - 1], w_used[PIECES - 1]
        y_act, y_dve, y_out, passed = (sem(n) for n in ("e_y_act", "e_y_dve", "e_y_out", "e_passed"))
        scattered = sem("e_scattered")
        block = ctx.enter_context(nc.Block())

        def windows(eng, body):
            pairs(eng, SURE, body)
            last = eng.value_load(g["window"][0:1, W_EXPERT, WINDOWS + 2:], min_val=SURE - 1, max_val=WINDOWS - 1)
            with eng.Fori(SURE // 2, (WINDOWS + 1) // 2) as i:
                for r in range(2):
                    with eng.If(i * 2 + r < last + 1):
                        body(i * 2 + r, r, i)
                    with eng.Else():
                        eng.sem_inc(passed, 1)
            return last

        def look(eng, row, w, low, high):
            return eng.value_load(g["window"][0:1, row, ds(w, 1)], min_val=low, max_val=high)

        def if_new(eng, w, what):
            if isinstance(w, int) and w == 0:
                what(1)
                return
            with eng.If(look(eng, W_NEW, w, 0, 1) > 0):
                what(look(eng, W_COUNT, w, 1, EXPERTS))
            with eng.Else():
                eng.sem_inc(passed, 1)

        @block.sync
        def _(q):
            def load(w, pieces):
                def what(count):
                    e = look(q, W_EXPERT, w, 0, EXPERTS - 1)
                    if at_least(w, 1):
                        before = look(q, W_BEFORE, w, 1, EXPERTS)
                    src = lambda name: t[name][0][ds(e, 1), :, :].rearrange("e (k p) n -> p (e k) n", p=P)
                    for p in pieces:
                        if at_least(w, 1):
                            wait_apart(q, lo_done[p], before, passed)
                        if p < GU:
                            k = slice(2 * p, 2 * p + 2)
                            q.dma_start(raw[p][:, :, 0:F_EXP], src("expert_w_gate")[:, k, :]).then_inc(raw_in[p], 16)
                            q.dma_start(raw[p][:, :, F_EXP:D], src("expert_w_up")[:, k, :]).then_inc(raw_in[p], 16)
                        else:
                            k = slice(2 * (p - GU), 2 * (p - GU) + 2)
                            q.dma_start(raw[p][:], src("expert_w_down")[:, k, :]).then_inc(raw_in[p], 16)

                if_new(q, w, what)

            load(0, range(GU))
            load(1, range(GU))

            def body(w, r, i):
                load(w, range(GU, PIECES))
                load(w + 2, range(GU))

            windows(q, body)

        @block.gpsimd
        def _(pool):
            def fetch(v, r):
                pool.dma_start(idx[r][:], t["slot_tok"][ds(v * P, P), :]).then_inc(idx_in[r], 16)

            def gather(v, r, i):
                pool.wait_ge(idx_in[r], i * 16 + 16)
                wait_apart(pool, xt_mm, pos(v - 1), passed)
                pool.indirect_dma_start(xrow[r][:], None, t["xh"],
                                        bass.IndirectOffsetOnAxis(ap=idx[r][:], axis=0)).then_inc(x_in[r], 16)
                wait_apart(pool, x_in[r], i * 16 + 16, passed)

            def down_lo(w):
                def what(count):
                    for p in range(GU, PIECES):
                        wait_apart(pool, hi_done[p], count, passed)
                        pool.tensor_tensor(w_lo[p][:], raw[p][:], w_hi[p][:].bitcast(F32), ALU.subtract).then_inc(lo_done[p], 1)

                if_new(pool, w, what)

            for i in range(TOK_TILES):
                for k in range(2):
                    pool.indirect_dma_start(t["slot_tok"], bass.IndirectOffsetOnAxis(ap=g["dest"][k][:, i:i + 1], axis=0),
                                            g["token"][:, i:i + 1], None).then_inc(scattered, 16)
            pool.wait_ge(scattered, 16 * 2 * TOK_TILES)
            fetch(0, 0)
            gather(0, 0, 0)
            fetch(1, 1)

            def body(w, r, i):
                gather(w + 1, 1 - r, i + r)
                fetch(w + 2, r)
                if at_least(w, 1):
                    down_lo(w - 1)

            last = windows(pool, body)
            down_lo(last)

        @block.scalar
        def _(act):
            def split(w, pieces):
                def what(count):
                    for p in pieces:
                        wait_apart(act, raw_in[p], count * (32 if p < GU else 16), passed)
                        if at_least(w, 1):
                            wait_apart(act, w_used[p], w, passed)
                        nc.scalar.activation(w_hi[p][:], raw[p][:], ACT.Copy).then_inc(hi_done[p], 1)

                if_new(act, w, what)

            def turned(v):
                act.wait_ge(xt_mm, v + 1)
                act.wait_ge(x_split, v)
                for k in range(KD // 2):
                    ins = nc.scalar.activation(xt[:, k, :], xt_ps[:, k * P:(k + 1) * P], ACT.Identity,
                                               bias=g["shift_ffn"][:, k:k + 1], scale=g["scale_ffn"][:, k:k + 1])
                ins.then_inc(xf_act, 1)
                act.wait_ge(xf_act, v + 1)
                act.wait_ge(gu_mm, v)
                nc.scalar.activation(x_hi[:, 0:KD // 2, :], xt[:, 0:KD // 2, :], ACT.Copy).then_inc(xh_act, 1)

            def prod_hi(w):
                act.wait_ge(at_mm, w + 1)
                act.wait_ge(y_mm, w)
                nc.scalar.activation(p_hi[:].rearrange("p k n -> p (k n)"), at_ps[:], ACT.Copy).then_inc(ph_done, 1)

            def store(v):
                act.wait_ge(y_mm, v + 1)
                act.wait_ge(y_out, v * 16)
                nc.scalar.activation(y[:, 0:BANK], y_ps[:, 0:BANK], ACT.Copy).then_inc(y_act, 1)
                act.wait_ge(y_act, v + 1)
                act.wait_ge(y_dve, v + 1)
                act.dma_start(t["ybuf"][ds(v * P, P), :], y[:]).then_inc(y_out, 16)

            split(0, range(GU))
            turned(0)

            def body(w, r, i):
                if at_least(w, 1):
                    split(w - 1, range(GU, PIECES))
                if at_least(w, 2):
                    store(w - 2)
                if at_least(w, 1):
                    prod_hi(w - 1)
                split(w + 1, range(EARLY))
                act.wait_ge(gu_mm, w + 1)
                act.wait_ge(prod_done, w)
                nc.scalar.activation(sg[:], gate_ps[:], ACT.Silu).then_inc(sg_done, 1)
                turned(w + 1)
                split(w + 1, range(EARLY, GU))

            last = windows(act, body)
            store(look(act, W_NEW, WINDOWS + 2, SURE - 2, WINDOWS - 2))
            prod_hi(last)
            split(last, range(GU, PIECES))
            store(last)
            act.wait_ge(y_out, last * 16 + 16)
            act.sem_inc(passed, 1)

        @block.vector
        def _(dve):
            def split(w, pieces):
                def what(count):
                    for p in pieces:
                        wait_apart(dve, hi_done[p], count, passed)
                        dve.tensor_tensor(w_lo[p][:], raw[p][:], w_hi[p][:].bitcast(F32), ALU.subtract).then_inc(lo_done[p], 1)

                if_new(dve, w, what)

            def turned(v):
                second = slice(KD // 2, KD)
                dve.wait_ge(xt_mm, v + 1)
                for k in range(KD // 2, KD):
                    ins = dve.tensor_scalar(xt[:, k, :], xt_ps[:, k * P:(k + 1) * P], g["scale_ffn"][:, k:k + 1],
                                            g["shift_ffn"][:, k:k + 1], ALU.mult, ALU.add)
                ins.then_inc(xf_dve, 1)
                dve.wait_ge(xf_dve, v + 1)
                dve.wait_ge(gu_mm, v)
                dve.tensor_copy(x_hi[:, second, :], xt[:, second, :]).then_inc(xh_dve, 1)
                dve.wait_ge(xh_dve, v + 1)
                dve.wait_ge(xh_act, v + 1)
                dve.tensor_tensor(x_lo[:], xt[:], x_hi[:].bitcast(F32), ALU.subtract).then_inc(x_split, 1)

            def prod_lo(w):
                dve.wait_ge(ph_done, w + 1)
                dve.tensor_tensor(p_lo[:].rearrange("p k n -> p (k n)"), at_ps[:],
                                  p_hi[:].rearrange("p k n -> p (k n)").bitcast(F32), ALU.subtract).then_inc(p_split, 1)

            def store(v):
                dve.wait_ge(y_mm, v + 1)
                dve.wait_ge(y_out, v * 16)
                dve.tensor_copy(y[:, BANK:D], y_ps[:, BANK:D]).then_inc(y_dve, 1)

            split(0, range(GU))
            turned(0)

            def body(w, r, i):
                if at_least(w, 2):
                    store(w - 2)
                if at_least(w, 1):
                    prod_lo(w - 1)
                split(w + 1, range(EARLY))
                dve.wait_ge(sg_done, w + 1)
                dve.wait_ge(at_mm, w)
                dve.tensor_tensor(prod[:], up_ps[:], sg[:], ALU.mult).then_inc(prod_done, 1)
                turned(w + 1)
                split(w + 1, range(EARLY, GU))

            last = windows(dve, body)
            store(look(dve, W_NEW, WINDOWS + 2, SURE - 2, WINDOWS - 2))
            prod_lo(last)
            store(last)

        @block.tensor
        def _(pe):
            def turn(v, r, i):
                pe.wait_ge(x_in[r], i * 16 + 16)
                pe.wait_ge(xf_act, v)
                pe.wait_ge(xf_dve, v)
                for k in range(KD):
                    tr = pe.transpose(xt_ps[:, k * P:(k + 1) * P], xrow[r][:, k * P:(k + 1) * P], g["ident"][:])
                tr.then_inc(xt_mm, 1)

            def down(v):
                count = 1 if isinstance(v, int) and v == 0 else look(pe, W_COUNT, v, 1, EXPERTS)
                pe.wait_ge(p_split, v + 1)
                pe.wait_ge(y_act, v)
                pe.wait_ge(y_dve, v)
                for p in range(GU, PIECES):
                    wait_apart(pe, lo_done[p], count, passed)
                    for k in range(2):
                        kk = 2 * (p - GU) + k
                        for a, b in ((p_hi, w_hi), (p_hi, w_lo), (p_lo, w_hi)):
                            for h in range(2):
                                mm = pe.matmul(y_ps[:, h * BANK:(h + 1) * BANK], a[:, kk, :], b[p][:, k, h * BANK:(h + 1) * BANK],
                                               start=(kk == 0 and a is p_hi and b is w_hi),
                                               stop=(kk == FT - 1 and a is p_lo), skip_group_check=True)
                    mm.then_inc(w_used[p], 1)

            def body(w, r, i):
                count = 1 if isinstance(w, int) and w == 0 else look(pe, W_COUNT, w, 1, EXPERTS)
                pe.wait_ge(x_split, w + 1)
                pe.wait_ge(prod_done, w)
                for p in range(GU):
                    wait_apart(pe, lo_done[p], count, passed)
                    for k in range(2):
                        kk = 2 * p + k
                        for a, b in ((x_hi, w_hi), (x_hi, w_lo), (x_lo, w_hi)):
                            for out, h in ((gate_ps, 0), (up_ps, 1)):
                                mm = pe.matmul(out[:], a[:, kk, :], b[p][:, k, h * BANK:(h + 1) * BANK],
                                               start=(kk == 0 and a is x_hi and b is w_hi), stop=(kk == KD - 1 and a is x_lo),
                                               skip_group_check=True)
                    mm.then_inc(w_used[p], 1)
                turn(w + 1, 1 - r, i + r)
                if at_least(w, 1):
                    down(w - 1)
                pe.wait_ge(prod_done, w + 1)
                pe.wait_ge(p_split, w)
                for k in range(FT):
                    tr = pe.transpose(at_ps[:, k * P:(k + 1) * P], prod[:, k * P:(k + 1) * P], g["ident"][:])
                tr.then_inc(at_mm, 1)

            turn(0, 0, 0)
            last = windows(pe, body)
            down(last)


def phase_combine(nc, t, g):
    with ExitStack() as ctx:
        sb = lambda n, s, d=F32: ctx.enter_context(nc.sbuf_tensor(n, s, d))
        sem = ctx.enter_context(semaphores(nc))
        SLOTS = 4
        buf = lambda n, s, d=F32: [sb(f"{n}{b}", s, d) for b in range(SLOTS)]
        sems = lambda n: [sem(f"{n}{b}") for b in range(SLOTS)]
        row = [buf(f"c_idx{k}_", [P, 1], U32) for k in range(2)]
        yr = [buf(f"c_y{k}_", [P, D]) for k in range(2)]
        wt, x2, acc, st, out = (buf(n, s) for n, s in (
            ("c_wt", [P, 2]), ("c_x2", [P, D]), ("c_acc", [P, D]), ("c_st", [P, 4]), ("c_out", [P, D])))
        sq = [sb(f"c_sq{b}", [P, D]) for b in range(2)]
        x2_in, y_in, outs = sems("c_x2_in"), [sems(f"c_y{k}_in") for k in range(2)], sems("c_outs")
        row_set, share, chain, summed, squared, root, done, used = (sem(n) for n in (
            "c_row_set", "c_share", "c_chain", "c_summed", "c_squared", "c_root", "c_done", "c_used"))
        block = ctx.enter_context(nc.Block())

        def tiles(eng, body):
            for k in range(SLOTS + 1):
                body(k, k % SLOTS, k // SLOTS)
            with eng.Fori(1, TOK_TILES // SLOTS - 1) as i:
                for r in range(1, SLOTS + 1):
                    body(i * SLOTS + r, r % SLOTS, i + r // SLOTS)
            for k in range(TOK_TILES - SLOTS + 1, TOK_TILES):
                body(k, k % SLOTS, k // SLOTS)

        is_first = lambda n: isinstance(n, int) and n == 0

        @block.sync
        def _(q):
            def body(n, r, i):
                if at_least(n, SLOTS):
                    wait_apart(q, summed, n - SLOTS + 1, used)
                q.dma_start(x2[r][:], t["x2"][ds(n * P, P), :]).then_inc(x2_in[r], 16)

            tiles(q, body)
            for r in range(SLOTS):
                q.wait_ge(outs[r], 16 * (TOK_TILES // SLOTS))

        @block.gpsimd
        def _(pool):
            def body(n, r, i):
                if at_least(n, SLOTS):
                    wait_apart(pool, summed, n - SLOTS + 1, used)
                for k in range(2):
                    pool.tensor_copy(wt[r][:, k:k + 1], g["weight"][k][:, ds(n, 1)])
                for k in range(2):
                    ins = pool.tensor_copy(row[k][r][:], g["dest"][k][:, ds(n, 1)])
                ins.then_inc(row_set, 1)
                wait_apart(pool, row_set, n + 1, used)
                for k in range(2):
                    pool.indirect_dma_start(yr[k][r][:], None, t["ybuf"],
                                            bass.IndirectOffsetOnAxis(ap=row[k][r][:], axis=0)).then_inc(y_in[k][r], 16)

            tiles(pool, body)

        @block.scalar
        def _(act):
            def norm(n, r):
                act.wait_ge(summed, n + 1)
                nc.scalar.activation(sq[r % 2][:], acc[r][:], ACT.Square, accum_out=st[r][:, 0:1]).then_inc(squared, 1)
                act.wait_ge(squared, n + 1)
                nc.scalar.activation(st[r][:, 1:2], st[r][:, 0:1], ACT.Sqrt, bias=g["eps"][:], scale=1.0 / D).then_inc(root, 1)

            def store(n, r):
                act.wait_ge(done, n + 1)
                act.dma_start(t["out"][0][ds(n * P, P), :], out[r][:]).then_inc(outs[r], 16)

            def body(n, r, i):
                act.wait_ge(y_in[0][r], i * 16 + 16)
                act.wait_ge(row_set, n + 1)
                if at_least(n, SLOTS):
                    act.wait_ge(done, n - SLOTS + 1)
                nc.scalar.activation(acc[r][:], yr[0][r][:], ACT.Copy, scale=wt[r][:, 0:1]).then_inc(share, 1)
                if not is_first(n):
                    norm(n - 1, (r - 1) % SLOTS)
                if not is_first(n) and not (isinstance(n, int) and n == 1):
                    store(n - 2, (r - 2) % SLOTS)

            tiles(act, body)
            norm(TOK_TILES - 1, SLOTS - 1)
            for n in (TOK_TILES - 2, TOK_TILES - 1):
                store(n, n % SLOTS)

        @block.vector
        def _(dve):
            def finish(n, r, i, links):
                c = Chain(dve, chain, links)
                dve.wait_ge(root, n + 1)
                c.link(dve.reciprocal(st[r][:, 2:3], st[r][:, 1:2]))
                if not (isinstance(i, int) and i == 0):
                    dve.wait_ge(outs[r], i * 16)
                dve.scalar_tensor_tensor(out=out[r][:], in0=acc[r][:], scalar=st[r][:, 2:3], in1=g["final_w"][:],
                                         op0=ALU.mult, op1=ALU.mult).then_inc(done, 1)

            def body(n, r, i):
                links = n * 3 - 1 if not is_first(n) else 0
                c = Chain(dve, chain, links)
                dve.wait_ge(share, n + 1)
                dve.wait_ge(y_in[1][r], i * 16 + 16)
                c.link(dve.scalar_tensor_tensor(out=acc[r][:], in0=yr[1][r][:], scalar=wt[r][:, 1:2], in1=acc[r][:],
                                                op0=ALU.mult, op1=ALU.add))
                c.link(dve.tensor_tensor(acc[r][:], acc[r][:], g["gates"][:, 1, :], ALU.mult))
                dve.wait_ge(x2_in[r], i * 16 + 16)
                dve.tensor_tensor(acc[r][:], acc[r][:], x2[r][:], ALU.add).then_inc(summed, 1)
                if not is_first(n):
                    finish(n - 1, (r - 1) % SLOTS, i if r > 0 else i - 1, n * 3 + 1)

            tiles(dve, body)
            finish(TOK_TILES - 1, SLOTS - 1, TOK_TILES // SLOTS - 1, TOK_TILES * 3 - 1)


_INS = ['x', 'c', 'ada_w', 'ada_b', 'norm_mix_w', 'w_in', 'conv_w', 'conv_b', 'lru_wa', 'lru_ba', 'lru_wx', 'lru_bx',
        'lru_lambda', 'norm_lru_w', 'hgrn_lb', 'norm_hgrn_w', 'w_out', 'norm_ffn_w', 'router_group_w', 'router_group_b',
        'router_expert_w', 'router_expert_b', 'expert_w_gate', 'expert_w_up', 'expert_w_down', 'final_norm_w']
_SCRATCH = [("projT", (GROUPS * CH, SEQ), F32), ("mergedT", (D, SEQ), F32), ("x2", (SEQ, D), F32), ("xh", (SEQ, D), F32),
            ("slot_tok", ((WINDOWS + 3) * P, 1), I32), ("ybuf", ((WINDOWS + 1) * P, D), F32)]


def build(nc, t):
    for name, shape, dt in _SCRATCH:
        t[name] = nc.dram_tensor(name, shape, dt, kind="Internal").ap()
    with ExitStack() as ctx:
        g = persistent(nc, ctx)
        with ExitStack() as own:
            g["hT"] = own.enter_context(nc.sbuf_tensor("hT", [P, KD, SEQ], F32))
            phase_modulate(nc, t, g)
            phase_project(nc, t, g)
        phase_hgrn(nc, t, g)
        persistent2(nc, ctx, g)
        phase_output(nc, t, g)
        phase_route(nc, t, g)
        phase_experts(nc, t, g)
        phase_combine(nc, t, g)


def kernel(**inputs):
    import numpy as np
    import concourse.bacc as bacc
    from concourse.bass_utils import run_bass_kernel_spmd

    nc = bacc.Bacc("TRN2", target_bir_lowering=False, num_devices=1)
    arrays, t = {}, {}
    for name in _INS:
        a = np.ascontiguousarray(inputs[name])
        arrays[f"in_{name}"] = a
        t[name] = nc.dram_tensor(f"in_{name}", a.shape, mybir.dt.from_np(a.dtype), kind="ExternalInput").ap()
    t["out"] = nc.dram_tensor("out", (1, SEQ, D), F32, kind="ExternalOutput").ap()
    build(nc, t)
    r = run_bass_kernel_spmd(nc, [arrays], core_ids=[0])
    return r.results[0]["out"]
```
